# Optimizing a Trainium2 kernel written in Bass

```python
import math
import jax, jax.numpy as jnp
from jax import lax
import numpy as np

D_MODEL = 2048
BATCH = 1
SEQ = 256
DEPTH = 1

D_RNN = 2048
RNN_HEADS = 16
RNN_BLOCK = D_RNN // RNN_HEADS
CONV_WIDTH = 4
LRU_C = 8.0
MLA_HEADS = 16
Q_LORA = 512
KV_LORA = 512
QK_NOPE = 128
QK_ROPE = 64
V_HEAD = 128
ROPE_THETA = 10000.0
Q_BLOCK = 128
PEER_HEADS = 8
N_KEYS = 128
N_EXPERTS = N_KEYS * N_KEYS
D_KEY = 256
PEER_TOPK = 16
PEER_CHUNK = 128
DN_ALPHA = (2.0 * DEPTH) ** 0.25
DN_BETA = (8.0 * DEPTH) ** -0.25
LN_EPS = 1e-5
RMS_EPS = 1e-6
IN_WIDTHS = (D_RNN, D_RNN, Q_LORA, KV_LORA, QK_ROPE, D_MODEL, D_MODEL)
IN_COLS = sum(IN_WIDTHS)
IN_SPLITS = tuple(int(v) for v in np.cumsum(IN_WIDTHS)[:-1])

kernel_name = "hybrid_rglru_mla_peer_deepnorm_adaln"

def layer_norm(x, g, b):
    xf = x.astype(jnp.float32)
    mu = jnp.mean(xf, -1, keepdims=True)
    var = jnp.mean(jnp.square(xf - mu), -1, keepdims=True)
    return ((xf - mu) * lax.rsqrt(var + LN_EPS)).astype(x.dtype) * g + b

def rms_norm(x, g):
    xf = x.astype(jnp.float32)
    return (xf * lax.rsqrt(jnp.mean(xf * xf, -1, keepdims=True) + RMS_EPS)).astype(x.dtype) * g

def apply_rope(x, cos, sin):
    x1, x2 = jnp.split(x, 2, axis=-1)
    return jnp.concatenate([x1 * cos - x2 * sin, x2 * cos + x1 * sin], axis=-1)

def rg_lru_branch(xr, gr, conv_w, conv_b, w_a, b_a, w_x, b_x, lam):
    B, S, _ = xr.shape
    xc = lax.conv_general_dilated(
        xr, conv_w[:, None, :], window_strides=(1,), padding=[(CONV_WIDTH - 1, 0)],
        dimension_numbers=('NWC', 'WIO', 'NWC'), feature_group_count=D_RNN) + conv_b
    xh = xc.reshape(B, S, RNN_HEADS, RNN_BLOCK)
    r = jax.nn.sigmoid(jnp.einsum('bshi,hij->bshj', xh, w_a).reshape(B, S, D_RNN) + b_a)
    i = jax.nn.sigmoid(jnp.einsum('bshi,hij->bshj', xh, w_x).reshape(B, S, D_RNN) + b_x)
    log_a = (-LRU_C * r.astype(jnp.float32)) * jax.nn.softplus(-lam.astype(jnp.float32))
    a = jnp.exp(log_a)
    mult = jnp.sqrt(-jnp.expm1(2.0 * log_a))
    bx = mult * (i * xc).astype(jnp.float32)

    def combine(left, right):
        a1, b1 = left
        a2, b2 = right
        return a1 * a2, a2 * b1 + b2

    _, h = lax.associative_scan(combine, (a, bx), axis=1)
    return h.astype(xr.dtype) * jax.nn.gelu(gr)

def mla_branch(q_c, kv_c, k_r, cos, sin, q_norm_g, w_uq, kv_norm_g, w_ukv):
    B, S, _ = q_c.shape
    q = (rms_norm(q_c, q_norm_g) @ w_uq).reshape(B, S, MLA_HEADS, QK_NOPE + QK_ROPE)
    q_nope = q[..., :QK_NOPE]
    q_rope = apply_rope(q[..., QK_NOPE:], cos[:, :, None, :], sin[:, :, None, :])
    kv = (rms_norm(kv_c, kv_norm_g) @ w_ukv).reshape(B, S, MLA_HEADS, QK_NOPE + V_HEAD)
    k_nope = kv[..., :QK_NOPE]
    v = kv[..., QK_NOPE:]
    k_rope = apply_rope(k_r, cos, sin)
    scale = (QK_NOPE + QK_ROPE) ** -0.5
    nb = S // Q_BLOCK
    qn_blocks = q_nope.reshape(B, nb, Q_BLOCK, MLA_HEADS, QK_NOPE).transpose(1, 0, 2, 3, 4)
    qr_blocks = q_rope.reshape(B, nb, Q_BLOCK, MLA_HEADS, QK_ROPE).transpose(1, 0, 2, 3, 4)
    key_pos = jnp.arange(S)

    def attend(args):
        qn, qr, blk = args
        s = (jnp.einsum('bqhd,bkhd->bhqk', qn, k_nope)
             + jnp.einsum('bqhr,bkr->bhqk', qr, k_rope)).astype(jnp.float32) * scale
        q_pos = blk * Q_BLOCK + jnp.arange(Q_BLOCK)
        causal = key_pos[None, :] <= q_pos[:, None]
        s = jnp.where(causal, s, -jnp.inf)
        p = jax.nn.softmax(s, axis=-1).astype(v.dtype)
        return jnp.einsum('bhqk,bkhd->bqhd', p, v)

    o = lax.map(attend, (qn_blocks, qr_blocks, jnp.arange(nb)))
    return o.transpose(1, 0, 2, 3, 4).reshape(B, S, MLA_HEADS * V_HEAD)

def peer_ffn(u, w_q, sub_keys, expert_u, expert_v):
    B, S, D = u.shape
    T = B * S
    ut = u.reshape(T, D)
    q = (ut @ w_q).reshape(T, PEER_HEADS, 2, D_KEY // 2)
    s = jnp.einsum('thpd,pnd->thpn', q, sub_keys).astype(jnp.float32)
    top_s, top_i = lax.top_k(s, PEER_TOPK)
    cand_s = top_s[:, :, 0, :, None] + top_s[:, :, 1, None, :]
    cand_i = top_i[:, :, 0, :, None] * N_KEYS + top_i[:, :, 1, None, :]
    best_s, best_j = lax.top_k(cand_s.reshape(T, PEER_HEADS, PEER_TOPK * PEER_TOPK), PEER_TOPK)
    idx = jnp.take_along_axis(cand_i.reshape(T, PEER_HEADS, PEER_TOPK * PEER_TOPK), best_j, axis=-1)
    g = jax.nn.softmax(best_s, axis=-1).astype(u.dtype)
    nc = T // PEER_CHUNK

    def experts(args):
        xc, ic, gc = args
        act = jax.nn.gelu(jnp.einsum('cd,chkd->chk', xc, jnp.take(expert_u, ic, axis=0))) * gc
        return jnp.einsum('chk,chkd->cd', act, jnp.take(expert_v, ic, axis=0))

    y = lax.map(experts, (ut.reshape(nc, PEER_CHUNK, D),
                          idx.reshape(nc, PEER_CHUNK, PEER_HEADS, PEER_TOPK),
                          g.reshape(nc, PEER_CHUNK, PEER_HEADS, PEER_TOPK)))
    return y.reshape(B, S, D)

def setup_inputs(seed: int = 0) -> dict:
    key = jax.random.key(seed)
    ks = jax.random.split(key, 32)
    L, D = DEPTH, D_MODEL
    f32 = jnp.float32

    def nrm(k, shape, scale):
        return jax.random.normal(k, shape, f32) * scale

    x = jax.random.normal(ks[0], (BATCH, SEQ, D), f32)
    c = jax.random.normal(ks[1], (BATCH, D), f32)
    offs = jax.random.randint(ks[2], (BATCH, 1), 0, 1024, dtype=jnp.int32)
    positions = (offs + jnp.arange(SEQ, dtype=jnp.int32)[None, :]).astype(jnp.int32)
    a0 = jax.random.uniform(ks[3], (L, D_RNN), f32, 0.9, 0.999)
    p0 = a0 ** (1.0 / LRU_C)
    rg_lambda = jnp.log(p0) - jnp.log1p(-p0)
    return {
        "x": x,
        "c": c,
        "positions": positions,
        "w_ada": nrm(ks[4], (L, D, 6 * D), 0.1 * D ** -0.5),
        "b_ada": nrm(ks[5], (L, 6 * D), 0.01),
        "w_in": nrm(ks[6], (L, D, IN_COLS), D ** -0.5),
        "conv_w": nrm(ks[7], (L, CONV_WIDTH, D_RNN), CONV_WIDTH ** -0.5),
        "conv_b": nrm(ks[8], (L, D_RNN), 0.01),
        "w_rg_a": nrm(ks[9], (L, RNN_HEADS, RNN_BLOCK, RNN_BLOCK), RNN_BLOCK ** -0.5),
        "b_rg_a": nrm(ks[10], (L, D_RNN), 0.01),
        "w_rg_x": nrm(ks[11], (L, RNN_HEADS, RNN_BLOCK, RNN_BLOCK), RNN_BLOCK ** -0.5),
        "b_rg_x": nrm(ks[12], (L, D_RNN), 0.01),
        "rg_lambda": rg_lambda,
        "w_rnn_out": nrm(ks[13], (L, D_RNN, D), DN_BETA * D_RNN ** -0.5),
        "q_norm_g": 1.0 + nrm(ks[14], (L, Q_LORA), 0.01),
        "w_uq": nrm(ks[15], (L, Q_LORA, MLA_HEADS * (QK_NOPE + QK_ROPE)), Q_LORA ** -0.5),
        "kv_norm_g": 1.0 + nrm(ks[16], (L, KV_LORA), 0.01),
        "w_ukv": nrm(ks[17], (L, KV_LORA, MLA_HEADS * (QK_NOPE + V_HEAD)), KV_LORA ** -0.5),
        "w_mla_out": nrm(ks[18], (L, MLA_HEADS * V_HEAD, D), DN_BETA * (MLA_HEADS * V_HEAD) ** -0.5),
        "w_o": nrm(ks[19], (L, D, D), DN_BETA * D ** -0.5),
        "ln1_g": 1.0 + nrm(ks[20], (L, D), 0.01),
        "ln1_b": nrm(ks[21], (L, D), 0.01),
        "peer_wq": nrm(ks[22], (L, D, PEER_HEADS * D_KEY), D ** -0.5),
        "peer_keys": nrm(ks[23], (L, 2, N_KEYS, D_KEY // 2), (D_KEY // 2) ** -0.5),
        "peer_u": nrm(ks[24], (L, N_EXPERTS, D), D ** -0.5),
        "peer_v": nrm(ks[25], (L, N_EXPERTS, D), DN_BETA),
        "ln2_g": 1.0 + nrm(ks[26], (L, D), 0.01),
        "ln2_b": nrm(ks[27], (L, D), 0.01),
    }

def reference(x, c, positions, w_ada, b_ada, w_in, conv_w, conv_b, w_rg_a, b_rg_a, w_rg_x, b_rg_x,
              rg_lambda, w_rnn_out, q_norm_g, w_uq, kv_norm_g, w_ukv, w_mla_out, w_o, ln1_g, ln1_b,
              peer_wq, peer_keys, peer_u, peer_v, ln2_g, ln2_b):
    inv_freq = ROPE_THETA ** (-jnp.arange(0, QK_ROPE, 2, dtype=jnp.float32) / QK_ROPE)
    ang = positions.astype(jnp.float32)[..., None] * inv_freq
    cos = jnp.cos(ang).astype(x.dtype)
    sin = jnp.sin(ang).astype(x.dtype)
    c_act = jax.nn.silu(c)
    for l in range(DEPTH):
        mod = c_act @ w_ada[l] + b_ada[l]
        sh1, sc1, gt1, sh2, sc2, gt2 = [m[:, None, :] for m in jnp.split(mod, 6, axis=-1)]

        h = x * (1.0 + sc1) + sh1
        proj = h @ w_in[l]
        xr, gr, q_c, kv_c, k_r, g_rnn, g_mla = jnp.split(proj, IN_SPLITS, axis=-1)
        y_rnn = rg_lru_branch(xr, gr, conv_w[l], conv_b[l], w_rg_a[l], b_rg_a[l],
                              w_rg_x[l], b_rg_x[l], rg_lambda[l]) @ w_rnn_out[l]
        y_mla = mla_branch(q_c, kv_c, k_r, cos, sin, q_norm_g[l], w_uq[l],
                           kv_norm_g[l], w_ukv[l]) @ w_mla_out[l]
        mixed = (jax.nn.sigmoid(g_rnn) * y_rnn + jax.nn.sigmoid(g_mla) * y_mla) @ w_o[l]
        x = layer_norm(DN_ALPHA * x + (1.0 + gt1) * mixed, ln1_g[l], ln1_b[l])

        h = x * (1.0 + sc2) + sh2
        y_ffn = peer_ffn(h, peer_wq[l], peer_keys[l], peer_u[l], peer_v[l])
        x = layer_norm(DN_ALPHA * x + (1.0 + gt2) * y_ffn, ln2_g[l], ln2_b[l])
    return x


_drawn_inputs = setup_inputs


def setup_inputs(seed=0):
    import zlib

    import numpy as np

    out = dict(_drawn_inputs(seed))
    spreads = {}
    factors = {'conv_b': 3.539,
     'b_rg_a': 180.083,
     'b_rg_x': 64.0,
     'q_norm_g': 8.0,
     'kv_norm_g': 8.0,
     'ln2_g': 195.621,
     'ln2_b': 190.139}
    for name, (base, spread) in spreads.items():
        noise = np.random.default_rng([zlib.crc32(name.encode()), seed]).standard_normal(out[name].shape)
        drawn = base * np.exp(spread * noise) if base else spread * noise
        out[name] = __import__('jax').numpy.asarray(drawn.astype(out[name].dtype))
    for name, factor in factors.items():
        out[name] = (out[name] * factor).astype(out[name].dtype)
    return out
```

```python
import math
from contextlib import ExitStack

import numpy as np

import concourse.bass as bass
from concourse import mybir

F32 = mybir.dt.float32
U32 = mybir.dt.uint32
I32 = mybir.dt.int32
ALU = mybir.AluOpType
ACT = mybir.ActivationFunctionType
AX_X = mybir.AxisListType.X

P = 128
D = 2048
S = 256
NT = S // P
KT = D // P
HEADS = 16
RANK = 512
LT = RANK // P
NOPE, ROPE, VH = 128, 64, 128
CONV = 4
PH, NK, TOPK = 8, 128, 16
HP = 2 * PH
EXPERTS = PH * TOPK
ALPHA = 2.0 ** 0.25
LN_EPS, RMS_EPS = 1e-5, 1e-6
SM_SCALE = (NOPE + ROPE) ** -0.5
GELU_C, GELU_S = 0.044715, 2.0 * math.sqrt(2.0 / math.pi)

C_XR, C_GR, C_QC, C_KVC = 0, D, 2 * D, 2 * D + RANK
C_KR = C_KVC + RANK
C_GRNN = C_KR + ROPE
C_GMLA = C_GRNN + D

UNIT = 2048
RING = 4
B_QC, B_KVC, B_XR, B_G, B_RNN, B_MLA, B_O, B_WQ = 0, 1, 2, 10, 18, 22, 26, 30
ADA_UNITS = 2 * KT
GROUP = 4
NGROUP = EXPERTS // GROUP

K_ID, K_MASK, K_ROT, K_IOTA, K_INVF, K_ONES, K_END = 0, 128, 512, 640, 656, 657, 785


def constants():
    c = np.zeros((P, K_END), np.float32)
    c[:, K_ID:K_ID + P] = np.eye(P)
    tri = np.where(np.arange(P)[None, :] <= np.arange(P)[:, None], 0.0, -1e30)
    c[:, K_MASK:K_MASK + P] = tri
    c[:, K_MASK + 2 * P:K_MASK + 3 * P] = tri
    half = ROPE // 2
    for m in range(half):
        c[m + half, K_ROT + m] = -1.0
        c[m, K_ROT + half + m] = 1.0
    c[:, K_IOTA:K_IOTA + TOPK] = np.arange(TOPK)
    freq = np.float32(10000.0) ** (-np.arange(0, ROPE, 2, dtype=np.float32) / np.float32(ROPE))
    c[:ROPE, K_INVF] = np.concatenate([freq, freq])
    c[:, K_ONES:K_ONES + P] = 1.0
    return c


class Chain:

    def __init__(self, eng, sem):
        self.eng, self.sem, self.base, self.n = eng, sem, 0, 0

    def do(self, ins):
        ins.then_inc(self.sem, 1)
        self.n += 1
        return ins

    def wait(self):
        self.eng.wait_ge(self.sem, self.base + self.n)

    def enter(self, i, first, per):
        self.kept, self.per = self.base + self.n, per
        self.base, self.n = i * per + (self.kept - first * per), 0

    def leave(self, rounds):
        assert self.n == self.per, (self.n, self.per)
        self.base, self.n = self.kept + rounds * self.per, 0


def build(nc, t, out):
    with ExitStack() as ctx:
        def sem(name):
            return ctx.enter_context(nc.semaphore(name))

        arena = ctx.enter_context(nc.sbuf_tensor("arena", [P, 53000], F32))
        ps = ctx.enter_context(nc.psum_tensor("ps", [P, 8, 512], F32))

        R_RING, R_MODS, R_PADA = 0, 8192, 16384
        R_HT, R_WORK, R_HG, R_G, R_OT, R_SM = 20480, 24576, 34816, 38912, 47104, 51200

        def at(off, n):
            return arena[:, off:off + n]

        def at3(off, a, b):
            return at(off, a * b).rearrange("p (a b) -> p a b", a=a)

        sm = [R_SM]

        def small(n):
            sm[0] += n
            assert sm[0] <= 53000
            return sm[0] - n

        ring = [at(R_RING + UNIT * s, UNIT) for s in range(RING)]
        ring3 = [r.rearrange("p (t c) -> p t c", t=4) for r in ring]
        mods = [at(R_MODS + D * i, D) for i in range(4)]
        pada = [at(R_PADA + D * i, D) for i in range(2)]
        hT = at3(R_HT, KT, S)
        hgT = at3(R_HG, KT, S)
        gT = [at3(R_G, KT, S), at3(R_G + KT * S, KT, S)]
        oT = at3(R_OT, KT, S)
        xin = at3(R_G, NT, D)
        acc = [at(R_G + KT * S + D * i, D) for i in range(2)]

        cst = at(small(K_END), K_END)
        ident = cst[:, K_ID:K_ID + P]
        ones = cst[:, K_ONES:K_ONES + P]
        eps_rms, eps_ln = at(small(1), 1), at(small(1), 1)
        colA = at(small(P), P)
        colB = at(small(24), 24)
        conv_c, convb_c, ba_c, bx_c, lam_c = (colA[:, a:b] for a, b in ((0, 64), (64, 80), (80, 96), (96, 112), (112, 128)))
        sigc = at(small(16), 16)
        cact = at(small(16), 16)
        sh1 = at(small(16), 16)
        sc1 = at(small(16), 16)
        sp4 = at(small(16), 16)
        lt = [at(small(16), 16) for _ in range(5)]
        smx = at(small(2), 2)
        snm = at(small(2), 2)
        ssum = at(small(2), 2)
        srec = at(small(2), 2)
        bn6 = at3(small(24), 4, 6)
        mv = at(small(2), 2)
        rstd = at(small(2), 2)
        gexp = at(small(24), 24)
        zraw = at(small(8), 8)
        zu = at(small(8), 8)
        zg = at(small(8), 8)
        zs = at(small(8), 8)
        za = at(small(8), 8)
        idxu, idxv = (at(small(8), 8).bitcast(U32) for _ in range(2))
        gate_w = [at(small(P), P) for _ in range(NT)]
        idx = [at(small(P), P).bitcast(U32) for _ in range(NT)]

        W = R_WORK
        qcT, kvT = at3(W, LT, S), at3(W + 1024, LT, S)
        cosT, sinT, krT = (arena[0:ROPE, W + o:W + o + S] for o in (2048, 2304, 2560))
        qkn = at(W + 2816, 2 * S)
        qn, kn = qkn[:, 0:S], qkn[:, S:2 * S]
        qr, qro = (arena[0:ROPE, W + o:W + o + S] for o in (3328, 3584))
        vv = at3(W + 3840, NT, VH)
        rt = arena[0:ROPE, W + 4096:W + 4352]
        sc = at(W + 4352, 384)
        pT = at3(W + 4736, 3, P)
        sq2 = [at3(W + 5120, LT, S), at3(W + 6144, LT, S)]
        rs2 = [at(W + 7168, S), at(W + 7424, S)]
        pt = [arena[0:ROPE, W + 7680 + S * i:W + 7680 + S * (i + 1)] for i in range(5)]
        krraw = arena[0:ROPE, W + 8960:W + 9216]
        stA, stB = at(W + 9216, P), arena[0:24, W + 9344:W + 9472]
        uq = [at3(R_HG + 768 * b, LT, 192) for b in range(2)]
        ukv = [at3(R_HG + 1536 + 1024 * b, LT, 256) for b in range(2)]
        krw = at3(R_OT, KT, ROPE)

        XR, GR, XC, RR, II, TP, QQ, GT = (W + 1024 * i for i in range(8))
        wg = at(W + 8192, 1024).rearrange("p (g h c) -> p g h c", g=2, h=4)

        def quad(off, j):
            return at(off + S * j, S)

        x1 = [at(W + D * i, D) for i in range(NT)]
        h2 = [at(W + 2 * D + D * i, D) for i in range(NT)]
        keys = at3(W + 8192, 2, P)
        keysT = at3(W + 8448, 2, P)
        tops = at3(W + 8704, HP, TOPK)
        topi = at3(W + 8960, HP, TOPK).bitcast(U32)
        topf = at3(W + 9216, HP, TOPK)
        best = at3(W + 9472, PH, TOPK)
        bestj = at3(W + 9600, PH, TOPK).bitcast(U32)
        ja, jb = at3(W + 9728, PH, TOPK), at3(W + 9856, PH, TOPK)
        i1, i2 = at(W + 9984, P), at(W + 10112, P)
        wo_t = [at(R_OT + 1024 * b, 1024) for b in range(2)]
        ln1 = [at(R_HG, D), at(R_HG + D, D)]
        ln2 = [mods[0], mods[1]]
        qT = gT[1]
        score = [at3(R_OT + D * i, HP, NK) for i in range(NT)]
        cand = at(R_HG, D).rearrange("p (h a b) -> p h a b", h=PH, a=TOPK)
        onehot = at(R_HG + D, D).rearrange("p (h a b) -> p h a b", h=PH, a=TOPK)
        uslot = [at(o, D) for o in [R_RING + D * i for i in range(4)] + [R_PADA, R_PADA + D, R_HT, R_HT + D]]
        vslot = [at(o, D) for o in [R_G + D * i for i in range(4)] + [R_HG, R_HG + D, R_OT, R_OT + D]]
        diag = [at(R_MODS + 2 * D + P * i, P) for i in range(8)]

        in_cst, in_par, in_pos, in_x, in_kr, in_bada = (sem(n) for n in ("in_cst", "in_par", "in_pos", "in_x", "in_kr", "in_bada"))
        in_ring = [sem(f"in_ring{i}") for i in range(RING)]
        in_head = [sem(f"in_head{i}") for i in range(2)]
        in_wg, in_x2, in_ln1, in_ln2, in_keys, in_pb = (sem(n) for n in ("in_wg", "in_x2", "in_ln1", "in_ln2", "in_keys", "in_pb"))
        in_pada = [sem(f"in_pada{i}") for i in range(2)]
        in_u = [sem(f"in_u{i}") for i in range(8)]
        in_v = [sem(f"in_v{i}") for i in range(8)]
        dve_s, act_s, pool_s = sem("dve_self"), sem("act_self"), sem("pool_self")
        pool_gate = sem("pool_gate")
        acc_zero, ada_used, cact_ok = sem("acc_zero"), sem("ada_used"), sem("cact_ok")
        cols_t, cols_ok, sigc_ok, y_need, y_ok = (sem(n) for n in ("cols_t", "cols_ok", "sigc_ok", "y_need", "y_ok"))
        r_ok, sin_ok = sem("angles_ok"), sem("sin_ok")
        xT_done, xT_out, acc_ok, modc_done, hT_ok = (sem(n) for n in ("xT_done", "xT_out", "acc_ok", "modc_done", "hT_ok"))
        unit_used, out_act, out_dve = (sem(n) for n in ("unit_used", "out_act", "out_dve"))
        kr_done, kr_out, krot_done, kr_ok = (sem(n) for n in ("kr_done", "kr_out", "krot_done", "kr_ok"))
        sq_ok, ssq_done, std_ok, lat_ok = (sem(n) for n in ("sq_ok", "ssq_done", "std_ok", "lat_ok"))
        h_qr, h_qrout, h_qk, h_qkout, h_rot, h_rope, h_v, h_vout = (sem(f"h_{n}") for n in ("qr", "qrout", "qk", "qkout", "rot", "rope", "v", "vout"))
        h_s, h_neg, h_exp, h_p, h_t, h_tout, h_o, h_oout = (sem(f"h_{n}") for n in ("s", "neg", "exp", "p", "t", "tout", "o", "oout"))
        xc_ok, gates_done, gates_out, tanh_ok, sqrt_ok, gelu_in, gelu_ok, hg_ok = (sem(n) for n in (
            "xc_ok", "gates_done", "gates_out", "tanh_ok", "sqrt_ok", "gelu_in", "gelu_ok", "hg_ok"))
        mod_part, mod_done, mod_ok, mix_ok = (sem(n) for n in ("mod_part", "mod_done", "mod_ok", "mix_ok"))
        keys_t, keys_ok = sem("keys_t"), sem("keys_ok")
        var_ok, std1_ok, h2_ok, h2T_done, h2T_out = (sem(n) for n in ("var_ok", "std1_ok", "h2_ok", "h2T_done", "h2T_out"))
        sc_done, sc_out, best_ok, gexp_ok, topk_ok = (sem(n) for n in ("sc_done", "sc_out", "best_ok", "gexp_ok", "topk_ok"))
        dots_done, z_ok, a_ok, diag_ok, pv_done, y_done = (sem(n) for n in ("dots_done", "z_ok", "a_ok", "diag_ok", "pv_done", "y_done"))
        ln2_ok, in_out = sem("ln2_ok"), sem("in_out")

        wv = {n: t[n][0].rearrange("(t p) c -> p t c", p=P) for n in ("w_in", "w_rnn_out", "w_mla_out", "w_o", "peer_wq")}
        ada_v = t["w_ada"][0].rearrange("(t p) c -> p t c", p=P)
        uq_v = t["w_uq"][0].rearrange("(t p) c -> p t c", p=P)
        ukv_v = t["w_ukv"][0].rearrange("(t p) c -> p t c", p=P)
        rows = {n: t[n].rearrange("a (r c) -> (a r) c", c=P) for n in ("conv_b", "b_rg_a", "b_rg_x", "rg_lambda", "c", "q_norm_g", "kv_norm_g")}
        conv_rows = t["conv_w"][0].rearrange("w (r c) -> (w r) c", c=P)

        block = ctx.enter_context(nc.Block())

        def psblock(b):
            return ps[:, 2 * (b % 2):2 * (b % 2) + 2, :]

        @block.sync
        def _(sp):
            sp.dma_start(cst, t["cst"]).then_inc(in_cst, 16)
            for o, n in ((0, "c"), (16, "q_norm_g"), (20, "kv_norm_g")):
                r = rows[n]
                sp.dma_start(arena[o:o + r.shape[0], W + 9344:W + 9472], r).then_inc(in_par, 16)
            sp.dma_start(arena[0:64, W + 9216:W + 9344], conv_rows).then_inc(in_par, 16)
            for i, n in enumerate(("conv_b", "b_rg_a", "b_rg_x", "rg_lambda")):
                sp.dma_start(arena[64 + 16 * i:80 + 16 * i, W + 9216:W + 9344], rows[n]).then_inc(in_par, 16)
            sp.wait_ge(acc_zero, 2)
            for i in range(2):
                sp.dma_start(acc[i][0:1, :], t["b_ada"][:, i * D:(i + 1) * D]).then_inc(in_bada, 16)
            pos = t["positions"]
            sp.dma_start(pt[0].bitcast(I32), bass.AP(pos.tensor, pos.offset, [[0, ROPE], [1, S]])).then_inc(in_pos, 16)
            for ch in range(2):
                def ada(i, first):
                    for s in range(RING):
                        if not first:
                            sp.wait_ge(ada_used, i * RING + (s - 3 + ch * KT))
                        sp.dma_start(ring[s], ada_v[:, bass.ds(i * RING + s, 1), ch * D:(ch + 1) * D].rearrange("p t c -> p (t c)")
                                     ).then_inc(in_ring[s], 16)
                if ch == 0:
                    ada(0, True)
                    sp.dma_start(xin[:, :, :], t["x"][0].rearrange("(t p) c -> p t c", p=P)).then_inc(in_x, 16)
                with sp.Fori(1 - ch, KT // RING) as i:
                    ada(i, False)

            def units(w, col, b, wait_dve=False):
                for s in range(RING):
                    if wait_dve:
                        sp.wait_ge(ada_used, ADA_UNITS - 3 + s)
                    else:
                        sp.wait_ge(unit_used, b * RING + (s - 3))
                    sp.dma_start(ring3[s], wv[w][:, 4 * s:4 * s + 4, bass.ds(col, 512)]).then_inc(in_ring[s], 16)

            units("w_in", C_QC, B_QC, wait_dve=True)
            sp.dma_start(krw, wv["w_in"][:, :, C_KR:C_KR + ROPE]).then_inc(in_kr, 16)
            units("w_in", C_KVC, B_KVC)
            for b in range(2):
                sp.dma_start(uq[b], uq_v[:, :, b * 192:b * 192 + 192]).then_inc(in_head[b], 16)
                sp.dma_start(ukv[b], ukv_v[:, :, b * 256:b * 256 + 256]).then_inc(in_head[b], 16)
            with sp.Fori(1, HEADS // 2) as i:
                for b in range(2):
                    sp.wait_ge(h_v, i * 2 + (b - 1))
                    sp.dma_start(uq[b], uq_v[:, :, bass.ds(i * 384 + b * 192, 192)]).then_inc(in_head[b], 16)
                    sp.dma_start(ukv[b], ukv_v[:, :, bass.ds(i * 512 + b * 256, 256)]).then_inc(in_head[b], 16)
            with sp.Fori(0, 4) as g:
                units("w_in", g * 512 + C_XR, g * 2 + B_XR)
                sp.wait_ge(gates_done, g + 1)
                sp.wait_ge(h_oout, HEADS)
                for k, n in enumerate(("w_rg_a", "w_rg_x")):
                    sp.dma_start(wg[:, k, :, :], t[n][0].rearrange("h i j -> i h j")[:, bass.ds(g * 4, 4), :]).then_inc(in_wg, 16)
                units("w_in", g * 512 + C_GR, g * 2 + B_XR + 1)
            with sp.Fori(0, 4) as g:
                units("w_in", g * 512 + C_GRNN, g * 2 + B_G)
                units("w_in", g * 512 + C_GMLA, g * 2 + B_G + 1)
            with sp.Fori(0, 4) as g:
                units("w_rnn_out", g * 512, g + B_RNN)
            sp.wait_ge(hg_ok, 5)
            sp.dma_start(at3(W, NT, D), t["x"][0].rearrange("(t p) c -> p t c", p=P)).then_inc(in_x2, 16)
            sp.dma_start(keys, t["peer_keys"][0].rearrange("a n d -> n a d")).then_inc(in_keys, 16)
            with sp.Fori(0, 4) as g:
                units("w_mla_out", g * 512, g + B_MLA)
            with sp.Fori(0, 4) as g:
                units("w_o", g * 512, g + B_O)
            sp.wait_ge(unit_used, 4 * (B_RNN + 4))
            for i, n in enumerate(("ln1_g", "ln1_b")):
                sp.dma_start(ln1[i], bass.AP(t[n].tensor, t[n].offset, [[0, P], [1, D]])).then_inc(in_ln1, 16)
            with sp.Fori(0, 4) as g:
                units("peer_wq", g * 512, g + B_WQ)
            sp.wait_ge(h2_ok, NT)
            for i, n in enumerate(("ln2_g", "ln2_b")):
                sp.dma_start(ln2[i], bass.AP(t[n].tensor, t[n].offset, [[0, P], [1, D]])).then_inc(in_ln2, 16)
            for T in range(NT):
                sp.wait_ge(ln2_ok, T + 1)
                sp.dma_start(out[0, T * P:(T + 1) * P, :], x1[T]).then_inc(in_out, 16)
            sp.wait_ge(in_out, 16 * NT)

        @block.gpsimd
        def _(pool):
            me = Chain(pool, pool_s)
            for ch in range(4):
                me.do(pool.memset(mods[ch], 0.0))
                me.wait()
                pool.dma_start(mods[ch][0:1, :], t["b_ada"][:, (2 + ch) * D:(3 + ch) * D]).then_inc(in_pb, 16)

            def ada_load(kt, ch):
                pool.dma_start(pada[ch % 2], ada_v[:, bass.ds(kt, 1), (2 + ch) * D:(3 + ch) * D].rearrange("p t c -> p (t c)")
                               ).then_inc(in_pada[ch % 2], 16)

            def ada_tile(kt, last):
                for ch in range(4):
                    b = ch % 2
                    pool.wait_ge(in_pada[b], kt * 32 + 16 * (ch // 2 + 1))
                    pool.sem_inc(pool_gate, 1)
                    me.do(pool.tensor_tensor(pada[b], pada[b], cact[:, bass.ds(kt, 1)].to_broadcast([P, D]), ALU.mult))
                    me.wait()
                    me.do(pool.tensor_tensor(mods[ch], mods[ch], pada[b], ALU.add))
                    me.wait()
                    pool.sem_inc(pool_gate, 1)
                    if ch < 2:
                        ada_load(kt, ch + 2)
                    elif not last:
                        ada_load(kt + 1, ch - 2)

            for ch in range(2):
                ada_load(0, ch)
            pool.wait_ge(cact_ok, 1)
            pool.wait_ge(in_pb, 64)
            with pool.Fori(0, KT - 1) as kt:
                me.enter(kt, 0, 8)
                ada_tile(kt, False)
            me.leave(KT - 1)
            ada_tile(KT - 1, True)
            pool.sem_inc(mod_part, 1)

            def gathers(T, i, first):
                for b in range(2):
                    n4 = T * EXPERTS + b * GROUP + (i * 2 * GROUP)
                    if first:
                        if b == 1:
                            pool.wait_ge(topk_ok, NT)
                    else:
                        pool.wait_ge(dots_done, n4 - GROUP)
                        pool.sem_inc(pool_gate, 1)
                    me.do(pool.tensor_copy(idxu[:, b * GROUP:(b + 1) * GROUP], idx[T][:, bass.ds(i * 2 * GROUP + b * GROUP, GROUP)]))
                    me.wait()
                    pool.sem_inc(pool_gate, 1)
                    for s in range(GROUP * b, GROUP * (b + 1)):
                        pool.indirect_dma_start(uslot[s], None, t["peer_u"][0], bass.IndirectOffsetOnAxis(idxu[:, s:s + 1], 0)
                                                ).then_inc(in_u[s], 16)
                    if not first:
                        pool.wait_ge(pv_done, n4 - GROUP)
                        pool.sem_inc(pool_gate, 1)
                    me.do(pool.tensor_copy(idxv[:, b * GROUP:(b + 1) * GROUP], idx[T][:, bass.ds(i * 2 * GROUP + b * GROUP, GROUP)]))
                    me.wait()
                    pool.sem_inc(pool_gate, 1)
                    for s in range(GROUP * b, GROUP * (b + 1)):
                        pool.indirect_dma_start(vslot[s], None, t["peer_v"][0], bass.IndirectOffsetOnAxis(idxv[:, s:s + 1], 0)
                                                ).then_inc(in_v[s], 16)

            for T in range(NT):
                pool.wait_ge(topk_ok, T + 1)
                if T == 0:
                    gathers(T, 0, True)
                with pool.Fori(1 - T, NGROUP // 2) as i:
                    me.enter(i, 1 - T, 4)
                    gathers(T, i, False)
                me.leave(NGROUP // 2 - 1 + T)

        @block.tensor
        def _(pe):
            def mm(o, l, r, start, stop, **k):
                return pe.matmul(o, l, r, start=start, stop=stop, skip_group_check=True, **k)

            pe.wait_ge(in_cst, 16)
            pe.wait_ge(in_par, 128)
            pe.transpose(ps[:, 0, 0:24], stB, ident[0:24, 0:24]).then_inc(cols_t, 1)
            pe.transpose(ps[:, 1, 0:P], stA, ident).then_inc(cols_t, 1)
            pe.wait_ge(in_x, 16)
            for g in range(KT // 2):
                if g >= 4:
                    pe.wait_ge(xT_out, g - 3)
                for a in range(2):
                    for T in range(NT):
                        last = pe.transpose(ps[:, 4 + g % 4, a * S + T * P:a * S + (T + 1) * P],
                                            xin[:, T, (2 * g + a) * P:(2 * g + a + 1) * P], ident)
                last.then_inc(xT_done, 1)
            for i in range(2):
                pe.wait_ge(acc_ok, i + 1)
                for k in range(KT):
                    last = mm(ps[:, 2, i * KT + k:i * KT + k + 1], acc[i][:, k * P:(k + 1) * P], ones[:, 0:1], True, True)
                last.then_inc(modc_done, 1)

            def channel_block(b, src, wait=None):
                o = psblock(b).rearrange("p b (h c) -> p (b h) c", h=2)
                for s in range(RING):
                    pe.wait_ge(in_ring[s], b * 16 + 16 * (ADA_UNITS // RING + 1))
                    for k in range(4):
                        kt = 4 * s + k
                        if wait is not None:
                            wait(kt)
                        for m in range(4):
                            last = mm(o[:, m, :], ring3[s][:, k, m * P:(m + 1) * P], src[:, kt, :],
                                      kt == 0 and m % 2 == 0, kt == KT - 1)
                    last.then_inc(unit_used, 1)

            channel_block(B_QC, hT, wait=lambda kt: pe.wait_ge(hT_ok, kt + 1))
            pe.wait_ge(in_kr, 16)
            pe.wait_ge(xT_out, KT // 2)
            for kt in range(KT):
                last = mm(ps[0:ROPE, 4, 0:S], krw[:, kt, :], hT[:, kt, :], kt == 0, kt == KT - 1)
            last.then_inc(kr_done, 1)
            channel_block(B_KVC, hT)
            pe.wait_ge(kr_out, 1)
            mm(ps[0:ROPE, 5, 0:S], cst[0:ROPE, K_ROT:K_ROT + ROPE], krraw, True, True).then_inc(krot_done, 1)
            for i in range(2):
                pe.wait_ge(sq_ok, i + 1)
                for k in range(LT):
                    last = mm(ps[:, 6 + i, 0:S], ones, sq2[i][:, k, :], k == 0, k == LT - 1)
                last.then_inc(ssq_done, 1)
            pe.wait_ge(lat_ok, 2)
            pe.wait_ge(kr_ok, 1)

            def transposes(h):
                pe.wait_ge(h_p, h + 1)
                for j in range(3):
                    last = pe.transpose(ps[:, 4, j * P:(j + 1) * P], sc[:, j * P:(j + 1) * P], ident)
                last.then_inc(h_t, 1)

            def values(h, n):
                pe.wait_ge(h_tout, h + 1)
                pe.wait_ge(h_vout, h + 1)
                if n:
                    pe.wait_ge(h_oout, h)
                mm(ps[:, 5, 0:P], vv[:, 0, :], pT[:, 0, :], True, True)
                mm(ps[:, 5, P:2 * P], vv[:, 0, :], pT[:, 1, :], True, False)
                mm(ps[:, 5, P:2 * P], vv[:, 1, :], pT[:, 2, :], False, True).then_inc(h_o, 1)

            def head(i, b, first):
                h = i * 2 + b
                pe.wait_ge(in_head[b], i * 32 + 32)
                if not first:
                    pe.wait_ge(h_rope, h)
                for k in range(LT):
                    last = mm(ps[0:ROPE, 0, 0:S], uq[b][:, k, NOPE:NOPE + ROPE], qcT[:, k, :], k == 0, k == LT - 1)
                last.then_inc(h_qr, 1)
                if not first:
                    pe.wait_ge(h_qkout, h)
                for k in range(LT):
                    mm(ps[:, 1, 0:S], uq[b][:, k, 0:NOPE], qcT[:, k, :], k == 0, k == LT - 1)
                for k in range(LT):
                    last = mm(ps[:, 1, S:2 * S], ukv[b][:, k, 0:NOPE], kvT[:, k, :], k == 0, k == LT - 1)
                last.then_inc(h_qk, 1)
                pe.wait_ge(h_qrout, h + 1)
                mm(ps[:, 0, S:2 * S], cst[0:ROPE, K_ROT:K_ROT + P], qr, True, True).then_inc(h_rot, 1)
                if not first:
                    pe.wait_ge(h_vout, h)
                for T in range(NT):
                    for k in range(LT):
                        last = mm(ps[:, 2, T * P:(T + 1) * P], kvT[:, k, T * P:(T + 1) * P], ukv[b][:, k, NOPE:], k == 0, k == LT - 1)
                last.then_inc(h_v, 1)
                if not first:
                    transposes(h - 1)
                pe.wait_ge(h_qkout, h + 1)
                pe.wait_ge(h_rope, h + 1)
                for T in range(NT):
                    o = ps[:, 3, T * P:(2 * T + 1) * P]
                    n = (T + 1) * P
                    mm(o, qn[:, T * P:(T + 1) * P], kn[:, 0:n], True, False)
                    last = mm(o, qro[:, T * P:(T + 1) * P], krT[:, 0:n], False, True)
                last.then_inc(h_s, 1)

            head(0, 0, True)
            head(0, 1, False)
            values(0, False)
            with pe.Fori(1, HEADS // 2) as i:
                for b in range(2):
                    head(i, b, False)
                    values(i * 2 + (b - 1), True)
            transposes(HEADS - 1)
            values(HEADS - 1, True)

            pe.wait_ge(h_oout, HEADS)
            pe.sem_inc(gates_done, 1)
            with pe.Fori(0, 4) as g:
                for k2 in range(2):
                    pe.wait_ge(out_act, g * 2 + (k2 + 1))
                    o = ps[:, 2 * k2:2 * k2 + 2, :].rearrange("p b (h c) -> p (b h) c", h=2)
                    for s in range(RING):
                        pe.wait_ge(in_ring[s], g * 32 + 16 * (B_XR + k2 + ADA_UNITS // RING + 1))
                        for k in range(4):
                            kt = 4 * s + k
                            for m in range(4):
                                last = mm(o[:, m, :], ring3[s][:, k, m * P:(m + 1) * P], hT[:, kt, :],
                                          kt == 0 and m % 2 == 0, kt == KT - 1)
                        last.then_inc(unit_used, 1)
                pe.wait_ge(in_wg, g * 32 + 32)
                pe.wait_ge(xc_ok, g + 1)
                pe.wait_ge(gates_out, g * 2 + 1)
                for k in range(2):
                    for m in range(4):
                        last = mm(ps[:, 4 + 2 * k + m // 2, (m % 2) * S:(m % 2 + 1) * S], wg[:, k, m, :], quad(XC, m), True, True)
                last.then_inc(gates_done, 1)

            def loop_blocks(b0, n, src, evac, token=False):
                with pe.Fori(0, n // 2) as g:
                    for k2 in range(2):
                        evac(g, k2)
                        o = ps[:, 2 * k2:2 * k2 + 2, :]
                        oc = o.rearrange("p b (h c) -> p (b h) c", h=2)
                        for s in range(RING):
                            pe.wait_ge(in_ring[s], g * 32 + 16 * (b0 + k2 + ADA_UNITS // RING + 1))
                            for k in range(4):
                                kt = 4 * s + k
                                if token:
                                    for T in range(NT):
                                        last = mm(o[:, T, :], src[:, kt, T * P:(T + 1) * P], ring3[s][:, k, :], kt == 0, kt == KT - 1)
                                else:
                                    for m in range(4):
                                        last = mm(oc[:, m, :], ring3[s][:, k, m * P:(m + 1) * P], src[:, kt, :],
                                                  kt == 0 and m % 2 == 0, kt == KT - 1)
                            last.then_inc(unit_used, 1)

            loop_blocks(B_G, 8, hT, lambda g, k: pe.wait_ge(out_act, g * 2 + (B_G + k - 1)))
            pe.wait_ge(hg_ok, 5)
            pe.wait_ge(out_act, B_RNN)
            loop_blocks(B_RNN, 4, hgT, lambda g, k: pe.wait_ge(out_dve, g * 2 + 1))
            loop_blocks(B_MLA, 4, oT, lambda g, k: pe.wait_ge(out_dve, g * 2 + (4 + k)))
            pe.wait_ge(in_keys, 16)
            pe.wait_ge(gates_out, 9)
            for a in range(2):
                last = pe.transpose(ps[:, 6, a * P:(a + 1) * P], keys[:, a, :], ident)
            last.then_inc(keys_t, 1)

            def modulation(ch):
                pe.wait_ge(mod_part, 1)
                if ch:
                    pe.wait_ge(mod_ok, ch)
                else:
                    pe.wait_ge(keys_ok, 1)
                for j in range(4):
                    last = mm(ps[:, 4 + j, :], ones, mods[ch][:, j * 512:(j + 1) * 512], True, True)
                last.then_inc(mod_done, 1)

            modulation(0)
            pe.wait_ge(mix_ok, 4)
            loop_blocks(B_O, 4, gT[0], lambda g, k: pe.wait_ge(out_dve, g * 2 + (8 + k)), token=True)
            for ch in range(1, 4):
                modulation(ch)
            pe.wait_ge(mod_ok, 4)
            for T in range(NT):
                pe.wait_ge(h2_ok, T + 1)
                for g in range(KT // 4):
                    if 4 * T + g >= 4:
                        pe.wait_ge(h2T_out, 4 * T + g - 3)
                    for a in range(4):
                        last = pe.transpose(ps[:, 4 + g % 4, a * P:(a + 1) * P], h2[T][:, (4 * g + a) * P:(4 * g + a + 1) * P], ident)
                    last.then_inc(h2T_done, 1)
            pe.wait_ge(h2T_out, 8)
            pe.wait_ge(out_dve, 13)
            loop_blocks(B_WQ, 4, hT, lambda g, k: pe.wait_ge(out_act, g * 2 + (B_RNN - 1 + k)))
            pe.wait_ge(out_act, B_RNN + 4)
            for T in range(NT):
                if T:
                    pe.wait_ge(sc_out, 1)
                for q in range(HP):
                    last = mm(ps[:, 4 + q // 4, (q % 4) * P:(q % 4 + 1) * P], qT[:, q, T * P:(T + 1) * P], keysT[:, q % 2, :], True, True)
                last.then_inc(sc_done, 1)

            def products(T, i, first, final):
                for b in range(2):
                    for s in range(GROUP):
                        q = b * GROUP + s
                        pe.wait_ge(in_v[q], i * 16 + 16 * (T * NGROUP // 2 + 1))
                        pe.wait_ge(diag_ok, i * 2 * GROUP + (T * EXPERTS + q + 1))
                        for j in range(4):
                            last = mm(ps[:, 4 * T + j, :], diag[q], vslot[q][:, j * 512:(j + 1) * 512],
                                      first and q == 0, final and q == 2 * GROUP - 1)
                        last.then_inc(pv_done, 1)

            for T in range(NT):
                if T:
                    pe.wait_ge(sc_out, 2)
                products(T, 0, True, False)
                with pe.Fori(1, NGROUP // 2 - 1) as i:
                    products(T, i, False, False)
                products(T, NGROUP // 2 - 1, False, True)

        @block.scalar
        def _(act):
            me = Chain(act, act_s)
            A = act.activation
            act.wait_ge(cols_ok, 1)
            A(sigc, colB[:, 0:16], ACT.Sigmoid).then_inc(sigc_ok, 1)
            for g in range(KT // 2):
                act.wait_ge(xT_done, g + 1)
                A(at(R_HT + g * 2 * S, 2 * S), ps[:, 4 + g % 4, :], ACT.Copy).then_inc(xT_out, 1)
            act.wait_ge(y_need, 1)
            A(lt[1], lt[0], ACT.Exp, scale=-1.0).then_inc(y_ok, 1)
            act.wait_ge(r_ok, 1)
            A(pt[3], pt[2], ACT.Sin).then_inc(sin_ok, 1)
            A(pt[4], pt[2], ACT.Sin, scale=0.5).then_inc(sin_ok, 1)

            def evac_static(b, off):
                act.wait_ge(unit_used, 4 * (b + 1))
                A(at(off, 1024), psblock(b).rearrange("p b c -> p (b c)"), ACT.Copy).then_inc(out_act, 1)

            evac_static(B_QC, W)
            act.wait_ge(kr_done, 1)
            A(krraw, ps[0:ROPE, 4, 0:S], ACT.Copy).then_inc(kr_out, 1)
            evac_static(B_KVC, W + 1024)
            for i in range(2):
                act.wait_ge(ssq_done, i + 1)
                A(rs2[i], ps[:, 6 + i, 0:S], ACT.Sqrt, bias=eps_rms, scale=1.0 / RANK).then_inc(std_ok, 1)

            def head(i, b, first):
                h = i * 2 + b
                act.wait_ge(h_qr, h + 1)
                A(qr, ps[0:ROPE, 0, 0:S], ACT.Copy).then_inc(h_qrout, 1)
                act.wait_ge(h_qk, h + 1)
                if not first:
                    act.wait_ge(h_s, h)
                A(qkn, ps[:, 1, :], ACT.Copy).then_inc(h_qkout, 1)
                act.wait_ge(h_v, h + 1)
                if not first:
                    act.wait_ge(h_o, h)
                    A(arena[:, bass.ds((h - 1) * S + R_OT, S)], ps[:, 5, 0:S], ACT.Copy).then_inc(h_oout, 1)
                A(at(W + 3840, NT * VH), ps[:, 2, 0:NT * VH], ACT.Copy).then_inc(h_vout, 1)
                act.wait_ge(h_neg, h + 1)
                A(sc[:, 0:P], sc[:, 0:P], ACT.Exp, bias=snm[:, 0:1], scale=SM_SCALE, accum_out=ssum[:, 0:1])
                A(sc[:, P:3 * P], sc[:, P:3 * P], ACT.Exp, bias=snm[:, 1:2], scale=SM_SCALE, accum_out=ssum[:, 1:2]).then_inc(h_exp, 1)

            head(0, 0, True)
            head(0, 1, False)
            with act.Fori(1, HEADS // 2) as i:
                for b in range(2):
                    head(i, b, False)
            act.wait_ge(h_o, HEADS)
            A(at(R_OT + (HEADS - 1) * S, S), ps[:, 5, 0:S], ACT.Copy).then_inc(h_oout, 1)

            act.sem_inc(gates_out, 1)
            with act.Fori(0, 4) as g:
                act.wait_ge(unit_used, g * 8 + 4 * (B_XR + 1))
                A(at(XR, 1024), ps[:, 0:2, :].rearrange("p b c -> p (b c)"), ACT.Copy).then_inc(out_act, 1)
                act.wait_ge(unit_used, g * 8 + 4 * (B_XR + 2))
                act.wait_ge(hg_ok, g + 1)
                A(at(GR, 1024), ps[:, 2:4, :].rearrange("p b c -> p (b c)"), ACT.Copy).then_inc(out_act, 1)
                act.wait_ge(gates_done, g + 2)
                for m in range(4):
                    last = A(quad(RR, m), ps[:, 4 + m // 2, (m % 2) * S:(m % 2 + 1) * S], ACT.Sigmoid, bias=ba_c[:, bass.ds(g * 4 + m, 1)])
                last.then_inc(gates_out, 1)
                for m in range(4):
                    last = A(quad(II, m), ps[:, 6 + m // 2, (m % 2) * S:(m % 2 + 1) * S], ACT.Sigmoid, bias=bx_c[:, bass.ds(g * 4 + m, 1)])
                last.then_inc(gates_out, 1)
                act.wait_ge(gates_out, g * 2 + 3)
                for m in range(4):
                    last = A(quad(TP, m), quad(RR, m), ACT.Tanh, scale=sp4[:, bass.ds(g * 4 + m, 1)])
                last.then_inc(tanh_ok, 1)
                act.wait_ge(gelu_in, g + 1)
                A(at(GT, 1024), at(GT, 1024), ACT.Sigmoid, scale=GELU_S).then_inc(gelu_ok, 1)
                act.wait_ge(tanh_ok, g + 1)
                A(at(RR, 1024), at(TP, 1024), ACT.Sqrt).then_inc(sqrt_ok, 1)

            with act.Fori(0, 4) as g:
                for k in range(2):
                    act.wait_ge(unit_used, g * 8 + 4 * (B_G + k + 1))
                    A(arena[:, bass.ds(g * 1024 + (R_G + 4096 * k), 1024)], ps[:, 2 * k:2 * k + 2, :].rearrange("p b c -> p (b c)"),
                      ACT.Sigmoid).then_inc(out_act, 1)

            act.wait_ge(keys_t, 1)
            A(at(W + 8448, 2 * P), ps[:, 6, 0:2 * P], ACT.Copy).then_inc(keys_ok, 1)

            def modulation(ch):
                act.wait_ge(mod_done, ch + 1)
                A(mods[ch], ps[:, 4:8, :].rearrange("p b c -> p (b c)"), ACT.Copy, bias=0.0 if ch == 1 else 1.0).then_inc(mod_ok, 1)

            for ch in range(4):
                modulation(ch)
            for T in range(NT):
                act.wait_ge(var_ok, T + 1)
                A(rstd[:, 0:1], mv[:, 1:2], ACT.Sqrt, bias=eps_ln).then_inc(std1_ok, 1)
            for T in range(NT):
                for g in range(KT // 4):
                    act.wait_ge(h2T_done, 4 * T + g + 1)
                    A(hT[:, 4 * g:4 * g + 4, T * P:(T + 1) * P], ps[:, 4 + g % 4, :].rearrange("p (a c) -> p a c", a=4), ACT.Copy).then_inc(h2T_out, 1)
            with act.Fori(0, 2) as g:
                for k in range(2):
                    act.wait_ge(unit_used, g * 8 + 4 * (B_WQ + k + 1))
                    A(arena[:, bass.ds(g * 2048 + (R_G + 4096 + 1024 * k), 1024)], ps[:, 2 * k:2 * k + 2, :].rearrange("p b c -> p (b c)"),
                      ACT.Copy).then_inc(out_act, 1)
            for T in range(NT):
                act.wait_ge(sc_done, T + 1)
                A(at(R_OT + D * T, D), ps[:, 4:8, :].rearrange("p b c -> p (b c)"), ACT.Copy).then_inc(sc_out, 1)
            for T in range(NT):
                act.wait_ge(best_ok, T + 1)
                A(gate_w[T], gate_w[T], ACT.Exp).then_inc(gexp_ok, 1)

            def diagonals(T, i, first):
                for b in range(2):
                    c0, c1 = b * GROUP, (b + 1) * GROUP
                    act.wait_ge(z_ok, i * 2 + (T * NGROUP + b + 1))
                    me.do(A(zs[:, c0:c1], zu[:, c0:c1], ACT.Sigmoid, scale=GELU_S))
                    me.wait()
                    for s in range(c0, c1):
                        last = A(za[:, s:s + 1], zs[:, s:s + 1], ACT.Copy, scale=zg[:, s:s + 1])
                    last.then_inc(a_ok, 1)
                    act.wait_ge(a_ok, i * 2 + (T * NGROUP + b + 1))
                    for s in range(c0, c1):
                        if not first:
                            act.wait_ge(pv_done, i * 2 * GROUP + (T * EXPERTS + s - 2 * GROUP + 1))
                        A(diag[s], ident, ACT.Copy, scale=za[:, s:s + 1]).then_inc(diag_ok, 1)

            def ln2_std(T):
                act.wait_ge(var_ok, NT + T + 1)
                A(rstd[:, 0:1], mv[:, 1:2], ACT.Sqrt, bias=eps_ln).then_inc(std1_ok, 1)

            for T in range(NT):
                diagonals(T, 0, T == 0)
                if T:
                    ln2_std(0)
                with act.Fori(1, NGROUP // 2) as i:
                    me.enter(i, 1, 2)
                    diagonals(T, i, False)
                me.leave(NGROUP // 2 - 1)
            ln2_std(1)

        @block.vector
        def _(dve):
            me = Chain(dve, dve_s)
            V = dve
            TT, TS, STT = V.tensor_tensor, V.tensor_scalar, V.scalar_tensor_tensor
            V.memset(acc[0], 0.0).then_inc(acc_zero, 1)
            V.memset(acc[1], 0.0).then_inc(acc_zero, 1)
            me.do(V.memset(eps_rms, RMS_EPS))
            me.do(V.memset(eps_ln, LN_EPS))
            dve.wait_ge(cols_t, 1)
            V.tensor_copy(colB, ps[:, 0, 0:24]).then_inc(cols_ok, 1)
            dve.wait_ge(cols_ok, 1)
            dve.wait_ge(sigc_ok, 1)
            me.do(TT(cact, colB[:, 0:16], sigc, ALU.mult))
            me.wait()
            dve.sem_inc(cact_ok, 1)
            dve.wait_ge(in_bada, 32)
            for ch in range(2):
                with dve.Fori(0, KT // RING) as i:
                    for s in range(RING):
                        dve.wait_ge(in_ring[s], i * 16 + 16 * (ch * (KT // RING) + 1))
                        STT(acc[ch], ring[s], cact[:, bass.ds(i * RING + s, 1)], acc[ch], ALU.mult, ALU.add).then_inc(ada_used, 1)
                        dve.wait_ge(ada_used, i * RING + (ch * KT + s + 1))
                dve.sem_inc(acc_ok, 1)
                if ch == 1:
                    break
                dve.wait_ge(cols_t, 2)
                me.do(V.tensor_copy(colA, ps[:, 1, 0:P]))
                me.wait()
                me.do(TS(lt[3], lam_c, -1.0, None, ALU.mult))
                me.wait()
                me.do(TT(lt[0], lt[3], lam_c, ALU.max))
                me.wait()
                dve.sem_inc(y_need, 1)
                dve.wait_ge(y_ok, 1)
                me.do(TS(lt[2], lt[1], 2.0, None, ALU.add))
                me.wait()
                me.do(V.reciprocal(lt[2], lt[2]))
                me.wait()
                me.do(TT(lt[1], lt[1], lt[2], ALU.mult))
                me.wait()
                me.do(TT(lt[2], lt[1], lt[1], ALU.mult))
                me.wait()
                me.do(TS(lt[4], lt[2], 1.0 / 19.0, None, ALU.mult))
                me.wait()
                for k in range(17, 2, -2):
                    me.do(STT(lt[4], lt[4], 1.0 / k, lt[2], ALU.add, ALU.mult))
                    me.wait()
                me.do(STT(lt[4], lt[4], 1.0, lt[1], ALU.add, ALU.mult))
                me.do(TS(lt[3], lt[3], 0.0, 4.0, ALU.max, ALU.mult))
                me.wait()
                me.do(STT(sp4, lt[4], 8.0, lt[3], ALU.mult, ALU.add))
                dve.wait_ge(in_pos, 16)
                me.do(V.tensor_copy(pt[1], pt[0].bitcast(I32)))
                me.wait()
                me.do(TS(pt[1], pt[1], cst[0:ROPE, K_INVF:K_INVF + 1], None, ALU.mult))
                me.wait()
                magic = 1.5 * 2.0 ** 23
                me.do(TS(pt[3], pt[1], 1.0 / (2.0 * math.pi), magic, ALU.mult, ALU.add))
                me.wait()
                me.do(TS(pt[3], pt[3], -magic, None, ALU.add))
                me.wait()
                c1 = 6.28125
                c2 = float(np.float32(np.round((2.0 * math.pi - c1) * 2.0 ** 21) / 2.0 ** 21))
                c3 = 2.0 * math.pi - c1 - c2
                src = pt[1]
                for c in (c1, c2, c3):
                    me.do(STT(pt[2], pt[3], -c, src, ALU.mult, ALU.add))
                    me.wait()
                    src = pt[2]
                me.do(TS(pt[2], pt[2], 3.1415925, -3.1415925, ALU.min, ALU.max))
                me.wait()
                dve.sem_inc(r_ok, 1)
                dve.wait_ge(sin_ok, 2)
                me.do(V.tensor_copy(sinT, pt[3]))
                me.do(TT(pt[4], pt[4], pt[4], ALU.mult))
                me.wait()
                me.do(TS(cosT, pt[4], -2.0, 1.0, ALU.mult, ALU.add))
            dve.wait_ge(modc_done, 2)
            me.do(V.tensor_copy(sh1, ps[:, 2, 0:KT]))
            me.do(TS(sc1, ps[:, 2, KT:2 * KT], 1.0, None, ALU.add))
            me.wait()
            dve.wait_ge(xT_out, KT // 2)
            for k in range(KT):
                TS(hT[:, k, :], hT[:, k, :], sc1[:, k:k + 1], sh1[:, k:k + 1], ALU.mult, ALU.add).then_inc(hT_ok, 1)
            for i, lat in enumerate((qcT, kvT)):
                dve.wait_ge(out_act, i + 1)
                TT(sq2[i], lat, lat, ALU.mult).then_inc(sq_ok, 1)
            dve.wait_ge(krot_done, 1)
            me.do(TT(rt, krraw, cosT, ALU.mult))
            me.do(TT(krT, ps[0:ROPE, 5, 0:S], sinT, ALU.mult))
            me.wait()
            TT(krT, krT, rt, ALU.add).then_inc(kr_ok, 1)
            for i, lat in enumerate((qcT, kvT)):
                dve.wait_ge(std_ok, i + 1)
                me.do(V.reciprocal(rs2[i], rs2[i]))
                me.wait()
                for k in range(LT):
                    last = STT(lat[:, k, :], lat[:, k, :], colB[:, 16 + LT * i + k:17 + LT * i + k], rs2[i], ALU.mult, ALU.mult)
                last.then_inc(lat_ok, 1)

            def transposed_out(h):
                dve.wait_ge(h_t, h + 1)
                if True:
                    V.tensor_copy(at(W + 4736, 3 * P), ps[:, 4, 0:3 * P]).then_inc(h_tout, 1)

            def softmax(h, first):
                dve.wait_ge(h_s, h + 1)
                if not first:
                    dve.wait_ge(h_t, h)
                me.do(TT(sc, ps[:, 3, 0:3 * P], cst[:, K_MASK:K_MASK + 3 * P], ALU.add))
                me.wait()
                me.do(V.tensor_reduce(smx[:, 0:1], sc[:, 0:P], AX_X, ALU.max))
                me.do(V.tensor_reduce(smx[:, 1:2], sc[:, P:3 * P], AX_X, ALU.max))
                me.wait()
                TS(snm, smx, -SM_SCALE, None, ALU.mult).then_inc(h_neg, 1)
                dve.wait_ge(h_exp, h + 1)
                me.do(V.reciprocal(srec, ssum))
                me.wait()
                me.do(TS(sc[:, 0:P], sc[:, 0:P], srec[:, 0:1], None, ALU.mult))
                TS(sc[:, P:3 * P], sc[:, P:3 * P], srec[:, 1:2], None, ALU.mult).then_inc(h_p, 1)

            def head(i, b, first):
                h = i * 2 + b
                dve.wait_ge(h_qrout, h + 1)
                me.do(TT(rt, qr, cosT, ALU.mult))
                dve.wait_ge(h_rot, h + 1)
                if not first:
                    dve.wait_ge(h_s, h)
                me.do(TT(qro, ps[0:ROPE, 0, S:2 * S], sinT, ALU.mult))
                me.wait()
                TT(qro, qro, rt, ALU.add).then_inc(h_rope, 1)
                if not first:
                    transposed_out(h - 1)
                softmax(h, first)

            head(0, 0, True)
            head(0, 1, False)
            with dve.Fori(1, HEADS // 2) as i:
                me.enter(i, 1, 14)
                for b in range(2):
                    head(i, b, False)
            me.leave(HEADS // 2 - 1)
            transposed_out(HEADS - 1)

            dve.sem_inc(hg_ok, 1)
            with dve.Fori(0, 4) as g:
                me.enter(g, 0, 30)
                dve.wait_ge(out_act, g * 2 + (B_XR + 1))
                for m in range(4):
                    me.do(TS(quad(XC, m), quad(XR, m), conv_c[:, bass.ds(g * 4 + (48 + m), 1)], convb_c[:, bass.ds(g * 4 + m, 1)], ALU.mult, ALU.add))
                for d in range(1, CONV):
                    me.wait()
                    for m in range(4):
                        o, x = at(XC + S * m + d, S - d), at(XR + S * m, S - d)
                        me.do(STT(o, x, conv_c[:, bass.ds(g * 4 + (16 * (3 - d) + m), 1)], o, ALU.mult, ALU.add))
                me.wait()
                dve.sem_inc(xc_ok, 1)
                dve.wait_ge(out_act, g * 2 + (B_XR + 2))
                gt, gr = at(GT, 1024), at(GR, 1024)
                me.do(TT(gt, gr, gr, ALU.mult))
                me.wait()
                me.do(TS(gt, gt, GELU_C, 1.0, ALU.mult, ALU.add))
                me.wait()
                TT(gt, gt, gr, ALU.mult).then_inc(gelu_in, 1)
                rr, ii, tp, qq, xc = (at(o, 1024) for o in (RR, II, TP, QQ, XC))
                dve.wait_ge(gates_out, g * 2 + 3)
                me.do(TT(ii, ii, xc, ALU.mult))
                dve.wait_ge(tanh_ok, g + 1)
                me.do(TS(qq, tp, 1.0, None, ALU.add))
                me.wait()
                me.do(V.reciprocal(qq, qq))
                me.wait()
                me.do(TT(ii, ii, qq, ALU.mult))
                dve.wait_ge(sqrt_ok, g + 1)
                me.do(TS(tp, qq, 2.0, -1.0, ALU.mult, ALU.add))
                me.wait()
                me.do(STT(ii, ii, 2.0, rr, ALU.mult, ALU.mult))
                dve.wait_ge(gelu_ok, g + 1)
                me.do(TT(gt, gt, gr, ALU.mult))
                me.wait()
                for m in range(4):
                    me.do(V.tensor_tensor_scan(quad(XC, m), quad(TP, m), quad(II, m), 0.0, ALU.mult, ALU.add))
                me.wait()
                me.do(TT(arena[:, bass.ds(g * 1024 + R_HG, 1024)], xc, gt, ALU.mult))
                me.wait()
                dve.sem_inc(hg_ok, 1)
            me.leave(4)

            dve.sem_inc(out_dve, 1)
            def gT_at(k, g, j):
                return arena[:, bass.ds(g * 2048 + (R_G + 4096 * k + 1024 * j), 1024)]

            with dve.Fori(0, 2) as g:
                me.enter(g, 0, 2)
                for k in range(2):
                    dve.wait_ge(unit_used, g * 8 + 4 * (B_RNN + k + 1))
                    me.do(TT(gT_at(0, g, k), gT_at(0, g, k), ps[:, 2 * k:2 * k + 2, :].rearrange("p b c -> p (b c)"), ALU.mult))
                    me.wait()
                    dve.sem_inc(out_dve, 1)
            me.leave(2)
            with dve.Fori(0, 2) as g:
                me.enter(g, 0, 4)
                for k in range(2):
                    dve.wait_ge(unit_used, g * 8 + 4 * (B_MLA + k + 1))
                    me.do(TT(gT_at(1, g, k), gT_at(1, g, k), ps[:, 2 * k:2 * k + 2, :].rearrange("p b c -> p (b c)"), ALU.mult))
                    me.wait()
                    dve.sem_inc(out_dve, 1)
                    me.do(TT(gT_at(0, g, k), gT_at(0, g, k), gT_at(1, g, k), ALU.add))
                    me.wait()
                    dve.sem_inc(mix_ok, 1)
            me.leave(2)
            dve.wait_ge(mod_ok, 1)
            dve.wait_ge(in_x2, 16)
            with dve.Fori(0, 2) as g:
                me.enter(g, 0, 8)
                for k in range(2):
                    dve.wait_ge(unit_used, g * 8 + 4 * (B_O + k + 1))
                    for T in range(NT):
                        me.do(TT(wo_t[k][:, T * 512:(T + 1) * 512], ps[:, 2 * k + T, :],
                                 arena[:, bass.ds(g * 1024 + (R_MODS + 512 * k), 512)], ALU.mult))
                    me.wait()
                    dve.sem_inc(out_dve, 1)
                    for T in range(NT):
                        xs = arena[:, bass.ds(g * 1024 + (W + D * T + 512 * k), 512)]
                        me.do(STT(xs, xs, ALPHA, wo_t[k][:, T * 512:(T + 1) * 512], ALU.mult, ALU.add))
            me.leave(2)

            def layer_norm(x, gb, n):
                me.wait()
                for j in range(4):
                    me.do(V.bn_stats(bn6[:, j, :], x[:, j * 512:(j + 1) * 512]))
                me.wait()
                me.do(V.bn_aggr(mv, bn6[:, :, :]))
                me.wait()
                dve.sem_inc(var_ok, 1)
                dve.wait_ge(std1_ok, n + 1)
                me.do(V.reciprocal(rstd[:, 1:2], rstd[:, 0:1]))
                me.wait()
                me.do(TS(x, x, mv[:, 0:1], rstd[:, 1:2], ALU.subtract, ALU.mult))
                me.wait()
                me.do(TT(x, x, gb[0], ALU.mult))
                me.wait()
                me.do(TT(x, x, gb[1], ALU.add))
                me.wait()

            dve.wait_ge(in_ln1, 32)
            dve.wait_ge(mod_ok, 3)
            for T in range(NT):
                layer_norm(x1[T], ln1, T)
                me.do(TT(h2[T], x1[T], mods[2], ALU.mult))
                me.wait()
                me.do(TT(h2[T], h2[T], mods[1], ALU.add))
                me.wait()
                dve.sem_inc(h2_ok, 1)

            def top16(vals, vo, io):
                me.do(V.max(vo[:, 0:8], vals))
                me.wait()
                me.do(V.max_index(io[:, 0:8], vo[:, 0:8], vals))
                me.wait()
                me.do(V.match_replace(vals, vo[:, 0:8], vals, -3.0e38))
                me.wait()
                me.do(V.max(vo[:, 8:16], vals))
                me.wait()
                me.do(V.max_index(io[:, 8:16], vo[:, 8:16], vals))

            for T in range(NT):
                dve.wait_ge(sc_out, T + 1)
                me.wait()
                for q in range(HP):
                    top16(score[T][:, q, :], tops[:, q, :], topi[:, q, :])
                me.wait()
                me.do(V.tensor_copy(topf, topi))
                tp4 = tops.rearrange("p (h a) k -> p h a k", a=2)
                me.do(TT(cand, tp4[:, :, 0, :].unsqueeze(3).to_broadcast([P, PH, TOPK, TOPK]),
                         tp4[:, :, 1, :].unsqueeze(2).to_broadcast([P, PH, TOPK, TOPK]), ALU.add))
                me.wait()
                for h in range(PH):
                    top16(cand[:, h, :, :].rearrange("p a b -> p (a b)"), best[:, h, :], bestj[:, h, :])
                me.wait()
                me.do(TS(topi[:, 0:8, :], bestj, 4, None, ALU.logical_shift_right))
                me.do(TS(topi[:, 8:16, :], bestj, 15, None, ALU.bitwise_and))
                me.wait()
                me.do(V.tensor_copy(ja, topi[:, 0:8, :]))
                me.do(V.tensor_copy(jb, topi[:, 8:16, :]))
                tf4 = topf.rearrange("p (h a) k -> p h a k", a=2)
                iota = cst[:, K_IOTA:K_IOTA + TOPK].unsqueeze(1).to_broadcast([P, EXPERTS, TOPK])
                oh3 = at3(R_HG + D, EXPERTS, TOPK)
                for a, (j, o) in enumerate(((ja, i1), (jb, i2))):
                    me.wait()
                    jf = j.rearrange("p h k -> p (h k)").unsqueeze(2).to_broadcast([P, EXPERTS, TOPK])
                    me.do(TT(oh3, jf, iota, ALU.is_equal))
                    me.wait()
                    me.do(TT(onehot, onehot, tf4[:, :, a, :].unsqueeze(2).to_broadcast([P, PH, TOPK, TOPK]), ALU.mult))
                    me.wait()
                    me.do(V.tensor_reduce(o, oh3, AX_X, ALU.add))
                me.wait()
                me.do(STT(idx[T], i1, float(NK), i2, ALU.mult, ALU.add))
                gw = gate_w[T].rearrange("p (h k) -> p h k", h=PH)
                me.do(TT(gw, best, best[:, :, 0:1].to_broadcast([P, PH, TOPK]), ALU.subtract))
                me.wait()
                dve.sem_inc(best_ok, 1)
                dve.wait_ge(gexp_ok, T + 1)
                me.do(V.tensor_reduce(gexp[:, 0:PH], gw, AX_X, ALU.add))
                me.wait()
                me.do(V.reciprocal(gexp[:, PH:2 * PH], gexp[:, 0:PH]))
                me.wait()
                me.do(TT(gw, gw, gexp[:, PH:2 * PH].unsqueeze(2).to_broadcast([P, PH, TOPK]), ALU.mult))
                me.wait()
                dve.sem_inc(topk_ok, 1)

            def dots(T, i, first):
                for b in range(2):
                    c0, c1 = b * GROUP, (b + 1) * GROUP
                    if not first:
                        dve.wait_ge(a_ok, i * 2 + (T * NGROUP + b - 1))
                    for s in range(c0, c1):
                        dve.wait_ge(in_u[s], i * 16 + 16 * (T * NGROUP // 2 + 1))
                        V.tensor_tensor_reduce(uslot[s], uslot[s], h2[T], 1.0, 0.0, ALU.mult, ALU.add, zraw[:, s:s + 1]).then_inc(dots_done, 1)
                    dve.wait_ge(dots_done, i * 2 * GROUP + (T * EXPERTS + c1))
                    z, u = zraw[:, c0:c1], zu[:, c0:c1]
                    me.do(TT(u, z, z, ALU.mult))
                    me.do(TT(zg[:, c0:c1], z, gate_w[T][:, bass.ds(i * 2 * GROUP + c0, GROUP)], ALU.mult))
                    me.wait()
                    me.do(TS(u, u, GELU_C, 1.0, ALU.mult, ALU.add))
                    me.wait()
                    TT(u, u, z, ALU.mult).then_inc(z_ok, 1)

            def finish(T):
                dve.wait_ge(pv_done, (T + 1) * EXPERTS)
                me.do(TT(h2[T], ps[:, 4 * T:4 * T + 4, :].rearrange("p b c -> p (b c)"), mods[3], ALU.mult))
                me.wait()
                me.do(STT(x1[T], x1[T], ALPHA, h2[T], ALU.mult, ALU.add))
                layer_norm(x1[T], ln2, NT + T)
                dve.sem_inc(ln2_ok, 1)

            dve.wait_ge(mod_ok, 4)
            for T in range(NT):
                dots(T, 0, T == 0)
                if T:
                    dve.wait_ge(in_ln2, 32)
                    finish(0)
                with dve.Fori(1, NGROUP // 2) as i:
                    me.enter(i, 1, 6)
                    dots(T, i, False)
                me.leave(NGROUP // 2 - 1)
            finish(1)


INPUTS = ("x", "c", "positions", "w_ada", "b_ada", "w_in", "conv_w", "conv_b", "w_rg_a", "b_rg_a", "w_rg_x", "b_rg_x",
          "rg_lambda", "w_rnn_out", "q_norm_g", "w_uq", "kv_norm_g", "w_ukv", "w_mla_out", "w_o", "ln1_g", "ln1_b",
          "peer_wq", "peer_keys", "peer_u", "peer_v", "ln2_g", "ln2_b")


def kernel(**inputs):
    import concourse.bacc as bacc
    from concourse.bass_utils import run_bass_kernel_spmd as run

    nc = bacc.Bacc("TRN2", target_bir_lowering=False, num_devices=1)
    arrays = {n: np.ascontiguousarray(inputs[n]) for n in INPUTS}
    arrays["cst"] = constants()
    t = {n: nc.dram_tensor(f"in_{n}", a.shape, mybir.dt.from_np(a.dtype), kind="ExternalInput").ap() for n, a in arrays.items()}
    out = nc.dram_tensor("out_y", (1, S, D), F32, kind="ExternalOutput").ap()
    build(nc, t, out)
    r = run(nc, [{f"in_{n}": a for n, a in arrays.items()}], core_ids=[0])
    return r.results[0]["out_y"]
```

```python
import math
from contextlib import ExitStack

import numpy as np

import concourse.bass as bass
from concourse import mybir

F32 = mybir.dt.float32
F32R = mybir.dt.float32r
U32 = mybir.dt.uint32
I32 = mybir.dt.int32
ALU = mybir.AluOpType
ACT = mybir.ActivationFunctionType
AX_X = mybir.AxisListType.X

P = 128
D = 2048
S = 256
NT = S // P
KT = D // P
HEADS = 16
RANK = 512
LT = RANK // P
NOPE, ROPE, VH = 128, 64, 128
CONV = 4
PH, NK, TOPK = 8, 128, 16
HP = 2 * PH
EXPERTS = PH * TOPK
ALPHA = 2.0 ** 0.25
LN_EPS, RMS_EPS = 1e-5, 1e-6
SM_SCALE = (NOPE + ROPE) ** -0.5
GELU_C, GELU_S = 0.044715, 2.0 * math.sqrt(2.0 / math.pi)

C_XR, C_GR, C_QC, C_KVC = 0, D, 2 * D, 2 * D + RANK
C_KR = C_KVC + RANK
C_GRNN = C_KR + ROPE
C_GMLA = C_GRNN + D

UNIT = 2048
RING = 4
B_QC, B_KVC, B_XR, B_G, B_G2, B_RNN, B_MLA, B_O, B_WQ, B_END = 0, 1, 2, 10, 14, 18, 22, 26, 30, 34
ADA_UNITS = 2 * KT
GROUP = 4
FRONT, ARENA = 20480, 32520

K_ID, K_MASK, K_ROT, K_IOTA, K_INVF, K_ONES, K_END = 0, 128, 512, 640, 656, 657, 785


def constants():
    c = np.zeros((P, K_END), np.float32)
    c[:, K_ID:K_ID + P] = np.eye(P)
    tri = np.where(np.arange(P)[None, :] <= np.arange(P)[:, None], 0.0, -1e30)
    c[:, K_MASK:K_MASK + P] = tri
    c[:, K_MASK + 2 * P:K_MASK + 3 * P] = tri
    half = ROPE // 2
    for m in range(half):
        c[m + half, K_ROT + m] = -1.0
        c[m, K_ROT + half + m] = 1.0
    c[:, K_IOTA:K_IOTA + TOPK] = np.arange(TOPK)
    freq = np.float32(10000.0) ** (-np.arange(0, ROPE, 2, dtype=np.float32) / np.float32(ROPE))
    c[:ROPE, K_INVF] = np.concatenate([freq, freq])
    c[:, K_ONES:K_ONES + P] = 1.0
    return c


DOTS_STEPS, TOPK_STEPS = 12, 25


class Chain:

    def __init__(self, eng, sem):
        self.eng, self.sem, self.base, self.n = eng, sem, 0, 0

    def do(self, ins):
        ins.then_inc(self.sem, 1)
        self.n += 1
        return ins

    def wait(self):
        self.eng.wait_ge(self.sem, self.base + self.n)

    def enter(self, i, first, per):
        self.kept, self.per = self.base + self.n, per
        self.base, self.n = i * per + (self.kept - first * per), 0

    def leave(self, rounds):
        assert self.n == self.per, (self.n, self.per)
        self.base, self.n = self.kept + rounds * self.per, 0


def build(nc, t, out):
    with ExitStack() as ctx:
        def sem(name):
            return ctx.enter_context(nc.semaphore(name))

        with nc.sbuf_tensor("front", [P, FRONT], F32) as front, nc.sbuf_tensor("arena", [P, ARENA], F32) as arena:
            pass
        split = {n: ctx.enter_context(nc.sbuf_tensor(f"split_{n}", [P, words], F32R)) for n, words in (
            ("ring", RING * UNIT), ("between0", 4 * D), ("pada", 2 * D), ("ht", KT * S), ("w0", 4096), ("w1", 4096), ("between1", 2048),
            ("hg", KT * S), ("g0", KT * S), ("between2", KT * S), ("ot", KT * S))}
        ps = ctx.enter_context(nc.psum_tensor("ps", [P, 8, 512], F32))

        R_RING, R_MODS, R_PADA = 0, 8192, 16384
        R_HT, R_WORK, R_HG, R_G, R_OT, R_SM = 0, 4096, 14336, 18432, 26624, 30720

        def at(off, n):
            return arena[:, off:off + n]

        def infront(off, n):
            return front[:, off:off + n]

        def at3(off, a, b):
            return at(off, a * b).rearrange("p (a b) -> p a b", a=a)

        sm = [R_SM]

        def small(n):
            sm[0] += n
            assert sm[0] <= ARENA
            return sm[0] - n

        ring = [infront(R_RING + UNIT * s, UNIT) for s in range(RING)]
        ring3 = [r.rearrange("p (t c) -> p t c", t=4) for r in ring]
        mods = [infront(R_MODS + D * i, D) for i in range(4)]
        pada = [infront(R_PADA + D * i, D) for i in range(2)]
        hT = at3(R_HT, KT, S)
        hgT = at3(R_HG, KT, S)
        gT = [at3(R_G, KT, S), at3(R_G + KT * S, KT, S)]
        oT = at3(R_OT, KT, S)
        xin = at3(R_G, NT, D)
        acc = [at(R_G + KT * S + D * i, D) for i in range(2)]

        eps_rms, eps_ln = at(small(1), 1), at(small(1), 1)
        cst = at(small(K_END), K_END)
        ident = cst[:, K_ID:K_ID + P]
        ones = cst[:, K_ONES:K_ONES + P]
        colA = at(small(P), P)
        colB = at(small(24), 24)
        conv_c, convb_c, ba_c, bx_c, lam_c = (colA[:, a:b] for a, b in ((0, 64), (64, 80), (80, 96), (96, 112), (112, 128)))
        sigc = at(small(16), 16)
        cact = at(small(16), 16)
        sh1 = at(small(16), 16)
        sc1 = at(small(16), 16)
        sp4 = at(small(16), 16)
        lt = [at(small(16), 16) for _ in range(5)]
        smx = at(small(2), 2)
        snm = at(small(2), 2)
        ssum = at(small(2), 2)
        srec = at(small(2), 2)
        o_bn = [small(24) for _ in range(NT)]
        bn6 = [at3(o, 4, 6) for o in o_bn]
        mv = [at(small(2), 2) for _ in range(NT)]
        rstd = [at(small(2), 2) for _ in range(NT)]
        zraw = at(small(8), 8)
        zu = at(small(8), 8)
        zg = at(small(8), 8)
        zs = at(small(8), 8)
        za = at(small(8), 8)
        idxu, idxv = (at(small(8), 8).bitcast(U32) for _ in range(2))
        o_gate = small(NT * EXPERTS)
        o_idx = small(NT * EXPERTS)

        W = R_WORK
        qcT, kvT = at3(W, LT, S), at3(W + 1024, LT, S)
        cosT, sinT, krT = (arena[0:ROPE, W + o:W + o + S] for o in (2048, 2304, 2560))
        qkn = at(W + 2816, 2 * S)
        qn, kn = qkn[:, 0:S], qkn[:, S:2 * S]
        qr, qro = (arena[0:ROPE, W + o:W + o + S] for o in (3328, 3584))
        vv = at3(W + 3840, NT, VH)
        rt = arena[0:ROPE, W + 4096:W + 4352]
        sc = at(W + 4352, 384)
        pT = at3(W + 4736, 3, P)
        sq2 = [at3(W + 5120, LT, S), at3(W + 6144, LT, S)]
        rs2 = [at(W + 7168, S), at(W + 7424, S)]
        pt = [arena[0:ROPE, W + 7680 + S * i:W + 7680 + S * (i + 1)] for i in range(5)]
        krraw = arena[0:ROPE, W + 8960:W + 9216]
        stA, stB = at(W + 9216, P), arena[0:24, W + 9344:W + 9472]
        uq = [at3(R_HG + 768 * b, LT, 192) for b in range(2)]
        ukv = [at3(R_HG + 1536 + 1024 * b, LT, 256) for b in range(2)]
        krw = at3(R_OT, KT, ROPE)

        XR, GR, XC, RR, II, TP, QQ, GT = (W + 1024 * i for i in range(8))
        wg = at(W + 8192, 1024).rearrange("p (g h c) -> p g h c", g=2, h=4)

        def quad(off, j):
            return at(off + S * j, S)

        x1 = [at(W + D * i, D) for i in range(NT)]
        h2 = [at(W + 2 * D + D * i, D) for i in range(NT)]
        keys = at3(W + 8192, 2, P)
        keysT = at3(W + 8448, 2, P)
        stage, cand, onehot = at(W + 9216, 2 * NK), at3(W + 9472, TOPK, TOPK), at3(W + 9728, 2 * TOPK, TOPK)
        tk = [R_SM + 2 + K_MASK]

        def tk_at(n):
            tk[0] += n
            assert tk[0] <= R_SM + 2 + K_ROT
            return at(tk[0] - n, n)

        tops, topi, topf = tk_at(2 * TOPK), tk_at(2 * TOPK).bitcast(U32), tk_at(2 * TOPK)
        best, bestj, ranki, rankf, keyf = tk_at(TOPK), tk_at(TOPK).bitcast(U32), tk_at(2 * TOPK).bitcast(U32), tk_at(2 * TOPK), tk_at(2 * TOPK)
        negbest, gexp, gsum, ginv = tk_at(1), tk_at(TOPK), tk_at(1), tk_at(1)
        wo_t = [at(R_OT + 1024 * b, 1024) for b in range(2)]

        S_HT, S_HG, S_OT, S_MIX, S_H2 = (
            (split[h][:, :], split[l][:, :], off) for h, l, off in (
                ("w0", "ht", R_HT), ("w1", "hg", R_HG), ("ht", "ot", R_OT), ("w1", "g0", R_G), ("ht", "g0", R_G)))

        def by_tile(part):
            return part.rearrange("p (k s) -> p k s", k=KT)

        whi = [split["pada"][:, UNIT * i:UNIT * (i + 1)] for i in range(2)]
        wlo = [split["ring"][:, UNIT * i:UNIT * (i + 1)] for i in range(RING)]
        ln1 = [at(R_HG, D), at(R_HG + D, D)]
        ln2 = [mods[2], at(R_OT, D)]
        ln_t = at(R_OT + D, D)
        zeros = colA
        zeros4 = zeros.unsqueeze(1).to_broadcast([P, 4, P])
        qT = gT[1]
        uslot = ring + pada + [at(R_HT, D), at(R_HT + D, D)]
        vslot = [at(o, D) for o in [R_G + D * i for i in range(4)] + [R_HG, R_HG + D]] + mods[:2]
        diag = [at(W + 8192 + P * i, P) for i in range(8)]

        in_cst, in_par, in_pos, in_x, in_kr, in_bada = (sem(n) for n in ("in_cst", "in_par", "in_pos", "in_x", "in_kr", "in_bada"))
        in_ring = [sem(f"in_ring{i}") for i in range(RING)]
        in_head = [sem(f"in_head{i}") for i in range(2)]
        in_wg, in_x2, in_ln1, in_ln2, in_keys, in_pb = (sem(n) for n in ("in_wg", "in_x2", "in_ln1", "in_ln2", "in_keys", "in_pb"))
        in_pada = [sem(f"in_pada{i}") for i in range(2)]
        in_u = [sem(f"in_u{i}") for i in range(8)]
        in_v = [sem(f"in_v{i}") for i in range(8)]
        dve_s, act_s, pool_s = sem("dve_self"), sem("act_self"), sem("pool_self")
        pool_gate, dve_gate = sem("pool_gate"), sem("dve_gate")
        acc_zero, ada_used, cact_ok = sem("acc_zero"), sem("ada_used"), sem("cact_ok")
        cols_t, cols_ok, sigc_ok, y_need, y_ok = (sem(n) for n in ("cols_t", "cols_ok", "sigc_ok", "y_need", "y_ok"))
        r_ok, sin_ok = sem("angles_ok"), sem("sin_ok")
        xT_done, xT_out, acc_ok, modc_done, hT_ok = (sem(n) for n in ("xT_done", "xT_out", "acc_ok", "modc_done", "hT_ok"))
        unit_used, out_act, out_dve = (sem(n) for n in ("unit_used", "out_act", "out_dve"))
        kr_done, kr_out, krot_done, kr_ok = (sem(n) for n in ("kr_done", "kr_out", "krot_done", "kr_ok"))
        sq_ok, ssq_done, std_ok, lat_ok = (sem(n) for n in ("sq_ok", "ssq_done", "std_ok", "lat_ok"))
        h_qr, h_qrout, h_qk, h_qkout, h_rot, h_rope, h_v, h_vout = (sem(f"h_{n}") for n in ("qr", "qrout", "qk", "qkout", "rot", "rope", "v", "vout"))
        h_s, h_neg, h_exp, h_p, h_t, h_tout, h_o, h_oout = (sem(f"h_{n}") for n in ("s", "neg", "exp", "p", "t", "tout", "o", "oout"))
        xc_ok, gates_done, gates_out, tanh_ok, sqrt_ok, gelu_in, gelu_ok, hg_ok = (sem(n) for n in (
            "xc_ok", "gates_done", "gates_out", "tanh_ok", "sqrt_ok", "gelu_in", "gelu_ok", "hg_ok"))
        mod_part, mod_done, mod_ok, mix_ok = (sem(n) for n in ("mod_part", "mod_done", "mod_ok", "mix_ok"))
        keys_t, keys_ok = sem("keys_t"), sem("keys_ok")
        var_ok, std1_ok, h2_ok, h2T_done, h2T_out = (sem(n) for n in ("var_ok", "std1_ok", "h2_ok", "h2T_done", "h2T_out"))
        sc_done, sc_out, stage_ok, best_ok, gexp_ok, topk_ok, zero_ok = (sem(n) for n in (
            "sc_done", "sc_out", "stage_ok", "best_ok", "gexp_ok", "topk_ok", "zero_ok"))
        whi_ok, wlo_ok, shi_ok, slo_ok = (sem(n) for n in ("whi_ok", "wlo_ok", "shi_ok", "slo_ok"))
        dots_done, z_ok, a_ok, diag_ok, pv_done, y_done = (sem(n) for n in ("dots_done", "z_ok", "a_ok", "diag_ok", "pv_done", "y_done"))
        ln2_ok, in_out = sem("ln2_ok"), sem("in_out")

        wv = {n: t[n][0].rearrange("(t p) c -> p t c", p=P) for n in ("w_in", "w_rnn_out", "w_mla_out", "w_o", "peer_wq")}
        ada_v = t["w_ada"][0].rearrange("(t p) c -> p t c", p=P)
        uq_v = t["w_uq"][0].rearrange("(t p) c -> p t c", p=P)
        ukv_v = t["w_ukv"][0].rearrange("(t p) c -> p t c", p=P)
        rows = {n: t[n].rearrange("a (r c) -> (a r) c", c=P) for n in ("conv_b", "b_rg_a", "b_rg_x", "rg_lambda", "c", "q_norm_g", "kv_norm_g")}
        conv_rows = t["conv_w"][0].rearrange("w (r c) -> (w r) c", c=P)

        block = ctx.enter_context(nc.Block())

        def psblock(b):
            return ps[:, 2 * (b % 2):2 * (b % 2) + 2, :]

        @block.sync
        def _(sp):
            sp.dma_start(cst, t["cst"]).then_inc(in_cst, 16)
            for o, n in ((0, "c"), (16, "q_norm_g"), (20, "kv_norm_g")):
                r = rows[n]
                sp.dma_start(arena[o:o + r.shape[0], W + 9344:W + 9472], r).then_inc(in_par, 16)
            sp.dma_start(arena[0:64, W + 9216:W + 9344], conv_rows).then_inc(in_par, 16)
            for i, n in enumerate(("conv_b", "b_rg_a", "b_rg_x", "rg_lambda")):
                sp.dma_start(arena[64 + 16 * i:80 + 16 * i, W + 9216:W + 9344], rows[n]).then_inc(in_par, 16)
            sp.wait_ge(acc_zero, 2)
            for i in range(2):
                sp.dma_start(acc[i][0:1, :], t["b_ada"][:, i * D:(i + 1) * D]).then_inc(in_bada, 16)
            pos = t["positions"]
            sp.dma_start(pt[0].bitcast(I32), bass.AP(pos.tensor, pos.offset, [[0, ROPE], [1, S]])).then_inc(in_pos, 16)
            for ch in range(2):
                def ada(i, first):
                    for s in range(RING):
                        if not first:
                            sp.wait_ge(ada_used, i * RING + (s - 3 + ch * KT))
                        sp.dma_start(ring[s], ada_v[:, bass.ds(i * RING + s, 1), ch * D:(ch + 1) * D].rearrange("p t c -> p (t c)")
                                     ).then_inc(in_ring[s], 16)
                if ch == 0:
                    ada(0, True)
                    sp.dma_start(xin[:, :, :], t["x"][0].rearrange("(t p) c -> p t c", p=P)).then_inc(in_x, 16)
                with sp.Fori(1 - ch, KT // RING) as i:
                    ada(i, False)

            def units(w, col, b, wait_dve=False):
                for s in range(RING):
                    if wait_dve:
                        sp.wait_ge(ada_used, ADA_UNITS - 3 + s)
                    else:
                        sp.wait_ge(unit_used, b * RING + (s - 3))
                    sp.dma_start(ring3[s], wv[w][:, 4 * s:4 * s + 4, bass.ds(col, 512)]).then_inc(in_ring[s], 16)

            units("w_in", C_QC, B_QC, wait_dve=True)
            sp.dma_start(krw, wv["w_in"][:, :, C_KR:C_KR + ROPE]).then_inc(in_kr, 16)
            units("w_in", C_KVC, B_KVC)
            for b in range(2):
                sp.dma_start(uq[b], uq_v[:, :, b * 192:b * 192 + 192]).then_inc(in_head[b], 16)
                sp.dma_start(ukv[b], ukv_v[:, :, b * 256:b * 256 + 256]).then_inc(in_head[b], 16)
            with sp.Fori(1, HEADS // 2) as i:
                for b in range(2):
                    sp.wait_ge(h_v, i * 2 + (b - 1))
                    sp.dma_start(uq[b], uq_v[:, :, bass.ds(i * 384 + b * 192, 192)]).then_inc(in_head[b], 16)
                    sp.dma_start(ukv[b], ukv_v[:, :, bass.ds(i * 512 + b * 256, 256)]).then_inc(in_head[b], 16)
            with sp.Fori(0, 4) as g:
                units("w_in", g * 512 + C_XR, g * 2 + B_XR)
                sp.wait_ge(gates_done, g + 1)
                sp.wait_ge(h_oout, HEADS)
                for k, n in enumerate(("w_rg_a", "w_rg_x")):
                    sp.dma_start(wg[:, k, :, :], t[n][0].rearrange("h i j -> i h j")[:, bass.ds(g * 4, 4), :]).then_inc(in_wg, 16)
                units("w_in", g * 512 + C_GR, g * 2 + B_XR + 1)
            with sp.Fori(0, 4) as g:
                units("w_in", g * 512 + C_GRNN, g * 2 + B_G)
                units("w_in", g * 512 + C_GMLA, g * 2 + B_G + 1)
            with sp.Fori(0, 4) as g:
                units("w_rnn_out", g * 512, g + B_RNN)
            sp.wait_ge(unit_used, 4 * B_RNN)
            sp.dma_start(at3(W, NT, D), t["x"][0].rearrange("(t p) c -> p t c", p=P)).then_inc(in_x2, 16)
            sp.dma_start(keys, t["peer_keys"][0].rearrange("a n d -> n a d")).then_inc(in_keys, 16)
            with sp.Fori(0, 4) as g:
                units("w_mla_out", g * 512, g + B_MLA)
            sp.wait_ge(unit_used, 4 * (B_RNN + 4))
            for i, n in enumerate(("ln1_g", "ln1_b")):
                sp.dma_start(ln1[i], bass.AP(t[n].tensor, t[n].offset, [[0, P], [1, D]])).then_inc(in_ln1, 16)
            with sp.Fori(0, 4) as g:
                units("w_o", g * 512, g + B_O)
            with sp.Fori(0, 4) as g:
                units("peer_wq", g * 512, g + B_WQ)
            sp.wait_ge(h2_ok, 2 * NT * 2)
            for i, n in enumerate(("ln2_g", "ln2_b")):
                if i == 1:
                    sp.wait_ge(stage_ok, PH + 1)
                sp.dma_start(ln2[i], bass.AP(t[n].tensor, t[n].offset, [[0, P], [1, D]])).then_inc(in_ln2, 16)
            for T in range(NT):
                for c in range(4):
                    sp.wait_ge(ln2_ok, 4 * T + c + 1)
                    sp.dma_start(out[0, T * P:(T + 1) * P, c * 512:(c + 1) * 512], x1[T][:, c * 512:(c + 1) * 512]).then_inc(in_out, 16)
            sp.wait_ge(in_out, 64 * NT)

        @block.gpsimd
        def _(pool):
            me = Chain(pool, pool_s)
            for ch in range(4):
                me.do(pool.memset(mods[ch], 0.0))
                me.wait()
                pool.dma_start(mods[ch][0:1, :], t["b_ada"][:, (2 + ch) * D:(3 + ch) * D]).then_inc(in_pb, 16)

            def ada_load(kt, ch):
                pool.dma_start(pada[ch % 2], ada_v[:, bass.ds(kt, 1), (2 + ch) * D:(3 + ch) * D].rearrange("p t c -> p (t c)")
                               ).then_inc(in_pada[ch % 2], 16)

            def ada_tile(kt, last):
                for ch in range(4):
                    b = ch % 2
                    pool.wait_ge(in_pada[b], kt * 32 + 16 * (ch // 2 + 1))
                    pool.sem_inc(pool_gate, 1)
                    me.do(pool.tensor_tensor(pada[b], pada[b], cact[:, bass.ds(kt, 1)].to_broadcast([P, D]), ALU.mult))
                    me.wait()
                    me.do(pool.tensor_tensor(mods[ch], mods[ch], pada[b], ALU.add))
                    me.wait()
                    pool.sem_inc(pool_gate, 1)
                    if ch < 2:
                        ada_load(kt, ch + 2)
                    elif not last:
                        ada_load(kt + 1, ch - 2)

            pool.wait_ge(ada_used, ADA_UNITS - RING)
            for ch in range(2):
                ada_load(0, ch)
            pool.wait_ge(cact_ok, 1)
            pool.wait_ge(in_pb, 64)
            with pool.Fori(0, KT - 1) as kt:
                me.enter(kt, 0, 8)
                ada_tile(kt, False)
            me.leave(KT - 1)
            ada_tile(KT - 1, True)
            pool.sem_inc(mod_part, 1)

            def gathers(H):
                pool.wait_ge(topk_ok, H + 1)
                for q in range(TOPK // GROUP):
                    b = q % 2
                    for slots, table, ix, used, landed in ((uslot, "peer_u", idxu, dots_done, in_u), (vslot, "peer_v", idxv, pv_done, in_v)):
                        pool.wait_ge(used, H * TOPK + (q * GROUP + GROUP))
                        pool.sem_inc(pool_gate, 1)
                        me.do(pool.tensor_copy(ix[:, b * GROUP:(b + 1) * GROUP],
                                               arena[:, bass.ds(H * TOPK + (o_idx + q * GROUP), GROUP)].bitcast(U32)))
                        me.wait()
                        pool.sem_inc(pool_gate, 1)
                        for s in range(GROUP * b, GROUP * (b + 1)):
                            pool.indirect_dma_start(slots[s], None, t[table][0], bass.IndirectOffsetOnAxis(ix[:, s:s + 1], 0)
                                                    ).then_inc(landed[s], 16)

            with pool.Fori(0, NT * PH) as H:
                me.enter(H, 0, 2 * TOPK // GROUP)
                gathers(H)
            me.leave(NT * PH)

        @block.tensor
        def _(pe):
            def mm(o, l, r, start, stop, **k):
                return pe.matmul(o, l, r, start=start, stop=stop, skip_group_check=True, **k)

            pe.wait_ge(in_cst, 16)
            pe.wait_ge(in_par, 128)
            pe.transpose(ps[:, 0, 0:24], stB, ident[0:24, 0:24]).then_inc(cols_t, 1)
            pe.transpose(ps[:, 1, 0:P], stA, ident).then_inc(cols_t, 1)
            pe.wait_ge(in_x, 16)
            for g in range(KT // 2):
                if g >= 4:
                    pe.wait_ge(xT_out, g - 3)
                for a in range(2):
                    for T in range(NT):
                        last = pe.transpose(ps[:, 4 + g % 4, a * S + T * P:a * S + (T + 1) * P],
                                            xin[:, T, (2 * g + a) * P:(2 * g + a + 1) * P], ident)
                last.then_inc(xT_done, 1)
            for i in range(2):
                pe.wait_ge(acc_ok, i + 1)
                for k in range(KT):
                    last = mm(ps[:, 2, i * KT + k:i * KT + k + 1], acc[i][:, k * P:(k + 1) * P], ones[:, 0:1], True, True)
                last.then_inc(modc_done, 1)

            def channel_block(b, src, wait=None):
                o = psblock(b).rearrange("p b (h c) -> p (b h) c", h=2)
                for s in range(RING):
                    pe.wait_ge(in_ring[s], b * 16 + 16 * (ADA_UNITS // RING + 1))
                    for k in range(4):
                        kt = 4 * s + k
                        if wait is not None:
                            wait(kt)
                        for m in range(4):
                            last = mm(o[:, m, :], ring3[s][:, k, m * P:(m + 1) * P], src[:, kt, :],
                                      kt == 0 and m % 2 == 0, kt == KT - 1)
                    last.then_inc(unit_used, 1)

            channel_block(B_QC, hT, wait=lambda kt: pe.wait_ge(hT_ok, kt + 1))
            pe.wait_ge(in_kr, 16)
            pe.wait_ge(xT_out, KT // 2)
            for kt in range(KT):
                last = mm(ps[0:ROPE, 4, 0:S], krw[:, kt, :], hT[:, kt, :], kt == 0, kt == KT - 1)
            last.then_inc(kr_done, 1)
            channel_block(B_KVC, hT)
            pe.wait_ge(kr_out, 1)
            mm(ps[0:ROPE, 5, 0:S], cst[0:ROPE, K_ROT:K_ROT + ROPE], krraw, True, True).then_inc(krot_done, 1)
            for i in range(2):
                pe.wait_ge(sq_ok, i + 1)
                for k in range(LT):
                    last = mm(ps[:, 6 + i, 0:S], ones, sq2[i][:, k, :], k == 0, k == LT - 1)
                last.then_inc(ssq_done, 1)
            pe.wait_ge(lat_ok, 2)
            pe.wait_ge(kr_ok, 1)

            def transposes(h):
                pe.wait_ge(h_p, h + 1)
                for j in range(3):
                    last = pe.transpose(ps[:, 4, j * P:(j + 1) * P], sc[:, j * P:(j + 1) * P], ident)
                last.then_inc(h_t, 1)

            def values(h, n):
                pe.wait_ge(h_tout, h + 1)
                pe.wait_ge(h_vout, h + 1)
                if n:
                    pe.wait_ge(h_oout, h)
                mm(ps[:, 5, 0:P], vv[:, 0, :], pT[:, 0, :], True, True)
                mm(ps[:, 5, P:2 * P], vv[:, 0, :], pT[:, 1, :], True, False)
                mm(ps[:, 5, P:2 * P], vv[:, 1, :], pT[:, 2, :], False, True).then_inc(h_o, 1)

            def head(i, b, first):
                h = i * 2 + b
                pe.wait_ge(in_head[b], i * 32 + 32)
                if not first:
                    pe.wait_ge(h_rope, h)
                for k in range(LT):
                    last = mm(ps[0:ROPE, 0, 0:S], uq[b][:, k, NOPE:NOPE + ROPE], qcT[:, k, :], k == 0, k == LT - 1)
                last.then_inc(h_qr, 1)
                if not first:
                    pe.wait_ge(h_qkout, h)
                for k in range(LT):
                    mm(ps[:, 1, 0:S], uq[b][:, k, 0:NOPE], qcT[:, k, :], k == 0, k == LT - 1)
                for k in range(LT):
                    last = mm(ps[:, 1, S:2 * S], ukv[b][:, k, 0:NOPE], kvT[:, k, :], k == 0, k == LT - 1)
                last.then_inc(h_qk, 1)
                pe.wait_ge(h_qrout, h + 1)
                mm(ps[:, 0, S:2 * S], cst[0:ROPE, K_ROT:K_ROT + P], qr, True, True).then_inc(h_rot, 1)
                if not first:
                    pe.wait_ge(h_vout, h)
                for T in range(NT):
                    for k in range(LT):
                        last = mm(ps[:, 2, T * P:(T + 1) * P], kvT[:, k, T * P:(T + 1) * P], ukv[b][:, k, NOPE:], k == 0, k == LT - 1)
                last.then_inc(h_v, 1)
                if not first:
                    transposes(h - 1)
                pe.wait_ge(h_qkout, h + 1)
                pe.wait_ge(h_rope, h + 1)
                for T in range(NT):
                    o = ps[:, 3, T * P:(2 * T + 1) * P]
                    n = (T + 1) * P
                    mm(o, qn[:, T * P:(T + 1) * P], kn[:, 0:n], True, False)
                    last = mm(o, qro[:, T * P:(T + 1) * P], krT[:, 0:n], False, True)
                last.then_inc(h_s, 1)

            head(0, 0, True)
            head(0, 1, False)
            values(0, False)
            with pe.Fori(1, HEADS // 2) as i:
                for b in range(2):
                    head(i, b, False)
                    values(i * 2 + (b - 1), True)
            transposes(HEADS - 1)
            values(HEADS - 1, True)

            pe.wait_ge(h_oout, HEADS)
            pe.sem_inc(gates_done, 1)
            with pe.Fori(0, 4) as g:
                for k2 in range(2):
                    pe.wait_ge(out_act, g * 2 + (k2 + 1))
                    o = ps[:, 2 * k2:2 * k2 + 2, :].rearrange("p b (h c) -> p (b h) c", h=2)
                    for s in range(RING):
                        pe.wait_ge(in_ring[s], g * 32 + 16 * (B_XR + k2 + ADA_UNITS // RING + 1))
                        for k in range(4):
                            kt = 4 * s + k
                            for m in range(4):
                                last = mm(o[:, m, :], ring3[s][:, k, m * P:(m + 1) * P], hT[:, kt, :],
                                          kt == 0 and m % 2 == 0, kt == KT - 1)
                        last.then_inc(unit_used, 1)
                pe.wait_ge(in_wg, g * 32 + 32)
                pe.wait_ge(xc_ok, g + 1)
                pe.wait_ge(gates_out, g * 2 + 1)
                for k in range(2):
                    for m in range(4):
                        last = mm(ps[:, 4 + 2 * k + m // 2, (m % 2) * S:(m % 2 + 1) * S], wg[:, k, m, :], quad(XC, m), True, True)
                last.then_inc(gates_done, 1)

            def loop_blocks(b0, n, src, evac):
                with pe.Fori(0, n // 2) as g:
                    for k2 in range(2):
                        evac(g, k2)
                        o = ps[:, 2 * k2:2 * k2 + 2, :]
                        oc = o.rearrange("p b (h c) -> p (b h) c", h=2)
                        for s in range(RING):
                            pe.wait_ge(in_ring[s], g * 32 + 16 * (b0 + k2 + ADA_UNITS // RING + 1))
                            for k in range(4):
                                kt = 4 * s + k
                                for m in range(4):
                                    last = mm(oc[:, m, :], ring3[s][:, k, m * P:(m + 1) * P], src[:, kt, :],
                                              kt == 0 and m % 2 == 0, kt == KT - 1)
                            last.then_inc(unit_used, 1)

            def split_blocks(b0, src, evac, token=False, ready=None):
                hi, lo = by_tile(src[0]), by_tile(src[1])
                with pe.Fori(0, 2) as g:
                    for k2 in range(2):
                        evac(g, k2)
                        o = ps[:, 2 * k2:2 * k2 + 2, :]
                        oc = o.rearrange("p b (h c) -> p (b h) c", h=2)
                        for s in range(RING):
                            pe.wait_ge(wlo_ok, g * 8 + 4 * (b0 + k2 - B_G2) + s + 1)
                            ready(s)
                            wh = whi[s % 2].rearrange("p (t c) -> p t c", t=4)
                            wl = wlo[s].rearrange("p (t c) -> p t c", t=4)
                            for k in range(4):
                                kt = 4 * s + k
                                first, end = kt == 0, kt == KT - 1
                                if token:
                                    for T in range(NT):
                                        rows = slice(T * P, (T + 1) * P)
                                        mm(o[:, T, :], hi[:, kt, rows], wh[:, k, :], first, False)
                                        mm(o[:, T, :], hi[:, kt, rows], wl[:, k, :], False, False)
                                        last = mm(o[:, T, :], lo[:, kt, rows], wh[:, k, :], False, end)
                                else:
                                    for m in range(4):
                                        cols = slice(m * P, (m + 1) * P)
                                        mm(oc[:, m, :], wh[:, k, cols], hi[:, kt, :], first and m % 2 == 0, False)
                                        mm(oc[:, m, :], wh[:, k, cols], lo[:, kt, :], False, False)
                                        last = mm(oc[:, m, :], wl[:, k, cols], hi[:, kt, :], False, end)
                            last.then_inc(unit_used, 1)

            def modulation(ch):
                pe.wait_ge(mod_part, 1)
                if ch:
                    pe.wait_ge(mod_ok, ch)
                for j in range(4):
                    last = mm(ps[:, 4 + j, :], ones, mods[ch][:, j * 512:(j + 1) * 512], True, True)
                last.then_inc(mod_done, 1)

            loop_blocks(B_G, 4, hT, lambda g, k: pe.wait_ge(out_act, g * 2 + (B_G + k - 1)))
            split_blocks(B_G2, S_HT, lambda g, k: pe.wait_ge(out_act, g * 2 + (B_G2 + k - 1)),
                         ready=lambda s: pe.wait_ge(slo_ok, 4 + s + 1))
            pe.wait_ge(out_act, B_RNN)
            modulation(0)
            split_blocks(B_RNN, S_HG, lambda g, k: pe.wait_ge(out_dve, g * 2 + (1 if k == 0 else 1)), ready=lambda s: pe.wait_ge(slo_ok, 4))
            modulation(1)
            split_blocks(B_MLA, S_OT, lambda g, k: pe.wait_ge(out_dve, g * 2 + (4 + k)), ready=lambda s: pe.wait_ge(slo_ok, 12))
            pe.wait_ge(in_keys, 16)
            pe.wait_ge(mod_ok, 2)
            for a in range(2):
                last = pe.transpose(ps[:, 6, a * P:(a + 1) * P], keys[:, a, :], ident)
            last.then_inc(keys_t, 1)
            pe.wait_ge(keys_ok, 1)
            modulation(2)
            split_blocks(B_O, S_MIX, lambda g, k: pe.wait_ge(out_dve, g * 2 + (8 + k)), token=True,
                         ready=lambda s: pe.wait_ge(slo_ok, 12 + s + 1))
            pe.wait_ge(mod_ok, 3)
            for n in range(4 * NT):
                c, T = n // NT, n % NT
                pe.wait_ge(h2_ok, n + 1)
                if n >= 4:
                    pe.wait_ge(slo_ok, 16 + n - 3)
                for a in range(4):
                    last = pe.transpose(ps[:, 4 + n % 4, a * P:(a + 1) * P], h2[T][:, (4 * c + a) * P:(4 * c + a + 1) * P], ident)
                last.then_inc(h2T_done, 1)
            pe.wait_ge(out_dve, 13)
            split_blocks(B_WQ, S_H2, lambda g, k: pe.wait_ge(out_act, g * 2 + (B_RNN - 1 + k)),
                         ready=lambda s: pe.wait_ge(slo_ok, 16 + NT * (s + 1)))
            pe.wait_ge(out_act, B_RNN + 4)
            for T in range(NT):
                for q in range(HP):
                    last = mm(ps[:, 4 * (1 - T) + q // 4, (q % 4) * P:(q % 4 + 1) * P], qT[:, q, T * P:(T + 1) * P], keysT[:, q % 2, :], True, True)
                last.then_inc(sc_done, 1)
            pe.wait_ge(sc_out, 1)
            modulation(3)
            pe.sem_inc(pv_done, 2 * GROUP)

            def products(H, T):
                for e in range(TOPK):
                    q = e % (2 * GROUP)
                    pe.wait_ge(in_v[q], H * 32 + 16 * (e // (2 * GROUP) + 1))
                    pe.wait_ge(diag_ok, H * TOPK + (e + 1))
                    for j in range(4):
                        last = mm(ps[:, 4 * T + j, :], diag[q], vslot[q][:, j * 512:(j + 1) * 512], False, False)
                    last.then_inc(pv_done, 1)

            pe.wait_ge(zero_ok, 1)
            for T in range(NT):
                pe.wait_ge(*((sc_out, 2) if T == 0 else (mod_ok, 4)))
                for j in range(4):
                    mm(ps[:, 4 * T + j, :], zeros, zeros4, True, False)
                with pe.Fori(T * PH, (T + 1) * PH) as H:
                    products(H, T)
                for j in range(4):
                    last = mm(ps[:, 4 * T + j, :], zeros, zeros4, False, True)
                last.then_inc(y_done, 1)

        @block.scalar
        def _(act):
            me = Chain(act, act_s)
            A = act.activation
            act.wait_ge(cols_ok, 1)
            A(sigc, colB[:, 0:16], ACT.Sigmoid).then_inc(sigc_ok, 1)
            for g in range(KT // 2):
                act.wait_ge(xT_done, g + 1)
                A(at(R_HT + g * 2 * S, 2 * S), ps[:, 4 + g % 4, :], ACT.Copy).then_inc(xT_out, 1)
            act.wait_ge(y_need, 1)
            A(lt[1], lt[0], ACT.Exp, scale=-1.0).then_inc(y_ok, 1)
            act.wait_ge(r_ok, 1)
            A(pt[3], pt[2], ACT.Sin).then_inc(sin_ok, 1)
            A(pt[4], pt[2], ACT.Sin, scale=0.5).then_inc(sin_ok, 1)

            def evac_static(b, off):
                act.wait_ge(unit_used, 4 * (b + 1))
                A(at(off, 1024), psblock(b).rearrange("p b c -> p (b c)"), ACT.Copy).then_inc(out_act, 1)

            evac_static(B_QC, W)
            act.wait_ge(kr_done, 1)
            A(krraw, ps[0:ROPE, 4, 0:S], ACT.Copy).then_inc(kr_out, 1)
            evac_static(B_KVC, W + 1024)
            for i in range(2):
                act.wait_ge(ssq_done, i + 1)
                A(rs2[i], ps[:, 6 + i, 0:S], ACT.Sqrt, bias=eps_rms, scale=1.0 / RANK).then_inc(std_ok, 1)

            def head(i, b, first):
                h = i * 2 + b
                act.wait_ge(h_qr, h + 1)
                A(qr, ps[0:ROPE, 0, 0:S], ACT.Copy).then_inc(h_qrout, 1)
                act.wait_ge(h_qk, h + 1)
                if not first:
                    act.wait_ge(h_s, h)
                A(qkn, ps[:, 1, :], ACT.Copy).then_inc(h_qkout, 1)
                act.wait_ge(h_v, h + 1)
                if not first:
                    act.wait_ge(h_o, h)
                    A(arena[:, bass.ds((h - 1) * S + R_OT, S)], ps[:, 5, 0:S], ACT.Copy).then_inc(h_oout, 1)
                A(at(W + 3840, NT * VH), ps[:, 2, 0:NT * VH], ACT.Copy).then_inc(h_vout, 1)
                act.wait_ge(h_neg, h + 1)
                A(sc[:, 0:P], sc[:, 0:P], ACT.Exp, bias=snm[:, 0:1], scale=SM_SCALE, accum_out=ssum[:, 0:1])
                A(sc[:, P:3 * P], sc[:, P:3 * P], ACT.Exp, bias=snm[:, 1:2], scale=SM_SCALE, accum_out=ssum[:, 1:2]).then_inc(h_exp, 1)

            head(0, 0, True)
            head(0, 1, False)
            with act.Fori(1, HEADS // 2) as i:
                for b in range(2):
                    head(i, b, False)
            act.wait_ge(h_o, HEADS)
            A(at(R_OT + (HEADS - 1) * S, S), ps[:, 5, 0:S], ACT.Copy).then_inc(h_oout, 1)

            act.sem_inc(gates_out, 1)
            with act.Fori(0, 4) as g:
                act.wait_ge(unit_used, g * 8 + 4 * (B_XR + 1))
                A(at(XR, 1024), ps[:, 0:2, :].rearrange("p b c -> p (b c)"), ACT.Copy).then_inc(out_act, 1)
                act.wait_ge(unit_used, g * 8 + 4 * (B_XR + 2))
                act.wait_ge(hg_ok, g + 1)
                A(at(GR, 1024), ps[:, 2:4, :].rearrange("p b c -> p (b c)"), ACT.Copy).then_inc(out_act, 1)
                act.wait_ge(gates_done, g + 2)
                for m in range(4):
                    last = A(quad(RR, m), ps[:, 4 + m // 2, (m % 2) * S:(m % 2 + 1) * S], ACT.Sigmoid, bias=ba_c[:, bass.ds(g * 4 + m, 1)])
                last.then_inc(gates_out, 1)
                for m in range(4):
                    last = A(quad(II, m), ps[:, 6 + m // 2, (m % 2) * S:(m % 2 + 1) * S], ACT.Sigmoid, bias=bx_c[:, bass.ds(g * 4 + m, 1)])
                last.then_inc(gates_out, 1)
                act.wait_ge(gates_out, g * 2 + 3)
                for m in range(4):
                    last = A(quad(TP, m), quad(RR, m), ACT.Tanh, scale=sp4[:, bass.ds(g * 4 + m, 1)])
                last.then_inc(tanh_ok, 1)
                act.wait_ge(gelu_in, g + 1)
                A(at(GT, 1024), at(GT, 1024), ACT.Sigmoid, scale=GELU_S).then_inc(gelu_ok, 1)
                act.wait_ge(tanh_ok, g + 1)
                A(at(RR, 1024), at(TP, 1024), ACT.Sqrt).then_inc(sqrt_ok, 1)

            def high(src):
                A(src[0], at(src[2], KT * S), ACT.Copy).then_inc(shi_ok, 1)

            def weight(g, b, s):
                act.wait_ge(in_ring[s], g * 32 + 16 * (b + ADA_UNITS // RING + 1))
                act.wait_ge(unit_used, g * 8 + (4 * b + s - 1))
                A(whi[s % 2], ring[s], ACT.Copy).then_inc(whi_ok, 1)

            def weights(b0, evac=None):
                with act.Fori(0, 2) as g:
                    for k in range(2):
                        weight(g, b0 + k, 2)
                        weight(g, b0 + k, 3)
                        weight(g, b0 + k + 1, 0)
                        if evac is not None:
                            evac(g, b0 + k)
                        weight(g, b0 + k + 1, 1)

            act.wait_ge(hg_ok, 5)
            high(S_HG)
            high(S_HT)

            def branch_gate(g, b):
                k = b % 2
                act.wait_ge(unit_used, g * 8 + 4 * (b + 1))
                A(arena[:, bass.ds(g * 1024 + (R_G + 4096 * k + 512 * (b - k - B_G)), 1024)],
                  ps[:, 2 * k:2 * k + 2, :].rearrange("p b c -> p (b c)"), ACT.Sigmoid).then_inc(out_act, 1)

            with act.Fori(0, 2) as g:
                for k in range(2):
                    branch_gate(g, B_G + k)
            act.wait_ge(wlo_ok, 2)
            weights(B_G2, branch_gate)

            def modulation(ch):
                act.wait_ge(mod_done, ch + 1)
                A(mods[ch], ps[:, 4:8, :].rearrange("p b c -> p (b c)"), ACT.Copy, bias=0.0 if ch == 1 else 1.0).then_inc(mod_ok, 1)

            high(S_OT)
            modulation(0)
            weights(B_RNN)
            modulation(1)
            weights(B_MLA)
            act.wait_ge(keys_t, 1)
            A(at(W + 8448, 2 * P), ps[:, 6, 0:2 * P], ACT.Copy).then_inc(keys_ok, 1)
            modulation(2)
            weights(B_O)
            for T in range(NT):
                act.wait_ge(var_ok, T + 1)
                A(rstd[T][:, 0:1], mv[T][:, 1:2], ACT.Sqrt, bias=eps_ln).then_inc(std1_ok, 1)
            h2hi = by_tile(S_H2[0])
            for n in range(4 * NT):
                c, T = n // NT, n % NT
                act.wait_ge(h2T_done, n + 1)
                A(h2hi[:, 4 * c:4 * c + 4, T * P:(T + 1) * P], ps[:, 4 + n % 4, :].rearrange("p (a c) -> p a c", a=4), ACT.Copy).then_inc(h2T_out, 1)

            def query(b):
                k = b % 2
                act.wait_ge(unit_used, 4 * (b + 1))
                A(at(R_G + 4096 + 1024 * (b - B_WQ), 1024), ps[:, 2 * k:2 * k + 2, :].rearrange("p b c -> p (b c)"), ACT.Copy).then_inc(out_act, 1)

            for b in range(B_WQ, B_END):
                for u in range(2, 6):
                    if b + u // 4 < B_END:
                        weight(0, b + u // 4, u % 4)
                    if u == 4:
                        query(b)
            for T in range(NT):
                act.wait_ge(sc_done, T + 1)
                A(at(R_OT + D * T, D), ps[:, 4 - 4 * T:8 - 4 * T, :].rearrange("p b c -> p (b c)"), ACT.Copy).then_inc(sc_out, 1)
            act.wait_ge(sc_out, 1)

            def stage_scores(H):
                A(stage, arena[:, bass.ds(H * (2 * NK) + R_OT, 2 * NK)], ACT.Copy).then_inc(stage_ok, 1)

            def gate_exp(H):
                act.wait_ge(best_ok, H + 1)
                A(gexp, best, ACT.Exp, bias=negbest, accum_out=gsum).then_inc(gexp_ok, 1)

            stage_scores(0)
            modulation(3)
            gate_exp(0)
            act.sem_inc(a_ok, 2)

            def diagonals(H, topk):
                for q in range(TOPK // GROUP):
                    b = q % 2
                    if q == 0 and topk:
                        act.wait_ge(topk_ok, H + 1)
                        stage_scores(H + 1)
                    if q == 1 and topk:
                        gate_exp(H + 1)
                    c0, c1 = b * GROUP, (b + 1) * GROUP
                    act.wait_ge(z_ok, H * (TOPK // GROUP) + (q + 1))
                    me.do(A(zs[:, c0:c1], zu[:, c0:c1], ACT.Sigmoid, scale=GELU_S))
                    me.wait()
                    for s in range(c0, c1):
                        last = A(za[:, s:s + 1], zs[:, s:s + 1], ACT.Copy, scale=zg[:, s:s + 1])
                    last.then_inc(a_ok, 1)
                    act.wait_ge(a_ok, H * (TOPK // GROUP) + (q + 3))
                    for s in range(c0, c1):
                        act.wait_ge(pv_done, H * TOPK + (q * GROUP + s - c0 + 1))
                        A(diag[s], ident, ACT.Copy, scale=za[:, s:s + 1]).then_inc(diag_ok, 1)

            def ln2_std(T):
                act.wait_ge(var_ok, NT + T + 1)
                A(rstd[T][:, 0:1], mv[T][:, 1:2], ACT.Sqrt, bias=eps_ln).then_inc(std1_ok, 1)

            def loop(first, end, topk=True):
                with act.Fori(first, end) as H:
                    me.enter(H, first, TOPK // GROUP)
                    diagonals(H, topk)
                me.leave(end - first)

            loop(0, PH)
            diagonals(PH, True)
            ln2_std(0)
            loop(PH + 1, NT * PH - 1)
            diagonals(NT * PH - 1, False)
            ln2_std(1)

        @block.vector
        def _(dve):
            me = Chain(dve, dve_s)
            V = dve
            TT, TS, STT = V.tensor_tensor, V.tensor_scalar, V.scalar_tensor_tensor
            V.memset(acc[0], 0.0).then_inc(acc_zero, 1)
            V.memset(acc[1], 0.0).then_inc(acc_zero, 1)
            me.do(V.memset(eps_rms, RMS_EPS))
            me.do(V.memset(eps_ln, LN_EPS))
            dve.wait_ge(cols_t, 1)
            V.tensor_copy(colB, ps[:, 0, 0:24]).then_inc(cols_ok, 1)
            dve.wait_ge(cols_ok, 1)
            dve.wait_ge(sigc_ok, 1)
            me.do(TT(cact, colB[:, 0:16], sigc, ALU.mult))
            me.wait()
            dve.sem_inc(cact_ok, 1)
            dve.wait_ge(cols_t, 2)
            me.do(V.tensor_copy(colA, ps[:, 1, 0:P]))
            dve.wait_ge(in_bada, 32)
            for ch in range(2):
                with dve.Fori(0, KT // RING) as i:
                    for s in range(RING):
                        dve.wait_ge(in_ring[s], i * 16 + 16 * (ch * (KT // RING) + 1))
                        STT(acc[ch], ring[s], cact[:, bass.ds(i * RING + s, 1)], acc[ch], ALU.mult, ALU.add).then_inc(ada_used, 1)
                        dve.wait_ge(ada_used, i * RING + (ch * KT + s + 1))
                dve.sem_inc(acc_ok, 1)
            dve.wait_ge(modc_done, 2)
            me.do(V.tensor_copy(sh1, ps[:, 2, 0:KT]))
            me.do(TS(sc1, ps[:, 2, KT:2 * KT], 1.0, None, ALU.add))
            me.wait()
            dve.wait_ge(xT_out, KT // 2)
            for k in range(KT):
                TS(hT[:, k, :], hT[:, k, :], sc1[:, k:k + 1], sh1[:, k:k + 1], ALU.mult, ALU.add).then_inc(hT_ok, 1)
            me.do(TS(lt[3], lam_c, -1.0, None, ALU.mult))
            me.wait()
            me.do(TT(lt[0], lt[3], lam_c, ALU.max))
            me.wait()
            dve.sem_inc(y_need, 1)
            dve.wait_ge(y_ok, 1)
            me.do(TS(lt[2], lt[1], 2.0, None, ALU.add))
            me.wait()
            me.do(V.reciprocal(lt[2], lt[2]))
            me.wait()
            me.do(TT(lt[1], lt[1], lt[2], ALU.mult))
            me.wait()
            me.do(TT(lt[2], lt[1], lt[1], ALU.mult))
            me.wait()
            me.do(TS(lt[4], lt[2], 1.0 / 19.0, None, ALU.mult))
            me.wait()
            for k in range(17, 2, -2):
                me.do(STT(lt[4], lt[4], 1.0 / k, lt[2], ALU.add, ALU.mult))
                me.wait()
            me.do(STT(lt[4], lt[4], 1.0, lt[1], ALU.add, ALU.mult))
            me.do(TS(lt[3], lt[3], 0.0, 4.0, ALU.max, ALU.mult))
            me.wait()
            me.do(STT(sp4, lt[4], 8.0, lt[3], ALU.mult, ALU.add))
            dve.wait_ge(in_pos, 16)
            me.do(V.tensor_copy(pt[1], pt[0].bitcast(I32)))
            me.wait()
            me.do(TS(pt[1], pt[1], cst[0:ROPE, K_INVF:K_INVF + 1], None, ALU.mult))
            me.wait()
            magic = 1.5 * 2.0 ** 23
            me.do(TS(pt[3], pt[1], 1.0 / (2.0 * math.pi), magic, ALU.mult, ALU.add))
            me.wait()
            me.do(TS(pt[3], pt[3], -magic, None, ALU.add))
            me.wait()
            c1 = 6.28125
            c2 = float(np.float32(np.round((2.0 * math.pi - c1) * 2.0 ** 21) / 2.0 ** 21))
            c3 = 2.0 * math.pi - c1 - c2
            src = pt[1]
            for c in (c1, c2, c3):
                me.do(STT(pt[2], pt[3], -c, src, ALU.mult, ALU.add))
                me.wait()
                src = pt[2]
            me.do(TS(pt[2], pt[2], 3.1415925, -3.1415925, ALU.min, ALU.max))
            me.wait()
            dve.sem_inc(r_ok, 1)
            dve.wait_ge(sin_ok, 2)
            me.do(V.tensor_copy(sinT, pt[3]))
            me.do(TT(pt[4], pt[4], pt[4], ALU.mult))
            me.wait()
            me.do(TS(cosT, pt[4], -2.0, 1.0, ALU.mult, ALU.add))
            for i, lat in enumerate((qcT, kvT)):
                dve.wait_ge(out_act, i + 1)
                TT(sq2[i], lat, lat, ALU.mult).then_inc(sq_ok, 1)
            dve.wait_ge(krot_done, 1)
            me.wait()
            me.do(TT(rt, krraw, cosT, ALU.mult))
            me.do(TT(krT, ps[0:ROPE, 5, 0:S], sinT, ALU.mult))
            me.wait()
            TT(krT, krT, rt, ALU.add).then_inc(kr_ok, 1)
            for i, lat in enumerate((qcT, kvT)):
                dve.wait_ge(std_ok, i + 1)
                me.do(V.reciprocal(rs2[i], rs2[i]))
                me.wait()
                for k in range(LT):
                    last = STT(lat[:, k, :], lat[:, k, :], colB[:, 16 + LT * i + k:17 + LT * i + k], rs2[i], ALU.mult, ALU.mult)
                last.then_inc(lat_ok, 1)

            def transposed_out(h):
                dve.wait_ge(h_t, h + 1)
                if True:
                    V.tensor_copy(at(W + 4736, 3 * P), ps[:, 4, 0:3 * P]).then_inc(h_tout, 1)

            def softmax(h, first):
                dve.wait_ge(h_s, h + 1)
                if not first:
                    dve.wait_ge(h_t, h)
                me.do(TT(sc, ps[:, 3, 0:3 * P], cst[:, K_MASK:K_MASK + 3 * P], ALU.add))
                me.wait()
                me.do(V.tensor_reduce(smx[:, 0:1], sc[:, 0:P], AX_X, ALU.max))
                me.do(V.tensor_reduce(smx[:, 1:2], sc[:, P:3 * P], AX_X, ALU.max))
                me.wait()
                TS(snm, smx, -SM_SCALE, None, ALU.mult).then_inc(h_neg, 1)
                dve.wait_ge(h_exp, h + 1)
                me.do(V.reciprocal(srec, ssum))
                me.wait()
                me.do(TS(sc[:, 0:P], sc[:, 0:P], srec[:, 0:1], None, ALU.mult))
                TS(sc[:, P:3 * P], sc[:, P:3 * P], srec[:, 1:2], None, ALU.mult).then_inc(h_p, 1)

            def head(i, b, first):
                h = i * 2 + b
                dve.wait_ge(h_qrout, h + 1)
                me.do(TT(rt, qr, cosT, ALU.mult))
                dve.wait_ge(h_rot, h + 1)
                if not first:
                    dve.wait_ge(h_s, h)
                me.do(TT(qro, ps[0:ROPE, 0, S:2 * S], sinT, ALU.mult))
                me.wait()
                TT(qro, qro, rt, ALU.add).then_inc(h_rope, 1)
                if not first:
                    transposed_out(h - 1)
                softmax(h, first)

            head(0, 0, True)
            head(0, 1, False)
            with dve.Fori(1, HEADS // 2) as i:
                me.enter(i, 1, 14)
                for b in range(2):
                    head(i, b, False)
            me.leave(HEADS // 2 - 1)
            transposed_out(HEADS - 1)

            dve.sem_inc(hg_ok, 1)
            with dve.Fori(0, 4) as g:
                me.enter(g, 0, 30)
                dve.wait_ge(out_act, g * 2 + (B_XR + 1))
                for m in range(4):
                    me.do(TS(quad(XC, m), quad(XR, m), conv_c[:, bass.ds(g * 4 + (48 + m), 1)], convb_c[:, bass.ds(g * 4 + m, 1)], ALU.mult, ALU.add))
                for d in range(1, CONV):
                    me.wait()
                    for m in range(4):
                        o, x = at(XC + S * m + d, S - d), at(XR + S * m, S - d)
                        me.do(STT(o, x, conv_c[:, bass.ds(g * 4 + (16 * (3 - d) + m), 1)], o, ALU.mult, ALU.add))
                me.wait()
                dve.sem_inc(xc_ok, 1)
                dve.wait_ge(out_act, g * 2 + (B_XR + 2))
                gt, gr = at(GT, 1024), at(GR, 1024)
                me.do(TT(gt, gr, gr, ALU.mult))
                me.wait()
                me.do(TS(gt, gt, GELU_C, 1.0, ALU.mult, ALU.add))
                me.wait()
                TT(gt, gt, gr, ALU.mult).then_inc(gelu_in, 1)
                rr, ii, tp, qq, xc = (at(o, 1024) for o in (RR, II, TP, QQ, XC))
                dve.wait_ge(gates_out, g * 2 + 3)
                me.do(TT(ii, ii, xc, ALU.mult))
                dve.wait_ge(tanh_ok, g + 1)
                me.do(TS(qq, tp, 1.0, None, ALU.add))
                me.wait()
                me.do(V.reciprocal(qq, qq))
                me.wait()
                me.do(TT(ii, ii, qq, ALU.mult))
                dve.wait_ge(sqrt_ok, g + 1)
                me.do(TS(tp, qq, 2.0, -1.0, ALU.mult, ALU.add))
                me.wait()
                me.do(STT(ii, ii, 2.0, rr, ALU.mult, ALU.mult))
                dve.wait_ge(gelu_ok, g + 1)
                me.do(TT(gt, gt, gr, ALU.mult))
                me.wait()
                for m in range(4):
                    me.do(V.tensor_tensor_scan(quad(XC, m), quad(TP, m), quad(II, m), 0.0, ALU.mult, ALU.add))
                me.wait()
                me.do(TT(arena[:, bass.ds(g * 1024 + R_HG, 1024)], xc, gt, ALU.mult))
                me.wait()
                dve.sem_inc(hg_ok, 1)
            me.leave(4)

            def low(src, n, j=None):
                o, w = (0, 4096) if j is None else (1024 * j, 1024)
                dve.wait_ge(shi_ok, n)
                TT(src[1][:, o:o + w], at(src[2] + o, w), src[0][:, o:o + w].bitcast(F32), ALU.subtract).then_inc(slo_ok, 4 if j is None else 1)

            def weight(g, b, s):
                dve.wait_ge(whi_ok, g * 8 + (4 * (b - B_G2) + s + 1))
                TT(wlo[s], ring[s], whi[s % 2].bitcast(F32), ALU.subtract).then_inc(wlo_ok, 1)

            def weights(b0, evac, more=None):
                with dve.Fori(0, 2) as g:
                    me.enter(g, 0, 2 * evac_steps[b0])
                    for k in range(2):
                        weight(g, b0 + k, 2)
                        weight(g, b0 + k, 3)
                        weight(g, b0 + k + 1, 0)
                        evac(g, b0 + k)
                        weight(g, b0 + k + 1, 1)
                        if more is not None:
                            more(g, b0 + k)
                me.leave(2)

            evac_steps = {B_G2: 0, B_RNN: 1, B_MLA: 2, B_O: 6}
            low(S_HG, 1)
            for j in range(4):
                dve.wait_ge(unit_used, 4 * (B_G2 - 1) + j + 1)
                low(S_HT, 2, j)
                if 1 <= j <= 2:
                    dve.wait_ge(in_ring[j - 1], 16 * (B_G2 + ADA_UNITS // RING + 1))
                    if j == 1:
                        dve.wait_ge(mod_part, 1)
                    V.tensor_copy(whi[j - 1], ring[j - 1]).then_inc(whi_ok, 1)
                    weight(0, B_G2, j - 1)
            weights(B_G2, lambda g, b: None)
            low(S_OT, 3)

            dve.sem_inc(out_dve, 1)

            def gT_at(k, g, j):
                return arena[:, bass.ds(g * 2048 + (R_G + 4096 * k + 1024 * j), 1024)]

            def gated(j, g, b):
                k = b % 2
                dve.wait_ge(unit_used, g * 8 + 4 * (b + 1))
                me.do(TT(gT_at(j, g, k), gT_at(j, g, k), ps[:, 2 * k:2 * k + 2, :].rearrange("p b c -> p (b c)"), ALU.mult))
                me.wait()
                dve.sem_inc(out_dve, 1)

            def mixed(g, b):
                k = b % 2
                me.do(TT(gT_at(0, g, k), gT_at(0, g, k), gT_at(1, g, k), ALU.add))
                me.wait()
                cols = bass.ds(g * 2048 + 1024 * k, 1024)
                V.tensor_copy(split["w1"][:, cols], gT_at(0, g, k)).then_inc(mix_ok, 1)
                dve.wait_ge(mix_ok, g * 2 + (k + 1))
                TT(split["g0"][:, cols], gT_at(0, g, k), split["w1"][:, cols].bitcast(F32), ALU.subtract).then_inc(slo_ok, 1)

            weights(B_RNN, lambda g, b: gated(0, g, b))
            weights(B_MLA, lambda g, b: gated(1, g, b), mixed)
            dve.wait_ge(in_ln1, 32)
            dve.wait_ge(mod_ok, 3)
            me.do(TT(ln_t, ln1[1], mods[2], ALU.mult))
            me.wait()
            me.do(TT(mods[1], mods[1], ln_t, ALU.add))
            me.do(TT(mods[2], mods[2], ln1[0], ALU.mult))
            dve.wait_ge(mod_ok, 1)
            dve.wait_ge(in_x2, 16)

            def gated_out(g, b):
                k = b % 2
                dve.wait_ge(unit_used, g * 8 + 4 * (b + 1))
                for T in range(NT):
                    me.do(TT(wo_t[k][:, T * 512:(T + 1) * 512], ps[:, 2 * k + T, :],
                             front[:, bass.ds(g * 1024 + (R_MODS + 512 * k), 512)], ALU.mult))
                me.wait()
                dve.sem_inc(out_dve, 1)

            def residual(g, b):
                k = b % 2
                for T in range(NT):
                    xs = arena[:, bass.ds(g * 1024 + (W + D * T + 512 * k), 512)]
                    me.do(STT(xs, xs, ALPHA, wo_t[k][:, T * 512:(T + 1) * 512], ALU.mult, ALU.add))
                me.wait()
                for T in range(NT):
                    me.do(V.bn_stats(arena[:, bass.ds(g * 12 + (o_bn[T] + 6 * k), 6)], arena[:, bass.ds(g * 1024 + (W + D * T + 512 * k), 512)]))

            weights(B_O, gated_out, residual)

            def scale_of(T, n):
                me.wait()
                V.bn_aggr(mv[T], bn6[T][:, :, :]).then_inc(var_ok, 1)
                dve.wait_ge(std1_ok, n + 1)
                me.do(V.reciprocal(rstd[T][:, 1:2], rstd[T][:, 0:1]))

            for T in range(NT):
                scale_of(T, T)
            me.wait()
            h2hi, h2lo = by_tile(S_H2[0]), by_tile(S_H2[1])

            def low_h2(n):
                c, T = n // NT, n % NT
                dve.wait_ge(h2T_out, n + 1)
                place = (slice(None), slice(4 * c, 4 * c + 4), slice(T * P, (T + 1) * P))
                TT(h2lo[place], ps[:, 4 + n % 4, :].rearrange("p (a c) -> p a c", a=4), h2hi[place].bitcast(F32), ALU.subtract).then_inc(slo_ok, 1)

            for c in range(4):
                cs = slice(512 * c, 512 * (c + 1))
                for T in range(NT):
                    me.do(TS(x1[T][:, cs], x1[T][:, cs], mv[T][:, 0:1], rstd[T][:, 1:2], ALU.subtract, ALU.mult))
                    me.wait()
                    me.do(TT(h2[T][:, cs], x1[T][:, cs], mods[2][:, cs], ALU.mult))
                    me.wait()
                    TT(h2[T][:, cs], h2[T][:, cs], mods[1][:, cs], ALU.add).then_inc(h2_ok, 1)
                    if c:
                        low_h2(NT * (c - 1) + T)
            for n in range(3 * NT, 4 * NT):
                low_h2(n)
            weight(0, B_WQ, 2)
            weight(0, B_WQ, 3)
            for T in range(NT):
                me.do(TT(x1[T], x1[T], ln1[0], ALU.mult))
                me.wait()
                me.do(TT(x1[T], x1[T], ln1[1], ALU.add))
            for b in range(B_WQ + 1, B_END):
                for s in range(RING):
                    weight(0, b, s)
            dve.wait_ge(sc_out, 2)
            V.memset(zeros, 0.0).then_inc(zero_ok, 1)
            dve.sem_inc(dots_done, 2 * GROUP)

            def topk(H):
                dve.wait_ge(stage_ok, H + 1)
                dve.sem_inc(dve_gate, 1)
                halves = [(stage[:, a * NK:(a + 1) * NK], tops[:, a * TOPK:(a + 1) * TOPK], topi[:, a * TOPK:(a + 1) * TOPK]) for a in range(2)]
                pairs = [(cand.rearrange("p a b -> p (a b)"), best, bestj)]

                def hold():
                    me.wait()
                    dve.sem_inc(dve_gate, 1)

                def top16(lots):
                    for v, vo, io in lots:
                        me.do(V.max(vo[:, 0:8], v))
                    hold()
                    for v, vo, io in lots:
                        me.do(V.max_index(io[:, 0:8], vo[:, 0:8], v))
                    hold()
                    for v, vo, io in lots:
                        me.do(V.match_replace(v, vo[:, 0:8], v, -3.0e38))
                    hold()
                    for v, vo, io in lots:
                        me.do(V.max(vo[:, 8:16], v))
                    hold()
                    for v, vo, io in lots:
                        me.do(V.max_index(io[:, 8:16], vo[:, 8:16], v))

                top16(halves)
                me.do(TT(cand, tops[:, 0:TOPK].unsqueeze(2).to_broadcast([P, TOPK, TOPK]),
                         tops[:, TOPK:].unsqueeze(1).to_broadcast([P, TOPK, TOPK]), ALU.add))
                me.wait()
                me.do(V.tensor_copy(topf, topi))
                hold()
                top16(pairs)
                me.wait()
                me.do(TS(ranki[:, 0:TOPK], bestj, 4, None, ALU.logical_shift_right))
                me.do(TS(ranki[:, TOPK:], bestj, 15, None, ALU.bitwise_and))
                TS(negbest, best[:, 0:1], -1.0, None, ALU.mult).then_inc(best_ok, 1)
                me.wait()
                me.do(V.tensor_copy(rankf, ranki))
                me.wait()
                me.do(TT(onehot, rankf.unsqueeze(2).to_broadcast([P, 2 * TOPK, TOPK]),
                         cst[:, K_IOTA:K_IOTA + TOPK].unsqueeze(1).to_broadcast([P, 2 * TOPK, TOPK]), ALU.is_equal))
                me.wait()
                oh4 = onehot.rearrange("p (a k) c -> p a k c", a=2)
                me.do(TT(oh4, oh4, topf.rearrange("p (a c) -> p a c", a=2).unsqueeze(2).to_broadcast([P, 2, TOPK, TOPK]), ALU.mult))
                me.wait()
                me.do(V.tensor_reduce(keyf, onehot, AX_X, ALU.add))
                me.wait()
                STT(arena[:, bass.ds(H * TOPK + o_idx, TOPK)].bitcast(U32), keyf[:, 0:TOPK], float(NK), keyf[:, TOPK:], ALU.mult, ALU.add
                    ).then_inc(topk_ok, 1)
                dve.wait_ge(gexp_ok, H + 1)
                me.do(V.reciprocal(ginv, gsum))
                me.wait()
                me.do(TS(arena[:, bass.ds(H * TOPK + o_gate, TOPK)], gexp, ginv, None, ALU.mult))

            def dots(H, T, topk_too):
                for q in range(TOPK // GROUP):
                    b = q % 2
                    c0, c1 = b * GROUP, (b + 1) * GROUP
                    dve.wait_ge(a_ok, H * (TOPK // GROUP) + (q + 1))
                    for s in range(c0, c1):
                        dve.wait_ge(in_u[s], H * 32 + 16 * (q // 2 + 1))
                        V.tensor_tensor_reduce(uslot[s], uslot[s], h2[T], 1.0, 0.0, ALU.mult, ALU.add, zraw[:, s:s + 1]).then_inc(dots_done, 1)
                    dve.wait_ge(dots_done, H * TOPK + (q * GROUP + 3 * GROUP))
                    z, u = zraw[:, c0:c1], zu[:, c0:c1]
                    me.do(TT(u, z, z, ALU.mult))
                    me.do(TT(zg[:, c0:c1], z, arena[:, bass.ds(H * TOPK + (o_gate + q * GROUP), GROUP)], ALU.mult))
                    me.wait()
                    me.do(TS(u, u, GELU_C, 1.0, ALU.mult, ALU.add))
                    me.wait()
                    TT(u, u, z, ALU.mult).then_inc(z_ok, 1)
                    if q == 0 and topk_too:
                        topk(H + 1)

            def finish(T):
                dve.wait_ge(y_done, T + 1)
                for c in range(4):
                    cs = slice(512 * c, 512 * (c + 1))
                    me.do(TT(h2[T][:, cs], ps[:, 4 * T + c, :], mods[3][:, cs], ALU.mult))
                    me.wait()
                    me.do(STT(x1[T][:, cs], x1[T][:, cs], ALPHA, h2[T][:, cs], ALU.mult, ALU.add))
                    me.wait()
                    me.do(V.bn_stats(bn6[T][:, c, :], x1[T][:, cs]))
                scale_of(T, NT + T)
                me.wait()
                for c in range(4):
                    cs = slice(512 * c, 512 * (c + 1))
                    me.do(TS(x1[T][:, cs], x1[T][:, cs], mv[T][:, 0:1], rstd[T][:, 1:2], ALU.subtract, ALU.mult))
                    me.wait()
                    me.do(TT(x1[T][:, cs], x1[T][:, cs], ln2[0][:, cs], ALU.mult))
                    me.wait()
                    TT(x1[T][:, cs], x1[T][:, cs], ln2[1][:, cs], ALU.add).then_inc(ln2_ok, 1)

            def loop(first, end, T):
                with dve.Fori(first, end) as H:
                    me.enter(H, first, DOTS_STEPS + TOPK_STEPS)
                    dots(H, T, True)
                me.leave(end - first)

            topk(0)
            dve.wait_ge(mod_ok, 4)
            loop(0, PH, 0)
            dots(PH, 1, True)
            dve.wait_ge(in_ln2, 32)
            finish(0)
            loop(PH + 1, NT * PH - 1, 1)
            dots(NT * PH - 1, 1, False)
            finish(1)


INPUTS = ("x", "c", "positions", "w_ada", "b_ada", "w_in", "conv_w", "conv_b", "w_rg_a", "b_rg_a", "w_rg_x", "b_rg_x",
          "rg_lambda", "w_rnn_out", "q_norm_g", "w_uq", "kv_norm_g", "w_ukv", "w_mla_out", "w_o", "ln1_g", "ln1_b",
          "peer_wq", "peer_keys", "peer_u", "peer_v", "ln2_g", "ln2_b")


def kernel(**inputs):
    import concourse.bacc as bacc
    from concourse.bass_utils import run_bass_kernel_spmd as run

    nc = bacc.Bacc("TRN2", target_bir_lowering=False, num_devices=1)
    arrays = {n: np.ascontiguousarray(inputs[n]) for n in INPUTS}
    arrays["cst"] = constants()
    t = {n: nc.dram_tensor(f"in_{n}", a.shape, mybir.dt.from_np(a.dtype), kind="ExternalInput").ap() for n, a in arrays.items()}
    out = nc.dram_tensor("out_y", (1, S, D), F32, kind="ExternalOutput").ap()
    build(nc, t, out)
    r = run(nc, [{f"in_{n}": a for n, a in arrays.items()}], core_ids=[0])
    return r.results[0]["out_y"]
```

```python
import math
from contextlib import ExitStack

import numpy as np

import concourse.bass as bass
from concourse import mybir

F32 = mybir.dt.float32
F32R = mybir.dt.float32r
U32 = mybir.dt.uint32
I32 = mybir.dt.int32
ALU = mybir.AluOpType
ACT = mybir.ActivationFunctionType
AX_X = mybir.AxisListType.X

P = 128
D = 2048
S = 256
NT = S // P
KT = D // P
HEADS = 16
RANK = 512
LT = RANK // P
NOPE, ROPE, VH = 128, 64, 128
CONV = 4
PH, NK, TOPK = 8, 128, 16
HP = 2 * PH
EXPERTS = PH * TOPK
ALPHA = 2.0 ** 0.25
LN_EPS, RMS_EPS = 1e-5, 1e-6
SM_SCALE = (NOPE + ROPE) ** -0.5
GELU_C, GELU_S = 0.044715, 2.0 * math.sqrt(2.0 / math.pi)

C_XR, C_GR, C_QC, C_KVC = 0, D, 2 * D, 2 * D + RANK
C_KR = C_KVC + RANK
C_GRNN = C_KR + ROPE
C_GMLA = C_GRNN + D

UNIT = 2048
RING = 4
B_QC, B_KVC, B_XR, B_G, B_G2, B_RNN, B_MLA, B_O, B_WQ, B_END = 0, 1, 2, 10, 12, 18, 22, 26, 30, 34
ADA_UNITS = 2 * KT
SLOT_BASE = 2 * ADA_UNITS // RING - B_XR + 1
GROUP = 4
FRONT, ARENA = 20480, 32520

K_ID, K_MASK, K_ROT, K_IOTA, K_INVF, K_ONES, K_END = 0, 128, 512, 640, 656, 657, 785


def constants():
    c = np.zeros((P, K_END), np.float32)
    c[:, K_ID:K_ID + P] = np.eye(P)
    tri = np.where(np.arange(P)[None, :] <= np.arange(P)[:, None], 0.0, -1e30)
    c[:, K_MASK:K_MASK + P] = tri
    c[:, K_MASK + 2 * P:K_MASK + 3 * P] = tri
    half = ROPE // 2
    for o in (0, ROPE):
        for m in range(half):
            c[o + m + half, K_ROT + o + m] = -1.0
            c[o + m, K_ROT + o + half + m] = 1.0
    c[:, K_IOTA:K_IOTA + TOPK] = np.arange(TOPK)
    freq = np.float32(10000.0) ** (-np.arange(0, ROPE, 2, dtype=np.float32) / np.float32(ROPE))
    c[:, K_INVF] = np.concatenate([freq] * 4)
    c[:, K_ONES:K_ONES + P] = 1.0
    return c


DOTS_STEPS, TOPK_STEPS = 12, 25


class Chain:

    def __init__(self, eng, sem):
        self.eng, self.sem, self.base, self.n = eng, sem, 0, 0

    def do(self, ins):
        ins.then_inc(self.sem, 1)
        self.n += 1
        return ins

    def wait(self):
        self.eng.wait_ge(self.sem, self.base + self.n)

    def enter(self, i, first, per):
        self.kept, self.per = self.base + self.n, per
        self.base, self.n = i * per + (self.kept - first * per), 0

    def leave(self, rounds):
        assert self.n == self.per, (self.n, self.per)
        self.base, self.n = self.kept + rounds * self.per, 0


def build(nc, t, out):
    with ExitStack() as ctx:
        def sem(name):
            return ctx.enter_context(nc.semaphore(name))

        with nc.sbuf_tensor("front", [P, FRONT], F32) as front, nc.sbuf_tensor("arena", [P, ARENA], F32) as arena:
            pass
        split = {n: ctx.enter_context(nc.sbuf_tensor(f"split_{n}", [P, words], F32R)) for n, words in (
            ("ring", RING * UNIT), ("between0", 4 * D), ("pada", 2 * D), ("ht", KT * S), ("w0", 4096), ("w1", 4096), ("between1", 2048),
            ("hg", KT * S), ("g0", KT * S), ("between2", KT * S), ("ot", KT * S))}
        ps = ctx.enter_context(nc.psum_tensor("ps", [P, 8, 512], F32))

        R_RING, R_MODS, R_PADA = 0, 8192, 16384
        R_HT, R_WORK, R_HG, R_G, R_OT, R_SM = 0, 4096, 14336, 18432, 26624, 30720

        def at(off, n):
            return arena[:, off:off + n]

        def infront(off, n):
            return front[:, off:off + n]

        def at3(off, a, b):
            return at(off, a * b).rearrange("p (a b) -> p a b", a=a)

        sm = [R_SM]

        def small(n):
            sm[0] += n
            assert sm[0] <= ARENA
            return sm[0] - n

        ring = [infront(R_RING + UNIT * s, UNIT) for s in range(RING)]
        ring3 = [r.rearrange("p (t c) -> p t c", t=4) for r in ring]
        mods = [infront(R_MODS + D * i, D) for i in range(4)]
        pada = [infront(R_PADA + D * i, D) for i in range(2)]
        hT = at3(R_HT, KT, S)
        hgT = at3(R_HG, KT, S)
        gT = [at3(R_G, KT, S), at3(R_G + KT * S, KT, S)]
        oT = at3(R_OT, KT, S)
        xin = at3(R_G, NT, D)
        acc = at(R_G + KT * S, 2 * D).rearrange("p (j h c) -> p j h c", j=4, h=2)
        lat_w = [at(o, D).rearrange("p (t c) -> p t c", t=4) for o in (R_HG, R_HG + D)] + [p.rearrange("p (t c) -> p t c", t=4) for p in pada]

        eps_rms, eps_ln = at(small(1), 1), at(small(1), 1)
        cst = at(small(K_END), K_END)
        ident = cst[:, K_ID:K_ID + P]
        ones = cst[:, K_ONES:K_ONES + P]
        colA = at(small(P), P)
        colB = at(small(24), 24)
        conv_c, convb_c, ba_c, bx_c, lam_c = (colA[:, a:b] for a, b in ((0, 64), (64, 80), (80, 96), (96, 112), (112, 128)))
        sigc = at(small(16), 16)
        cact = at(small(16), 16)
        sh1 = at(small(4), 4)
        sc1 = at(small(4), 4)
        sp4 = at(small(16), 16)
        lt = [at(small(16), 16) for _ in range(5)]
        smx = at(small(2), 2)
        snm = at(small(2), 2)
        ssum = at(small(2), 2)
        srec = at(small(2), 2)
        o_bn = [small(24) for _ in range(NT)]
        bn6 = [at3(o, 4, 6) for o in o_bn]
        mv = [at(small(2), 2) for _ in range(NT)]
        rstd = [at(small(2), 2) for _ in range(NT)]
        shift = [at(small(1), 1) for _ in range(NT)]
        zraw = at(small(8), 8)
        zu = at(small(8), 8)
        zg = at(small(8), 8)
        zs = at(small(8), 8)
        za = at(small(8), 8)
        idxu, idxv = (at(small(8), 8).bitcast(U32) for _ in range(2))
        o_gate = small(NT * EXPERTS)
        o_idx = small(NT * EXPERTS)

        W = R_WORK
        qcT, kvT = at3(W, LT, S), at3(W + 1024, LT, S)
        cosT, sinT, krT = (at(W + o, S) for o in (2048, 2304, 2560))
        qkn = at(W + 2816, 2 * S)
        qn, kn = qkn[:, 0:S], qkn[:, S:2 * S]
        qro = at(W + 3584, S)
        uqr = at3(R_G, LT, HEADS * ROPE)
        o_qr, o_qrs = R_G + 4096, R_G + 6144
        vv = at3(W + 3840, NT, VH)
        rt = at(W + 4096, S)
        sc = at(W + 4352, 384)
        pT = at3(W + 4736, 3, P)
        sq2 = [at3(W + 5120, LT, S), at3(W + 6144, LT, S)]
        rs2 = [at(W + 7168, S), at(W + 7424, S)]
        pt = [at(W + 7680 + S * i, S) for i in range(5)]
        krraw = at(W + 8960, S)
        stA, stB = at(W + 9216, P), arena[0:24, W + 9344:W + 9472]
        uq = [at3(R_HG + 768 * b, LT, NOPE) for b in range(2)]
        ukv = [at3(R_HG + 1536 + 1024 * b, LT, 256) for b in range(2)]
        krw = at3(R_OT, KT, 2 * ROPE)

        XR, GR, XC, RR, II, TP, QQ, GT = (W + 1024 * i for i in range(8))
        wg = at(W + 8192, 1024).rearrange("p (g h c) -> p g h c", g=2, h=4)

        def quad(off, j):
            return at(off + S * j, S)

        x1 = [at(W + D * i, D) for i in range(NT)]
        h2 = [at(W + 2 * D + D * i, D) for i in range(NT)]
        keys = at3(W + 8192, 2, P)
        keysT = at3(W + 8448, 2, P)
        stage, cand, onehot = at(W + 9216, 2 * NK), at3(W + 9472, TOPK, TOPK), at3(W + 9728, 2 * TOPK, TOPK)
        tk = [R_SM + 2 + K_MASK]

        def tk_at(n):
            tk[0] += n
            assert tk[0] <= R_SM + 2 + K_ROT
            return at(tk[0] - n, n)

        tops, topi, topf = tk_at(2 * TOPK), tk_at(2 * TOPK).bitcast(U32), tk_at(2 * TOPK)
        best, bestj, ranki, rankf, keyf = tk_at(TOPK), tk_at(TOPK).bitcast(U32), tk_at(2 * TOPK).bitcast(U32), tk_at(2 * TOPK), tk_at(2 * TOPK)
        negbest, gexp, gsum, ginv = tk_at(1), tk_at(TOPK), tk_at(1), tk_at(1)
        wo_t = [at(R_OT + 1024 * b, 1024) for b in range(2)]

        S_HT, S_HG, S_OT, S_MIX, S_H2 = (
            (split[h][:, :], split[l][:, :], off) for h, l, off in (
                ("w0", "ht", R_HT), ("w1", "hg", R_HG), ("ht", "ot", R_OT), ("w1", "g0", R_G), ("ht", "g0", R_G)))

        def by_tile(part):
            return part.rearrange("p (k s) -> p k s", k=KT)

        whi = [split["pada"][:, UNIT * i:UNIT * (i + 1)] for i in range(2)]
        wlo = [split["ring"][:, UNIT * i:UNIT * (i + 1)] for i in range(RING)]
        ln1 = [at(R_HG, D), at(R_HG + D, D)]
        ln2 = [at(R_G + 2 * D, D), at(R_OT, D)]
        ln_t = at(R_OT + D, D)
        zeros = colA
        zeros4 = zeros.unsqueeze(1).to_broadcast([P, 4, P])
        qT = [at3(R_G + KT * S + 1024 * i, 4, S) for i in range(2)]
        mslot = [at(R_G + D * i, D) for i in range(4)]
        uslot = [at(R_HG, D), at(R_HG + D, D)] + mods[:2] + [pada[0], ring[2], pada[1], ring[3]]
        vslot = [at(R_G + 3 * D, D), mods[2], ring[0], ring[1]] + [at(R_HT, D), at(R_HT + D, D), at(R_G, D), at(R_G + D, D)]
        diag = [at(W + 8192 + P * i, P) for i in range(8)]

        in_cst, in_par, in_pos, in_x, in_kr, in_bada = (sem(n) for n in ("in_cst", "in_par", "in_pos", "in_x", "in_kr", "in_bada"))
        in_ring = [sem(f"in_ring{i}") for i in range(RING)]
        in_head = [sem(f"in_head{i}") for i in range(2)]
        in_wg, in_x2, in_ln1, in_ln2, in_keys, in_pb = (sem(n) for n in ("in_wg", "in_x2", "in_ln1", "in_ln2", "in_keys", "in_pb"))
        in_lat = [sem(f"in_lat{i}") for i in range(4)]
        in_mod = [sem(f"in_mod{i}") for i in range(4)]
        mod_used = sem("mod_used")
        in_pada = [sem(f"in_pada{i}") for i in range(2)]
        in_u = [sem(f"in_u{i}") for i in range(8)]
        in_v = [sem(f"in_v{i}") for i in range(8)]
        dve_s, act_s, pool_s = sem("dve_self"), sem("act_self"), sem("pool_self")
        pool_gate, dve_gate = sem("pool_gate"), sem("dve_gate")
        acc_zero, ada_used, cact_ok = sem("acc_zero"), sem("ada_used"), sem("cact_ok")
        cols_t, cols_ok, sigc_ok, y_need, y_ok = (sem(n) for n in ("cols_t", "cols_ok", "sigc_ok", "y_need", "y_ok"))
        r_ok, sin_ok = sem("angles_ok"), sem("sin_ok")
        xT_done, xT_out, acc_ok, modc_done, hT_ok = (sem(n) for n in ("xT_done", "xT_out", "acc_ok", "modc_done", "hT_ok"))
        unit_used, out_act, out_dve = (sem(n) for n in ("unit_used", "out_act", "out_dve"))
        kr_done, kr_out, krot_done, kr_ok = (sem(n) for n in ("kr_done", "kr_out", "krot_done", "kr_ok"))
        sq_ok, ssq_done, std_ok, lat_ok = (sem(n) for n in ("sq_ok", "ssq_done", "std_ok", "lat_ok"))
        krw_ok = sem("krw_ok")
        in_uqr, q_done, q_out, q_rot, q_rotout = (sem(n) for n in ("in_uqr", "q_done", "q_out", "q_rot", "q_rotout"))
        h_qk, h_qkout, h_rope, h_v, h_vout = (sem(f"h_{n}") for n in ("qk", "qkout", "rope", "v", "vout"))
        h_s, h_neg, h_exp, h_p, h_t, h_tout, h_o, h_oout = (sem(f"h_{n}") for n in ("s", "neg", "exp", "p", "t", "tout", "o", "oout"))
        xc_ok, gates_done, gates_out, tanh_ok, sqrt_ok, gelu_in, gelu_ok, hg_ok = (sem(n) for n in (
            "xc_ok", "gates_done", "gates_out", "tanh_ok", "sqrt_ok", "gelu_in", "gelu_ok", "hg_ok"))
        mod_part, mod_done, mod_ok, mix_ok = (sem(n) for n in ("mod_part", "mod_done", "mod_ok", "mix_ok"))
        keys_t, keys_ok = sem("keys_t"), sem("keys_ok")
        var_ok, std1_ok, h2_ok, h2T_done, h2T_out = (sem(n) for n in ("var_ok", "std1_ok", "h2_ok", "h2T_done", "h2T_out"))
        sc_done, sc_out, stage_ok, best_ok, gexp_ok, topk_ok, zero_ok = (sem(n) for n in (
            "sc_done", "sc_out", "stage_ok", "best_ok", "gexp_ok", "topk_ok", "zero_ok"))
        shift_ok, norm_ok = sem("shift_ok"), sem("norm_ok")
        whi_ok, wlo_ok, shi_ok, slo_ok = (sem(n) for n in ("whi_ok", "wlo_ok", "shi_ok", "slo_ok"))
        dots_done, z_ok, a_ok, diag_ok, pv_done, y_done = (sem(n) for n in ("dots_done", "z_ok", "a_ok", "diag_ok", "pv_done", "y_done"))
        ln2_ok, in_out = sem("ln2_ok"), sem("in_out")

        wv = {n: t[n][0].rearrange("(t p) c -> p t c", p=P) for n in ("w_in", "w_rnn_out", "w_mla_out", "w_o", "peer_wq")}
        ada_g = t["w_ada"][0].rearrange("(t p) (h j c) -> p t h j c", p=P, h=6, j=4)
        ada_v = t["w_ada"][0].rearrange("(t p) c -> p t c", p=P)
        uq_v = t["w_uq"][0].rearrange("(t p) c -> p t c", p=P)
        ukv_v = t["w_ukv"][0].rearrange("(t p) c -> p t c", p=P)
        rows = {n: t[n].rearrange("a (r c) -> (a r) c", c=P) for n in ("conv_b", "b_rg_a", "b_rg_x", "rg_lambda", "c", "q_norm_g", "kv_norm_g")}
        conv_rows = t["conv_w"][0].rearrange("w (r c) -> (w r) c", c=P)

        block = ctx.enter_context(nc.Block())

        def psblock(b):
            return ps[:, 2 * (b % 2):2 * (b % 2) + 2, :]

        @block.sync
        def _(sp):
            sp.dma_start(cst, t["cst"]).then_inc(in_cst, 16)
            for o, n in ((0, "c"), (16, "q_norm_g"), (20, "kv_norm_g")):
                r = rows[n]
                sp.dma_start(arena[o:o + r.shape[0], W + 9344:W + 9472], r).then_inc(in_par, 16)
            sp.dma_start(arena[0:64, W + 9216:W + 9344], conv_rows).then_inc(in_par, 16)
            for i, n in enumerate(("conv_b", "b_rg_a", "b_rg_x", "rg_lambda")):
                sp.dma_start(arena[64 + 16 * i:80 + 16 * i, W + 9216:W + 9344], rows[n]).then_inc(in_par, 16)
            sp.dma_start(xin[:, :, :], t["x"][0].rearrange("(t p) c -> p t c", p=P)).then_inc(in_x, 16)
            sp.wait_ge(acc_zero, 1)
            for h in range(2):
                sp.dma_start(acc[0:1, :, h, :], t["b_ada"][:, h * D:(h + 1) * D].rearrange("a (j c) -> a j c", j=4)).then_inc(in_bada, 16)
            pos = t["positions"]
            sp.dma_start(pt[0].bitcast(I32), bass.AP(pos.tensor, pos.offset, [[0, P], [1, S]])).then_inc(in_pos, 16)
            def ada(j, i, first):
                for s in range(RING):
                    if not first:
                        sp.wait_ge(ada_used, i * 8 + (16 * j + 2 * (s - 3)))
                    for h in range(2):
                        sp.dma_start(ring[s].rearrange("p (t h c) -> p t h c", t=2, h=2)[:, :, h, :],
                                     ada_g[:, bass.ds(i * 8 + 2 * s, 2), h, j, :]).then_inc(in_ring[s], 16)

            for j in range(4):
                if j == 0:
                    ada(0, 0, True)
                with sp.Fori(1 if j == 0 else 0, 2) as i:
                    ada(j, i, False)
                for c, col in enumerate((C_QC, C_KVC)):
                    if j >= 2:
                        sp.wait_ge(unit_used, 2 * j - 3 + c)
                    sp.dma_start(lat_w[2 * (j % 2) + c], wv["w_in"][:, 4 * j:4 * j + 4, col:col + RANK]).then_inc(in_lat[2 * (j % 2) + c], 16)
                if j == 0:
                    sp.dma_start(krw[:, :, 0:ROPE], wv["w_in"][:, :, C_KR:C_KR + ROPE]).then_inc(in_kr, 16)

            def units(w, col, b):
                for s in range(RING):
                    sp.wait_ge(unit_used, b * RING + (s - 3))
                    sp.dma_start(ring3[s], wv[w][:, 4 * s:4 * s + 4, bass.ds(col, 512)]).then_inc(in_ring[s], 16)

            for k in range(LT):
                sp.dma_start(uqr[:, k, :].rearrange("p (h c) -> p h c", c=ROPE), uq_v[:, k, :].rearrange("p (h c) -> p h c", h=HEADS)[:, :, NOPE:]
                             ).then_inc(in_uqr, 16)
            sp.wait_ge(unit_used, 6)
            for b in range(2):
                sp.dma_start(uq[b], uq_v[:, :, b * 192:b * 192 + NOPE]).then_inc(in_head[b], 16)
                sp.dma_start(ukv[b], ukv_v[:, :, b * 256:b * 256 + 256]).then_inc(in_head[b], 16)
            def mod_loads(g, half):
                for j in range(4):
                    sp.dma_start(mslot[j], ada_v[:, bass.ds(g * 4 + (2 * half + j // 2), 1), (2 + j % 2) * D:(3 + j % 2) * D].rearrange("p t c -> p (t c)")
                                 ).then_inc(in_mod[j], 16)

            with sp.Fori(1, HEADS // 2) as i:
                for b in range(2):
                    sp.wait_ge(h_v, i * 2 + (b - 1))
                    sp.dma_start(uq[b], uq_v[:, :, bass.ds(i * 384 + b * 192, NOPE)]).then_inc(in_head[b], 16)
                    sp.dma_start(ukv[b], ukv_v[:, :, bass.ds(i * 512 + b * 256, 256)]).then_inc(in_head[b], 16)
            sp.wait_ge(ada_used, 2 * ADA_UNITS)
            with sp.Fori(0, 4) as g:
                units("w_in", g * 512 + C_XR, g * 2 + B_XR)
                sp.wait_ge(gates_done, g + 1)
                sp.wait_ge(h_oout, HEADS)
                sp.wait_ge(mod_used, g * 8 + 1)
                for k, n in enumerate(("w_rg_a", "w_rg_x")):
                    sp.dma_start(wg[:, k, :, :], t[n][0].rearrange("h i j -> i h j")[:, bass.ds(g * 4, 4), :]).then_inc(in_wg, 16)
                mod_loads(g, 0)
                units("w_in", g * 512 + C_GR, g * 2 + B_XR + 1)
                sp.wait_ge(mod_used, g * 8 + 5)
                mod_loads(g, 1)
            with sp.Fori(0, 4) as g:
                units("w_in", g * 512 + C_GRNN, g * 2 + B_G)
                units("w_in", g * 512 + C_GMLA, g * 2 + B_G + 1)
            with sp.Fori(0, 4) as g:
                units("w_rnn_out", g * 512, g + B_RNN)
            sp.wait_ge(unit_used, 4 * B_RNN)
            sp.dma_start(at3(W, NT, D), t["x"][0].rearrange("(t p) c -> p t c", p=P)).then_inc(in_x2, 16)
            sp.dma_start(keys, t["peer_keys"][0].rearrange("a n d -> n a d")).then_inc(in_keys, 16)
            with sp.Fori(0, 4) as g:
                units("w_mla_out", g * 512, g + B_MLA)
            sp.wait_ge(unit_used, 4 * (B_RNN + 4))
            for i, n in enumerate(("ln1_g", "ln1_b")):
                sp.dma_start(ln1[i], bass.AP(t[n].tensor, t[n].offset, [[0, P], [1, D]])).then_inc(in_ln1, 16)
            with sp.Fori(0, 4) as g:
                units("w_o", g * 512, g + B_O)
            with sp.Fori(0, 4) as g:
                units("peer_wq", g * 512, g + B_WQ)
            sp.wait_ge(sc_done, 4)
            for i, n in enumerate(("ln2_g", "ln2_b")):
                if i == 1:
                    sp.wait_ge(stage_ok, PH + 1)
                sp.dma_start(ln2[i], bass.AP(t[n].tensor, t[n].offset, [[0, P], [1, D]])).then_inc(in_ln2, 16)
            for T in range(NT):
                for c in range(4):
                    sp.wait_ge(ln2_ok, 4 * T + c + 1)
                    sp.dma_start(out[0, T * P:(T + 1) * P, c * 512:(c + 1) * 512], x1[T][:, c * 512:(c + 1) * 512]).then_inc(in_out, 16)
            sp.wait_ge(in_out, 64 * NT)

        @block.gpsimd
        def _(pool):
            me = Chain(pool, pool_s)
            for ch in range(4):
                me.do(pool.memset(mods[ch], 0.0))
                me.wait()
                pool.dma_start(mods[ch][0:1, :], t["b_ada"][:, (2 + ch) * D:(3 + ch) * D]).then_inc(in_pb, 16)

            def ada_load(kt, ch):
                pool.dma_start(pada[ch - 2], ada_v[:, bass.ds(kt, 1), (2 + ch) * D:(3 + ch) * D].rearrange("p t c -> p (t c)")
                               ).then_inc(in_pada[ch - 2], 16)

            def ada_tile(kt, last):
                for ch in range(2, 4):
                    b = ch - 2
                    pool.wait_ge(in_pada[b], kt * 16 + 16)
                    pool.sem_inc(pool_gate, 1)
                    me.do(pool.tensor_tensor(pada[b], pada[b], cact[:, bass.ds(kt, 1)].to_broadcast([P, D]), ALU.mult))
                    me.wait()
                    me.do(pool.tensor_tensor(mods[ch], mods[ch], pada[b], ALU.add))
                    me.wait()
                    pool.sem_inc(pool_gate, 1)
                    if not last:
                        ada_load(kt + 1, ch)

            pool.wait_ge(unit_used, 8)
            for ch in range(2, 4):
                ada_load(0, ch)
            pool.wait_ge(cact_ok, 1)
            pool.wait_ge(in_pb, 64)
            with pool.Fori(0, KT - 1) as kt:
                me.enter(kt, 0, 4)
                ada_tile(kt, False)
            me.leave(KT - 1)
            ada_tile(KT - 1, True)
            pool.sem_inc(mod_part, 1)

            def gathers(H, first):
                pool.wait_ge(topk_ok, H + 1)
                for q in range(TOPK // GROUP):
                    b = q % 2
                    for slots, table, ix, used, landed in ((uslot, "peer_u", idxu, dots_done, in_u), (vslot, "peer_v", idxv, pv_done, in_v)):
                        if not first or q >= 2:
                            pool.wait_ge(used, H * TOPK + (q * GROUP + GROUP))
                        elif table == "peer_u" and q == 0:
                            pool.wait_ge(dots_done, 2 * GROUP)
                        pool.sem_inc(pool_gate, 1)
                        me.do(pool.tensor_copy(ix[:, b * GROUP:(b + 1) * GROUP],
                                               arena[:, bass.ds(H * TOPK + (o_idx + q * GROUP), GROUP)].bitcast(U32)))
                        me.wait()
                        pool.sem_inc(pool_gate, 1)
                        for s in range(GROUP * b, GROUP * (b + 1)):
                            if first and (table, s) in last_unit:
                                pool.wait_ge(unit_used, last_unit[table, s])
                            pool.indirect_dma_start(slots[s], None, t[table][0], bass.IndirectOffsetOnAxis(ix[:, s:s + 1], 0)
                                                    ).then_inc(landed[s], 16)

            N = 4 * B_END
            last_unit = {("peer_v", 2): N - 3, ("peer_v", 3): N - 2, ("peer_u", 4): N - 1, ("peer_u", 5): N - 1,
                         ("peer_u", 6): N, ("peer_u", 7): N, ("peer_v", 4): N}
            gathers(0, True)
            with pool.Fori(1, NT * PH) as H:
                me.enter(H, 1, 2 * TOPK // GROUP)
                gathers(H, False)
            me.leave(NT * PH - 1)

        @block.tensor
        def _(pe):
            def mm(o, l, r, start, stop, **k):
                return pe.matmul(o, l, r, start=start, stop=stop, skip_group_check=True, **k)

            pe.wait_ge(in_cst, 16)
            pe.wait_ge(in_par, 128)
            pe.transpose(ps[:, 0, 0:24], stB, ident[0:24, 0:24]).then_inc(cols_t, 1)
            pe.transpose(ps[:, 1, 0:P], stA, ident).then_inc(cols_t, 1)
            pe.wait_ge(in_x, 16)
            for g in range(KT // 2):
                if g >= 4:
                    pe.wait_ge(xT_out, g - 3)
                for a in range(2):
                    for T in range(NT):
                        last = pe.transpose(ps[:, 4 + g % 4, a * S + T * P:a * S + (T + 1) * P],
                                            xin[:, T, (2 * g + a) * P:(2 * g + a + 1) * P], ident)
                last.then_inc(xT_done, 1)
            def channel_block(b, src):
                o = psblock(b).rearrange("p b (h c) -> p (b h) c", h=2)
                for s in range(RING):
                    pe.wait_ge(in_ring[s], b * 16 + 16 * (SLOT_BASE))
                    for k in range(4):
                        kt = 4 * s + k
                        for m in range(4):
                            last = mm(o[:, m, :], ring3[s][:, k, m * P:(m + 1) * P], src[:, kt, :],
                                      kt == 0 and m % 2 == 0, kt == KT - 1)
                    last.then_inc(unit_used, 1)

            pe.wait_ge(xT_out, KT // 2)
            for j in range(4):
                pe.wait_ge(acc_ok, j + 1)
                for h in range(2):
                    for k in range(4):
                        last = mm(ps[:, 5, 4 * h + k:4 * h + k + 1], acc[:, j, h, k * P:(k + 1) * P], ones[:, 0:1], True, True)
                last.then_inc(modc_done, 1)
                pe.wait_ge(hT_ok, 4 * j + 4)
                for c in range(2):
                    o = psblock(c).rearrange("p b (h c) -> p (b h) c", h=2)
                    pe.wait_ge(in_lat[2 * (j % 2) + c], 16 * (j // 2 + 1))
                    for k in range(4):
                        kt = 4 * j + k
                        for m in range(4):
                            last = mm(o[:, m, :], lat_w[2 * (j % 2) + c][:, k, m * P:(m + 1) * P], hT[:, kt, :],
                                      kt == 0 and m % 2 == 0, kt == KT - 1)
                    last.then_inc(unit_used, 1)
                pe.wait_ge(krw_ok, 1)
                for kt in range(4 * j, 4 * j + 4):
                    last = mm(ps[:, 4, 0:S], krw[:, kt, :], hT[:, kt, :], kt == 0, kt == KT - 1)
            last.then_inc(kr_done, 1)
            pe.wait_ge(kr_out, 1)
            mm(ps[:, 5, 0:S], cst[:, K_ROT:K_ROT + P], krraw, True, True).then_inc(krot_done, 1)
            for i in range(2):
                pe.wait_ge(sq_ok, i + 1)
                for k in range(LT):
                    last = mm(ps[:, 6 + i, 0:S], ones, sq2[i][:, k, :], k == 0, k == LT - 1)
                last.then_inc(ssq_done, 1)
            pe.wait_ge(lat_ok, 1)
            pe.wait_ge(in_uqr, 16 * LT)
            for g in range(4):
                for a in range(2):
                    for k in range(LT):
                        last = mm(ps[:, g, a * S:(a + 1) * S], uqr[:, k, (2 * g + a) * P:(2 * g + a + 1) * P], qcT[:, k, :], k == 0, k == LT - 1)
                last.then_inc(q_done, 1)
            pe.wait_ge(lat_ok, 2)
            pe.wait_ge(kr_ok, 1)
            for g in range(4):
                pe.wait_ge(q_out, g + 1)
                mm(ps[:, 4 + g, :], cst[:, K_ROT:K_ROT + P], at(o_qr + 512 * g, 512), True, True).then_inc(q_rot, 1)

            def transposes(h):
                pe.wait_ge(h_p, h + 1)
                for j in range(3):
                    last = pe.transpose(ps[:, 4, j * P:(j + 1) * P], sc[:, j * P:(j + 1) * P], ident)
                last.then_inc(h_t, 1)

            def values(h, n):
                pe.wait_ge(h_tout, h + 1)
                pe.wait_ge(h_vout, h + 1)
                if n:
                    pe.wait_ge(h_oout, h)
                mm(ps[:, 5, 0:P], vv[:, 0, :], pT[:, 0, :], True, True)
                mm(ps[:, 5, P:2 * P], vv[:, 0, :], pT[:, 1, :], True, False)
                mm(ps[:, 5, P:2 * P], vv[:, 1, :], pT[:, 2, :], False, True).then_inc(h_o, 1)

            def head(i, b, first):
                h = i * 2 + b
                pe.wait_ge(in_head[b], i * 32 + 32)
                if not first:
                    pe.wait_ge(h_qkout, h)
                for k in range(LT):
                    mm(ps[:, 1, 0:S], uq[b][:, k, 0:NOPE], qcT[:, k, :], k == 0, k == LT - 1)
                for k in range(LT):
                    last = mm(ps[:, 1, S:2 * S], ukv[b][:, k, 0:NOPE], kvT[:, k, :], k == 0, k == LT - 1)
                last.then_inc(h_qk, 1)
                if not first:
                    pe.wait_ge(h_vout, h)
                for T in range(NT):
                    for k in range(LT):
                        last = mm(ps[:, 2, T * P:(T + 1) * P], kvT[:, k, T * P:(T + 1) * P], ukv[b][:, k, NOPE:], k == 0, k == LT - 1)
                last.then_inc(h_v, 1)
                if not first:
                    transposes(h - 1)
                pe.wait_ge(h_qkout, h + 1)
                pe.wait_ge(h_rope, i + 1)
                for T in range(NT):
                    o = ps[:, 3, T * P:(2 * T + 1) * P]
                    n = (T + 1) * P
                    mm(o, qn[:, T * P:(T + 1) * P], kn[:, 0:n], True, False)
                    half = slice(b * ROPE, (b + 1) * ROPE)
                    last = mm(o, qro[half, T * P:(T + 1) * P], krT[half, 0:n], False, True)
                last.then_inc(h_s, 1)

            head(0, 0, True)
            pe.wait_ge(q_rotout, 4)
            head(0, 1, False)
            values(0, False)
            with pe.Fori(1, HEADS // 2) as i:
                for b in range(2):
                    head(i, b, False)
                    values(i * 2 + (b - 1), True)
            transposes(HEADS - 1)
            values(HEADS - 1, True)

            pe.wait_ge(h_oout, HEADS)
            pe.sem_inc(gates_done, 1)
            with pe.Fori(0, 4) as g:
                for k2 in range(2):
                    pe.wait_ge(out_act, g * 2 + (k2 + 1))
                    o = ps[:, 2 * k2:2 * k2 + 2, :].rearrange("p b (h c) -> p (b h) c", h=2)
                    for s in range(RING):
                        pe.wait_ge(in_ring[s], g * 32 + 16 * (B_XR + k2 + SLOT_BASE))
                        for k in range(4):
                            kt = 4 * s + k
                            for m in range(4):
                                last = mm(o[:, m, :], ring3[s][:, k, m * P:(m + 1) * P], hT[:, kt, :],
                                          kt == 0 and m % 2 == 0, kt == KT - 1)
                        last.then_inc(unit_used, 1)
                pe.wait_ge(in_wg, g * 32 + 32)
                pe.wait_ge(xc_ok, g + 1)
                pe.wait_ge(gates_out, g * 2 + 1)
                for k in range(2):
                    for m in range(4):
                        last = mm(ps[:, 4 + 2 * k + m // 2, (m % 2) * S:(m % 2 + 1) * S], wg[:, k, m, :], quad(XC, m), True, True)
                last.then_inc(gates_done, 1)

            def split_blocks(b0, src, evac, ready, token=False, rounds=2, after=None):
                hi, lo = by_tile(src[0]), by_tile(src[1])
                with pe.Fori(0, rounds) as g:
                    for k2 in range(2):
                        evac(g, k2)
                        o = ps[:, 2 * k2:2 * k2 + 2, :]
                        oc = o.rearrange("p b (h c) -> p (b h) c", h=2)
                        for s in range(RING):
                            pe.wait_ge(wlo_ok, g * 8 + 4 * (b0 + k2 - B_G2) + s + 1)
                            ready(s)
                            wh = whi[s % 2].rearrange("p (t c) -> p t c", t=4)
                            wl = wlo[s].rearrange("p (t c) -> p t c", t=4)
                            for k in range(4):
                                kt = 4 * s + k
                                first, end = kt == 0, kt == KT - 1
                                if token:
                                    for T in range(NT):
                                        rows = slice(T * P, (T + 1) * P)
                                        mm(o[:, T, :], hi[:, kt, rows], wh[:, k, :], first, False)
                                        mm(o[:, T, :], hi[:, kt, rows], wl[:, k, :], False, False)
                                        last = mm(o[:, T, :], lo[:, kt, rows], wh[:, k, :], False, end)
                                else:
                                    for m in range(4):
                                        cols = slice(m * P, (m + 1) * P)
                                        mm(oc[:, m, :], wh[:, k, cols], hi[:, kt, :], first and m % 2 == 0, False)
                                        mm(oc[:, m, :], wh[:, k, cols], lo[:, kt, :], False, False)
                                        last = mm(oc[:, m, :], wl[:, k, cols], hi[:, kt, :], False, end)
                            last.then_inc(unit_used, 1)
                            if after is not None:
                                after(g, k2, s)

            def modulation(ch):
                pe.wait_ge(mod_part, 2)
                if ch:
                    pe.wait_ge(mod_ok, ch)
                for j in range(4):
                    last = mm(ps[:, 4 + j, :], ones, mods[ch][:, j * 512:(j + 1) * 512], True, True)
                last.then_inc(mod_done, 1)

            for b in range(B_G, B_G2):
                pe.wait_ge(out_act, b - 1)
                channel_block(b, hT)
            split_blocks(B_G2, S_HT, lambda g, k: pe.wait_ge(out_act, g * 2 + (B_G2 + k - 1)),
                         rounds=3, ready=lambda s: pe.wait_ge(slo_ok, 4 + s + 1))
            pe.wait_ge(out_act, B_RNN)
            modulation(0)
            split_blocks(B_RNN, S_HG, lambda g, k: pe.wait_ge(out_dve, g * 2 + (1 if k == 0 else 1)), ready=lambda s: pe.wait_ge(slo_ok, 4))
            modulation(1)
            split_blocks(B_MLA, S_OT, lambda g, k: pe.wait_ge(out_dve, g * 2 + (4 + k)), ready=lambda s: pe.wait_ge(slo_ok, 12))
            pe.wait_ge(in_keys, 16)
            pe.wait_ge(mod_ok, 2)
            for a in range(2):
                last = pe.transpose(ps[:, 6, a * P:(a + 1) * P], keys[:, a, :], ident)
            last.then_inc(keys_t, 1)
            pe.wait_ge(keys_ok, 1)
            modulation(2)
            split_blocks(B_O, S_MIX, lambda g, k: pe.wait_ge(out_dve, g * 2 + (8 + k)), token=True,
                         ready=lambda s: pe.wait_ge(slo_ok, 12 + s + 1))
            pe.wait_ge(mod_ok, 3)
            for n in range(4 * NT):
                c, T = n // NT, n % NT
                pe.wait_ge(h2_ok, n + 1)
                if n >= 4:
                    pe.wait_ge(slo_ok, 16 + n - 3)
                for a in range(4):
                    last = pe.transpose(ps[:, 4 + n % 4, a * P:(a + 1) * P], h2[T][:, (4 * c + a) * P:(4 * c + a + 1) * P], ident)
                last.then_inc(h2T_done, 1)
            pe.wait_ge(out_dve, 13)

            def scores(g, k):
                pe.wait_ge(out_act, g * 2 + (B_RNN + k + 1))
                pe.wait_ge(sc_out, g * 4 + (2 * k + 2))
                for T in range(NT):
                    for q in range(4):
                        last = mm(ps[:, 4 + 2 * k + T, q * P:(q + 1) * P], qT[k][:, q, T * P:(T + 1) * P], keysT[:, q % 2, :], True, True)
                last.then_inc(sc_done, 1)

            def scores_after(g, k, s):
                if k == 1 and s == 0:
                    scores(g, 0)
                if k == 1 and s == RING - 1:
                    scores(g, 1)

            split_blocks(B_WQ, S_H2, lambda g, k: pe.wait_ge(out_act, g * 2 + (B_RNN - 1 + k)),
                         ready=lambda s: pe.wait_ge(slo_ok, 16 + NT * (s + 1)), after=scores_after)
            pe.wait_ge(sc_done, 4)
            pe.sem_inc(pv_done, 2 * GROUP)
            pe.wait_ge(sc_out, 12)
            modulation(3)

            def products(H, T, end=False):
                for e in range(TOPK):
                    q = e % (2 * GROUP)
                    pe.wait_ge(in_v[q], H * 32 + 16 * (e // (2 * GROUP) + 1))
                    pe.wait_ge(diag_ok, H * TOPK + (e + 1))
                    for j in range(4):
                        last = mm(ps[:, 4 * T + j, :], diag[q], vslot[q][:, j * 512:(j + 1) * 512], False, end and e == TOPK - 1)
                    last.then_inc(pv_done, 1)

            pe.wait_ge(zero_ok, 1)
            for T in range(NT):
                pe.wait_ge(*((out_act, B_RNN + 4) if T == 0 else (mod_ok, 4)))
                for j in range(4):
                    mm(ps[:, 4 * T + j, :], zeros, zeros4, True, False)
                with pe.Fori(T * PH, (T + 1) * PH - 1) as H:
                    products(H, T)
                products((T + 1) * PH - 1, T, end=True)
                pe.wait_ge(pv_done, 2 * GROUP + (T + 1) * EXPERTS)
                pe.sem_inc(y_done, 1)

        @block.scalar
        def _(act):
            me = Chain(act, act_s)
            A = act.activation
            act.wait_ge(cols_ok, 1)
            A(sigc, colB[:, 0:16], ACT.Sigmoid).then_inc(sigc_ok, 1)
            for g in range(KT // 2):
                act.wait_ge(xT_done, g + 1)
                A(at(R_HT + g * 2 * S, 2 * S), ps[:, 4 + g % 4, :], ACT.Copy).then_inc(xT_out, 1)
            act.wait_ge(in_kr, 16)
            A(krw[:, :, ROPE:], krw[:, :, 0:ROPE], ACT.Copy).then_inc(krw_ok, 1)
            act.wait_ge(r_ok, 1)
            A(pt[3], pt[2], ACT.Sin).then_inc(sin_ok, 1)
            A(pt[4], pt[2], ACT.Sin, scale=0.5).then_inc(sin_ok, 1)

            def latent(b, off):
                act.wait_ge(unit_used, 7 + b)
                A(at(off, 1024), psblock(b).rearrange("p b c -> p (b c)"), ACT.Copy).then_inc(out_act, 1)

            latent(B_QC, W)
            latent(B_KVC, W + 1024)
            act.wait_ge(kr_done, 1)
            A(krraw, ps[:, 4, 0:S], ACT.Copy).then_inc(kr_out, 1)
            for i in range(2):
                act.wait_ge(ssq_done, i + 1)
                A(rs2[i], ps[:, 6 + i, 0:S], ACT.Sqrt, bias=eps_rms, scale=1.0 / RANK).then_inc(std_ok, 1)

            for g in range(4):
                act.wait_ge(q_done, g + 1)
                A(at(o_qr + 512 * g, 512), ps[:, g, :], ACT.Copy).then_inc(q_out, 1)

            def head(i, b, first):
                h = i * 2 + b
                act.wait_ge(h_qk, h + 1)
                if not first:
                    act.wait_ge(h_s, h)
                A(qkn, ps[:, 1, :], ACT.Copy).then_inc(h_qkout, 1)
                act.wait_ge(h_v, h + 1)
                if not first:
                    act.wait_ge(h_o, h)
                    A(arena[:, bass.ds((h - 1) * S + R_OT, S)], ps[:, 5, 0:S], ACT.Copy).then_inc(h_oout, 1)
                A(at(W + 3840, NT * VH), ps[:, 2, 0:NT * VH], ACT.Copy).then_inc(h_vout, 1)
                act.wait_ge(h_neg, h + 1)
                A(sc[:, 0:P], sc[:, 0:P], ACT.Exp, bias=snm[:, 0:1], scale=SM_SCALE, accum_out=ssum[:, 0:1])
                A(sc[:, P:3 * P], sc[:, P:3 * P], ACT.Exp, bias=snm[:, 1:2], scale=SM_SCALE, accum_out=ssum[:, 1:2]).then_inc(h_exp, 1)

            head(0, 0, True)
            head(0, 1, False)
            with act.Fori(1, HEADS // 2) as i:
                for b in range(2):
                    head(i, b, False)
            act.wait_ge(h_o, HEADS)
            A(at(R_OT + (HEADS - 1) * S, S), ps[:, 5, 0:S], ACT.Copy).then_inc(h_oout, 1)

            act.wait_ge(y_need, 1)
            A(lt[1], lt[0], ACT.Exp, scale=-1.0).then_inc(y_ok, 1)

            act.sem_inc(gates_out, 1)
            with act.Fori(0, 4) as g:
                act.wait_ge(unit_used, g * 8 + 4 * (B_XR + 1))
                A(at(XR, 1024), ps[:, 0:2, :].rearrange("p b c -> p (b c)"), ACT.Copy).then_inc(out_act, 1)
                act.wait_ge(unit_used, g * 8 + 4 * (B_XR + 2))
                act.wait_ge(hg_ok, g + 1)
                A(at(GR, 1024), ps[:, 2:4, :].rearrange("p b c -> p (b c)"), ACT.Copy).then_inc(out_act, 1)
                act.wait_ge(gates_done, g + 2)
                for m in range(4):
                    last = A(quad(RR, m), ps[:, 4 + m // 2, (m % 2) * S:(m % 2 + 1) * S], ACT.Sigmoid, bias=ba_c[:, bass.ds(g * 4 + m, 1)])
                last.then_inc(gates_out, 1)
                for m in range(4):
                    last = A(quad(II, m), ps[:, 6 + m // 2, (m % 2) * S:(m % 2 + 1) * S], ACT.Sigmoid, bias=bx_c[:, bass.ds(g * 4 + m, 1)])
                last.then_inc(gates_out, 1)
                act.wait_ge(gates_out, g * 2 + 3)
                for m in range(4):
                    last = A(quad(TP, m), quad(RR, m), ACT.Tanh, scale=sp4[:, bass.ds(g * 4 + m, 1)])
                last.then_inc(tanh_ok, 1)
                act.wait_ge(gelu_in, g + 1)
                A(at(GT, 1024), at(GT, 1024), ACT.Sigmoid, scale=GELU_S).then_inc(gelu_ok, 1)
                act.wait_ge(tanh_ok, g + 1)
                A(at(RR, 1024), at(TP, 1024), ACT.Sqrt).then_inc(sqrt_ok, 1)

            def high(src):
                A(src[0], at(src[2], KT * S), ACT.Copy).then_inc(shi_ok, 1)

            def weight(g, b, s):
                act.wait_ge(in_ring[s], g * 32 + 16 * (b + SLOT_BASE))
                act.wait_ge(unit_used, g * 8 + (4 * b + s - 1))
                A(whi[s % 2], ring[s], ACT.Copy).then_inc(whi_ok, 1)

            def weights(b0, evac=None, rounds=2):
                with act.Fori(0, rounds) as g:
                    for k in range(2):
                        weight(g, b0 + k, 2)
                        weight(g, b0 + k, 3)
                        weight(g, b0 + k + 1, 0)
                        if evac is not None:
                            evac(g, b0 + k)
                        weight(g, b0 + k + 1, 1)

            act.wait_ge(hg_ok, 5)
            high(S_HG)
            high(S_HT)

            def branch_gate(g, b):
                k = b % 2
                act.wait_ge(unit_used, g * 8 + 4 * (b + 1))
                A(arena[:, bass.ds(g * 1024 + (R_G + 4096 * k + 512 * (b - k - B_G)), 1024)],
                  ps[:, 2 * k:2 * k + 2, :].rearrange("p b c -> p (b c)"), ACT.Sigmoid).then_inc(out_act, 1)

            for b in range(B_G, B_G2):
                branch_gate(0, b)
            act.wait_ge(wlo_ok, 2)
            weights(B_G2, branch_gate, 3)

            def modulation(ch):
                act.wait_ge(mod_done, ch + 1)
                A(mods[ch], ps[:, 4:8, :].rearrange("p b c -> p (b c)"), ACT.Copy, bias=0.0 if ch == 1 else 1.0).then_inc(mod_ok, 1)

            high(S_OT)
            modulation(0)
            weights(B_RNN)
            modulation(1)
            weights(B_MLA)
            act.wait_ge(keys_t, 1)
            A(at(W + 8448, 2 * P), ps[:, 6, 0:2 * P], ACT.Copy).then_inc(keys_ok, 1)
            modulation(2)
            weights(B_O)
            for T in range(NT):
                act.wait_ge(var_ok, T + 1)
                A(rstd[T][:, 0:1], mv[T][:, 1:2], ACT.Sqrt, bias=eps_ln).then_inc(std1_ok, 1)

            def norm(T, c, n):
                act.wait_ge(shift_ok, n + 1)
                x = x1[T][:, 512 * c:512 * (c + 1)]
                A(x, x, ACT.Identity, bias=shift[T], scale=rstd[T][:, 1:2]).then_inc(norm_ok, 1)

            h2hi = by_tile(S_H2[0])
            for T in range(NT):
                norm(T, 0, T)
            for n in range(4 * NT):
                c, T = n // NT, n % NT
                if c < 3:
                    norm(T, c + 1, T)
                act.wait_ge(h2T_done, n + 1)
                A(h2hi[:, 4 * c:4 * c + 4, T * P:(T + 1) * P], ps[:, 4 + n % 4, :].rearrange("p (a c) -> p a c", a=4), ACT.Copy).then_inc(h2T_out, 1)

            def stage_scores(H):
                A(stage, arena[:, bass.ds(H * (2 * NK) + R_OT, 2 * NK)], ACT.Copy).then_inc(stage_ok, 1)

            def gate_exp(H):
                act.wait_ge(best_ok, H + 1)
                A(gexp, best, ACT.Exp, bias=negbest, accum_out=gsum).then_inc(gexp_ok, 1)

            def query(b):
                k = b % 2
                act.wait_ge(unit_used, 4 * (b + 1))
                if b >= B_WQ + 2:
                    act.wait_ge(sc_done, b - B_WQ - 1)
                A(at(R_G + KT * S + 1024 * k, 1024), ps[:, 2 * k:2 * k + 2, :].rearrange("p b c -> p (b c)"), ACT.Copy).then_inc(out_act, 1)

            def scores_out(b):
                act.wait_ge(sc_done, b - B_WQ + 1)
                for T in range(NT):
                    A(at(R_OT + D * T + 512 * (b - B_WQ), 512), ps[:, 4 + 2 * (b % 2) + T, :], ACT.Copy).then_inc(sc_out, 1)

            act.sem_inc(sc_out, 4)
            for b in range(B_WQ, B_END):
                for u in range(2, 6):
                    if b + u // 4 < B_END:
                        weight(0, b + u // 4, u % 4)
                    if u == 2 and b > B_WQ:
                        scores_out(b - 1)
                        if b == B_WQ + 1:
                            act.wait_ge(sc_out, 6)
                            stage_scores(0)
                    if u == 4:
                        query(b)
                    if u == 5 and b == B_WQ + 1:
                        gate_exp(0)
            scores_out(B_END - 1)
            modulation(3)
            act.sem_inc(a_ok, 2)

            def diagonals(H, topk):
                for q in range(TOPK // GROUP):
                    b = q % 2
                    if q == 0 and topk:
                        act.wait_ge(topk_ok, H + 1)
                        stage_scores(H + 1)
                    if q == 1 and topk:
                        gate_exp(H + 1)
                    c0, c1 = b * GROUP, (b + 1) * GROUP
                    act.wait_ge(z_ok, H * (TOPK // GROUP) + (q + 1))
                    me.do(A(zs[:, c0:c1], zu[:, c0:c1], ACT.Sigmoid, scale=GELU_S))
                    me.wait()
                    for s in range(c0, c1):
                        last = A(za[:, s:s + 1], zs[:, s:s + 1], ACT.Copy, scale=zg[:, s:s + 1])
                    last.then_inc(a_ok, 1)
                    act.wait_ge(a_ok, H * (TOPK // GROUP) + (q + 3))
                    for s in range(c0, c1):
                        act.wait_ge(pv_done, H * TOPK + (q * GROUP + s - c0 + 1))
                        A(diag[s], ident, ACT.Copy, scale=za[:, s:s + 1]).then_inc(diag_ok, 1)

            def ln2_std(T):
                act.wait_ge(var_ok, NT + T + 1)
                A(rstd[T][:, 0:1], mv[T][:, 1:2], ACT.Sqrt, bias=eps_ln).then_inc(std1_ok, 1)
                for c in range(4):
                    norm(T, c, NT + T)

            def loop(first, end, topk=True):
                with act.Fori(first, end) as H:
                    me.enter(H, first, TOPK // GROUP)
                    diagonals(H, topk)
                me.leave(end - first)

            loop(0, PH)
            diagonals(PH, True)
            ln2_std(0)
            loop(PH + 1, NT * PH - 1)
            diagonals(NT * PH - 1, False)
            ln2_std(1)

        @block.vector
        def _(dve):
            me = Chain(dve, dve_s)
            V = dve
            TT, TS, STT = V.tensor_tensor, V.tensor_scalar, V.scalar_tensor_tensor
            V.memset(acc, 0.0).then_inc(acc_zero, 1)
            me.do(V.memset(eps_rms, RMS_EPS))
            me.do(V.memset(eps_ln, LN_EPS))
            dve.wait_ge(cols_t, 1)
            V.tensor_copy(colB, ps[:, 0, 0:24]).then_inc(cols_ok, 1)
            dve.wait_ge(cols_ok, 1)
            dve.wait_ge(sigc_ok, 1)
            me.do(TT(cact, colB[:, 0:16], sigc, ALU.mult))
            me.wait()
            dve.sem_inc(cact_ok, 1)
            dve.wait_ge(cols_t, 2)
            me.do(V.tensor_copy(colA, ps[:, 1, 0:P]))
            dve.wait_ge(in_bada, 32)
            with dve.Fori(0, 4) as j:
                me.enter(j, 0, 2)
                part = arena[:, bass.ds(j * 1024 + (R_G + KT * S), 1024)]
                for kt in range(KT):
                    i, s = kt // 8, kt // 2 % RING
                    if kt % 2 == 0:
                        dve.wait_ge(in_ring[s], j * 64 + 32 * (i + 1))
                    if kt:
                        dve.wait_ge(ada_used, j * KT + kt)
                    STT(part, ring[s][:, kt % 2 * 1024:(kt % 2 + 1) * 1024], cact[:, kt:kt + 1], part, ALU.mult, ALU.add).then_inc(ada_used, 1)
                dve.wait_ge(ada_used, j * KT + KT)
                dve.sem_inc(acc_ok, 1)
                dve.wait_ge(modc_done, j + 1)
                dve.wait_ge(xT_out, KT // 2)
                me.do(V.tensor_copy(sh1, ps[:, 5, 0:4]))
                me.do(TS(sc1, ps[:, 5, 4:8], 1.0, None, ALU.add))
                me.wait()
                for k in range(4):
                    h = arena[:, bass.ds(j * 1024 + (R_HT + S * k), S)]
                    TS(h, h, sc1[:, k:k + 1], sh1[:, k:k + 1], ALU.mult, ALU.add).then_inc(hT_ok, 1)
            me.leave(4)
            dve.wait_ge(in_pos, 16)
            me.do(V.tensor_copy(pt[1], pt[0].bitcast(I32)))
            me.wait()
            me.do(TS(pt[1], pt[1], cst[:, K_INVF:K_INVF + 1], None, ALU.mult))
            me.wait()
            magic = 1.5 * 2.0 ** 23
            me.do(TS(pt[3], pt[1], 1.0 / (2.0 * math.pi), magic, ALU.mult, ALU.add))
            me.wait()
            me.do(TS(pt[3], pt[3], -magic, None, ALU.add))
            me.wait()
            c1 = 6.28125
            c2 = float(np.float32(np.round((2.0 * math.pi - c1) * 2.0 ** 21) / 2.0 ** 21))
            c3 = 2.0 * math.pi - c1 - c2
            src = pt[1]
            for c in (c1, c2, c3):
                me.do(STT(pt[2], pt[3], -c, src, ALU.mult, ALU.add))
                me.wait()
                src = pt[2]
            me.do(TS(pt[2], pt[2], 3.1415925, -3.1415925, ALU.min, ALU.max))
            me.wait()
            dve.sem_inc(r_ok, 1)
            dve.wait_ge(sin_ok, 2)
            me.do(V.tensor_copy(sinT, pt[3]))
            me.do(TT(pt[4], pt[4], pt[4], ALU.mult))
            me.wait()
            me.do(TS(cosT, pt[4], -2.0, 1.0, ALU.mult, ALU.add))
            for i, lat in enumerate((qcT, kvT)):
                dve.wait_ge(out_act, i + 1)
                TT(sq2[i], lat, lat, ALU.mult).then_inc(sq_ok, 1)
            dve.wait_ge(krot_done, 1)
            me.wait()
            me.do(TT(rt, krraw, cosT, ALU.mult))
            me.do(TT(krT, ps[:, 5, 0:S], sinT, ALU.mult))
            me.wait()
            TT(krT, krT, rt, ALU.add).then_inc(kr_ok, 1)
            for i, lat in enumerate((qcT, kvT)):
                dve.wait_ge(std_ok, i + 1)
                me.do(V.reciprocal(rs2[i], rs2[i]))
                me.wait()
                for k in range(LT):
                    last = STT(lat[:, k, :], lat[:, k, :], colB[:, 16 + LT * i + k:17 + LT * i + k], rs2[i], ALU.mult, ALU.mult)
                last.then_inc(lat_ok, 1)

            def transposed_out(h):
                dve.wait_ge(h_t, h + 1)
                V.tensor_copy(at(W + 4736, 3 * P), ps[:, 4, 0:3 * P]).then_inc(h_tout, 1)

            def softmax(h, first):
                dve.wait_ge(h_s, h + 1)
                if not first:
                    dve.wait_ge(h_t, h)
                me.do(TT(sc, ps[:, 3, 0:3 * P], cst[:, K_MASK:K_MASK + 3 * P], ALU.add))
                me.wait()
                me.do(V.tensor_reduce(smx[:, 0:1], sc[:, 0:P], AX_X, ALU.max))
                me.do(V.tensor_reduce(smx[:, 1:2], sc[:, P:3 * P], AX_X, ALU.max))
                me.wait()
                TS(snm, smx, -SM_SCALE, None, ALU.mult).then_inc(h_neg, 1)
                dve.wait_ge(h_exp, h + 1)
                me.do(V.reciprocal(srec, ssum))
                me.wait()
                me.do(TS(sc[:, 0:P], sc[:, 0:P], srec[:, 0:1], None, ALU.mult))
                TS(sc[:, P:3 * P], sc[:, P:3 * P], srec[:, 1:2], None, ALU.mult).then_inc(h_p, 1)

            for g in range(4):
                dve.wait_ge(q_rot, g + 1)
                x, xs = (at3(o + 512 * g, 2, S) for o in (o_qr, o_qrs))
                me.do(TT(x, x, cosT.unsqueeze(1).to_broadcast([P, 2, S]), ALU.mult))
                TT(xs, ps[:, 4 + g, :].rearrange("p (a s) -> p a s", a=2), sinT.unsqueeze(1).to_broadcast([P, 2, S]), ALU.mult).then_inc(q_rotout, 1)
            me.wait()
            dve.wait_ge(q_rotout, 4)

            def head(i, b, first):
                h = i * 2 + b
                if b == 0:
                    if not first:
                        dve.wait_ge(h_s, h)
                    TT(qro, arena[:, bass.ds(i * S + o_qr, S)], arena[:, bass.ds(i * S + o_qrs, S)], ALU.add).then_inc(h_rope, 1)
                if not first:
                    transposed_out(h - 1)
                softmax(h, first)

            head(0, 0, True)
            head(0, 1, False)
            with dve.Fori(1, HEADS // 2) as i:
                me.enter(i, 1, 10)
                for b in range(2):
                    head(i, b, False)
            me.leave(HEADS // 2 - 1)
            transposed_out(HEADS - 1)

            def modulate(g, half):
                for j in range(4):
                    dve.wait_ge(in_mod[j], g * 32 + 16 * (half + 1))
                    if j >= 2:
                        dve.wait_ge(mod_used, g * 8 + (4 * half + j + 1))
                    STT(mods[j % 2], mslot[j], cact[:, bass.ds(g * 4 + (2 * half + j // 2), 1)], mods[j % 2], ALU.mult, ALU.add).then_inc(mod_used, 1)

            me.do(TS(lt[3], lam_c, -1.0, None, ALU.mult))
            me.wait()
            me.do(TT(lt[0], lt[3], lam_c, ALU.max))
            me.wait()
            dve.sem_inc(y_need, 1)
            dve.wait_ge(y_ok, 1)
            me.do(TS(lt[2], lt[1], 2.0, None, ALU.add))
            me.wait()
            me.do(V.reciprocal(lt[2], lt[2]))
            me.wait()
            me.do(TT(lt[1], lt[1], lt[2], ALU.mult))
            me.wait()
            me.do(TT(lt[2], lt[1], lt[1], ALU.mult))
            me.wait()
            me.do(TS(lt[4], lt[2], 1.0 / 19.0, None, ALU.mult))
            me.wait()
            for k in range(17, 2, -2):
                me.do(STT(lt[4], lt[4], 1.0 / k, lt[2], ALU.add, ALU.mult))
                me.wait()
            me.do(STT(lt[4], lt[4], 1.0, lt[1], ALU.add, ALU.mult))
            me.do(TS(lt[3], lt[3], 0.0, 4.0, ALU.max, ALU.mult))
            me.wait()
            me.do(STT(sp4, lt[4], 8.0, lt[3], ALU.mult, ALU.add))

            dve.wait_ge(in_pb, 64)
            dve.sem_inc(mod_used, 1)
            dve.sem_inc(hg_ok, 1)
            with dve.Fori(0, 4) as g:
                me.enter(g, 0, 30)
                modulate(g, 0)
                dve.wait_ge(out_act, g * 2 + (B_XR + 1))
                for m in range(4):
                    me.do(TS(quad(XC, m), quad(XR, m), conv_c[:, bass.ds(g * 4 + (48 + m), 1)], convb_c[:, bass.ds(g * 4 + m, 1)], ALU.mult, ALU.add))
                for d in range(1, CONV):
                    me.wait()
                    for m in range(4):
                        o, x = at(XC + S * m + d, S - d), at(XR + S * m, S - d)
                        me.do(STT(o, x, conv_c[:, bass.ds(g * 4 + (16 * (3 - d) + m), 1)], o, ALU.mult, ALU.add))
                me.wait()
                dve.sem_inc(xc_ok, 1)
                modulate(g, 1)
                dve.wait_ge(out_act, g * 2 + (B_XR + 2))
                gt, gr = at(GT, 1024), at(GR, 1024)
                me.do(TT(gt, gr, gr, ALU.mult))
                me.wait()
                me.do(TS(gt, gt, GELU_C, 1.0, ALU.mult, ALU.add))
                me.wait()
                TT(gt, gt, gr, ALU.mult).then_inc(gelu_in, 1)
                rr, ii, tp, qq, xc = (at(o, 1024) for o in (RR, II, TP, QQ, XC))
                dve.wait_ge(gates_out, g * 2 + 3)
                me.do(TT(ii, ii, xc, ALU.mult))
                dve.wait_ge(tanh_ok, g + 1)
                me.do(TS(qq, tp, 1.0, None, ALU.add))
                me.wait()
                me.do(V.reciprocal(qq, qq))
                me.wait()
                me.do(TT(ii, ii, qq, ALU.mult))
                dve.wait_ge(sqrt_ok, g + 1)
                me.do(TS(tp, qq, 2.0, -1.0, ALU.mult, ALU.add))
                me.wait()
                me.do(STT(ii, ii, 2.0, rr, ALU.mult, ALU.mult))
                dve.wait_ge(gelu_ok, g + 1)
                me.do(TT(gt, gt, gr, ALU.mult))
                me.wait()
                for m in range(4):
                    me.do(V.tensor_tensor_scan(quad(XC, m), quad(TP, m), quad(II, m), 0.0, ALU.mult, ALU.add))
                me.wait()
                me.do(TT(arena[:, bass.ds(g * 1024 + R_HG, 1024)], xc, gt, ALU.mult))
                me.wait()
                dve.sem_inc(hg_ok, 1)
            me.leave(4)
            dve.wait_ge(mod_used, 2 * KT + 1)
            dve.sem_inc(mod_part, 1)

            def low(src, n, j=None):
                o, w = (0, 4096) if j is None else (1024 * j, 1024)
                dve.wait_ge(shi_ok, n)
                TT(src[1][:, o:o + w], at(src[2] + o, w), src[0][:, o:o + w].bitcast(F32), ALU.subtract).then_inc(slo_ok, 4 if j is None else 1)

            def weight(g, b, s):
                dve.wait_ge(whi_ok, g * 8 + (4 * (b - B_G2) + s + 1))
                TT(wlo[s], ring[s], whi[s % 2].bitcast(F32), ALU.subtract).then_inc(wlo_ok, 1)

            def weights(b0, evac, more=None, rounds=2):
                with dve.Fori(0, rounds) as g:
                    me.enter(g, 0, 2 * evac_steps[b0])
                    for k in range(2):
                        weight(g, b0 + k, 2)
                        weight(g, b0 + k, 3)
                        weight(g, b0 + k + 1, 0)
                        evac(g, b0 + k)
                        weight(g, b0 + k + 1, 1)
                        if more is not None:
                            more(g, b0 + k)
                me.leave(rounds)

            evac_steps = {B_G2: 0, B_RNN: 1, B_MLA: 2, B_O: 6}
            low(S_HG, 1)
            for j in range(4):
                dve.wait_ge(unit_used, 4 * (B_G2 - 1) + j + 1)
                low(S_HT, 2, j)
                if 1 <= j <= 2:
                    dve.wait_ge(in_ring[j - 1], 16 * (B_G2 + SLOT_BASE))
                    if j == 1:
                        dve.wait_ge(mod_part, 2)
                    V.tensor_copy(whi[j - 1], ring[j - 1]).then_inc(whi_ok, 1)
                    weight(0, B_G2, j - 1)
            weights(B_G2, lambda g, b: None, rounds=3)
            low(S_OT, 3)

            dve.sem_inc(out_dve, 1)

            def gT_at(k, g, j):
                return arena[:, bass.ds(g * 2048 + (R_G + 4096 * k + 1024 * j), 1024)]

            def gated(j, g, b):
                k = b % 2
                dve.wait_ge(unit_used, g * 8 + 4 * (b + 1))
                me.do(TT(gT_at(j, g, k), gT_at(j, g, k), ps[:, 2 * k:2 * k + 2, :].rearrange("p b c -> p (b c)"), ALU.mult))
                me.wait()
                dve.sem_inc(out_dve, 1)

            def mixed(g, b):
                k = b % 2
                me.do(TT(gT_at(0, g, k), gT_at(0, g, k), gT_at(1, g, k), ALU.add))
                me.wait()
                cols = bass.ds(g * 2048 + 1024 * k, 1024)
                V.tensor_copy(split["w1"][:, cols], gT_at(0, g, k)).then_inc(mix_ok, 1)
                dve.wait_ge(mix_ok, g * 2 + (k + 1))
                TT(split["g0"][:, cols], gT_at(0, g, k), split["w1"][:, cols].bitcast(F32), ALU.subtract).then_inc(slo_ok, 1)

            weights(B_RNN, lambda g, b: gated(0, g, b))
            weights(B_MLA, lambda g, b: gated(1, g, b), mixed)
            dve.wait_ge(in_ln1, 32)
            dve.wait_ge(mod_ok, 3)
            me.do(TT(ln_t, ln1[1], mods[2], ALU.mult))
            me.wait()
            me.do(TT(mods[1], mods[1], ln_t, ALU.add))
            me.do(TT(mods[2], mods[2], ln1[0], ALU.mult))
            dve.wait_ge(mod_ok, 1)
            dve.wait_ge(in_x2, 16)

            def gated_out(g, b):
                k = b % 2
                dve.wait_ge(unit_used, g * 8 + 4 * (b + 1))
                for T in range(NT):
                    me.do(TT(wo_t[k][:, T * 512:(T + 1) * 512], ps[:, 2 * k + T, :],
                             front[:, bass.ds(g * 1024 + (R_MODS + 512 * k), 512)], ALU.mult))
                me.wait()
                dve.sem_inc(out_dve, 1)

            def residual(g, b):
                k = b % 2
                for T in range(NT):
                    xs = arena[:, bass.ds(g * 1024 + (W + D * T + 512 * k), 512)]
                    me.do(STT(xs, xs, ALPHA, wo_t[k][:, T * 512:(T + 1) * 512], ALU.mult, ALU.add))
                me.wait()
                for T in range(NT):
                    me.do(V.bn_stats(arena[:, bass.ds(g * 12 + (o_bn[T] + 6 * k), 6)], arena[:, bass.ds(g * 1024 + (W + D * T + 512 * k), 512)]))

            weights(B_O, gated_out, residual)

            def scale_of(T, n):
                me.wait()
                V.bn_aggr(mv[T], bn6[T][:, :, :]).then_inc(var_ok, 1)
                dve.wait_ge(std1_ok, n + 1)
                me.do(V.reciprocal(rstd[T][:, 1:2], rstd[T][:, 0:1]))
                me.wait()
                TS(shift[T], mv[T][:, 0:1], rstd[T][:, 1:2], -1.0, ALU.mult, ALU.mult).then_inc(shift_ok, 1)

            for T in range(NT):
                scale_of(T, T)
            me.wait()
            h2hi, h2lo = by_tile(S_H2[0]), by_tile(S_H2[1])

            def low_h2(n):
                c, T = n // NT, n % NT
                dve.wait_ge(h2T_out, n + 1)
                place = (slice(None), slice(4 * c, 4 * c + 4), slice(T * P, (T + 1) * P))
                TT(h2lo[place], ps[:, 4 + n % 4, :].rearrange("p (a c) -> p a c", a=4), h2hi[place].bitcast(F32), ALU.subtract).then_inc(slo_ok, 1)

            for c in range(4):
                cs = slice(512 * c, 512 * (c + 1))
                for T in range(NT):
                    dve.wait_ge(norm_ok, NT * c + T + 1)
                    me.do(TT(h2[T][:, cs], x1[T][:, cs], mods[2][:, cs], ALU.mult))
                    me.wait()
                    TT(h2[T][:, cs], h2[T][:, cs], mods[1][:, cs], ALU.add).then_inc(h2_ok, 1)
                    if c:
                        low_h2(NT * (c - 1) + T)
            for n in range(3 * NT, 4 * NT):
                low_h2(n)
            def topk(H):
                top_halves(H)
                top_pairs()
                experts(H)
                expert_gates(H)

            halves = [(stage[:, a * NK:(a + 1) * NK], tops[:, a * TOPK:(a + 1) * TOPK], topi[:, a * TOPK:(a + 1) * TOPK]) for a in range(2)]
            pairs = [(cand.rearrange("p a b -> p (a b)"), best, bestj)]

            def hold():
                me.wait()
                dve.sem_inc(dve_gate, 1)

            def top16(lots):
                for v, vo, io in lots:
                    me.do(V.max(vo[:, 0:8], v))
                hold()
                for v, vo, io in lots:
                    me.do(V.max_index(io[:, 0:8], vo[:, 0:8], v))
                hold()
                for v, vo, io in lots:
                    me.do(V.match_replace(v, vo[:, 0:8], v, -3.0e38))
                hold()
                for v, vo, io in lots:
                    me.do(V.max(vo[:, 8:16], v))
                hold()
                for v, vo, io in lots:
                    me.do(V.max_index(io[:, 8:16], vo[:, 8:16], v))

            def top_halves(H):
                dve.wait_ge(stage_ok, H + 1)
                dve.sem_inc(dve_gate, 1)
                top16(halves)

            def top_pairs():
                me.do(TT(cand, tops[:, 0:TOPK].unsqueeze(2).to_broadcast([P, TOPK, TOPK]),
                         tops[:, TOPK:].unsqueeze(1).to_broadcast([P, TOPK, TOPK]), ALU.add))
                me.wait()
                me.do(V.tensor_copy(topf, topi))
                hold()
                top16(pairs)
                TS(negbest, best[:, 0:1], -1.0, None, ALU.mult).then_inc(best_ok, 1)

            def experts(H):
                me.wait()
                me.do(TS(ranki[:, 0:TOPK], bestj, 4, None, ALU.logical_shift_right))
                me.do(TS(ranki[:, TOPK:], bestj, 15, None, ALU.bitwise_and))
                me.wait()
                me.do(V.tensor_copy(rankf, ranki))
                me.wait()
                me.do(TT(onehot, rankf.unsqueeze(2).to_broadcast([P, 2 * TOPK, TOPK]),
                         cst[:, K_IOTA:K_IOTA + TOPK].unsqueeze(1).to_broadcast([P, 2 * TOPK, TOPK]), ALU.is_equal))
                me.wait()
                oh4 = onehot.rearrange("p (a k) c -> p a k c", a=2)
                me.do(TT(oh4, oh4, topf.rearrange("p (a c) -> p a c", a=2).unsqueeze(2).to_broadcast([P, 2, TOPK, TOPK]), ALU.mult))
                me.wait()
                me.do(V.tensor_reduce(keyf, onehot, AX_X, ALU.add))
                me.wait()
                STT(arena[:, bass.ds(H * TOPK + o_idx, TOPK)].bitcast(U32), keyf[:, 0:TOPK], float(NK), keyf[:, TOPK:], ALU.mult, ALU.add
                    ).then_inc(topk_ok, 1)

            def expert_gates(H):
                dve.wait_ge(gexp_ok, H + 1)
                me.do(V.reciprocal(ginv, gsum))
                me.wait()
                me.do(TS(arena[:, bass.ds(H * TOPK + o_gate, TOPK)], gexp, ginv, None, ALU.mult))

            def after_norm(T):
                me.do(TT(x1[T], x1[T], ln1[0], ALU.mult))
                me.wait()
                me.do(TT(x1[T], x1[T], ln1[1], ALU.add))

            weight(0, B_WQ, 2)
            weight(0, B_WQ, 3)
            weight(0, B_WQ + 1, 0)
            after_norm(0)
            weight(0, B_WQ + 1, 1)
            after_norm(1)
            V.memset(zeros, 0.0).then_inc(zero_ok, 1)
            me.wait()
            dve.sem_inc(dots_done, 2 * GROUP)
            weight(0, B_WQ + 1, 2)
            top_halves(0)
            weight(0, B_WQ + 1, 3)
            top_pairs()
            weight(0, B_WQ + 2, 0)
            experts(0)
            weight(0, B_WQ + 2, 1)
            expert_gates(0)
            weight(0, B_WQ + 2, 2)
            weight(0, B_WQ + 2, 3)
            for s in range(RING):
                weight(0, B_WQ + 3, s)

            def dots(H, T, topk_too):
                for q in range(TOPK // GROUP):
                    b = q % 2
                    c0, c1 = b * GROUP, (b + 1) * GROUP
                    dve.wait_ge(a_ok, H * (TOPK // GROUP) + (q + 1))
                    for s in range(c0, c1):
                        dve.wait_ge(in_u[s], H * 32 + 16 * (q // 2 + 1))
                        V.tensor_tensor_reduce(uslot[s], uslot[s], h2[T], 1.0, 0.0, ALU.mult, ALU.add, zraw[:, s:s + 1]).then_inc(dots_done, 1)
                    dve.wait_ge(dots_done, H * TOPK + (q * GROUP + 3 * GROUP))
                    z, u = zraw[:, c0:c1], zu[:, c0:c1]
                    me.do(TT(u, z, z, ALU.mult))
                    me.do(TT(zg[:, c0:c1], z, arena[:, bass.ds(H * TOPK + (o_gate + q * GROUP), GROUP)], ALU.mult))
                    me.wait()
                    me.do(TS(u, u, GELU_C, 1.0, ALU.mult, ALU.add))
                    me.wait()
                    TT(u, u, z, ALU.mult).then_inc(z_ok, 1)
                    if q == 0 and topk_too:
                        topk(H + 1)

            def finish(T):
                dve.wait_ge(y_done, T + 1)
                for c in range(4):
                    cs = slice(512 * c, 512 * (c + 1))
                    me.do(TT(h2[T][:, cs], ps[:, 4 * T + c, :], mods[3][:, cs], ALU.mult))
                    me.wait()
                    me.do(STT(x1[T][:, cs], x1[T][:, cs], ALPHA, h2[T][:, cs], ALU.mult, ALU.add))
                    me.wait()
                    me.do(V.bn_stats(bn6[T][:, c, :], x1[T][:, cs]))
                scale_of(T, NT + T)
                me.wait()
                for c in range(4):
                    cs = slice(512 * c, 512 * (c + 1))
                    dve.wait_ge(norm_ok, 4 * NT + 4 * T + c + 1)
                    me.do(TT(x1[T][:, cs], x1[T][:, cs], ln2[0][:, cs], ALU.mult))
                    me.wait()
                    TT(x1[T][:, cs], x1[T][:, cs], ln2[1][:, cs], ALU.add).then_inc(ln2_ok, 1)

            def loop(first, end, T):
                with dve.Fori(first, end) as H:
                    me.enter(H, first, DOTS_STEPS + TOPK_STEPS)
                    dots(H, T, True)
                me.leave(end - first)

            loop(0, PH, 0)
            dots(PH, 1, True)
            dve.wait_ge(in_ln2, 32)
            dve.wait_ge(mod_ok, 4)
            finish(0)
            loop(PH + 1, NT * PH - 1, 1)
            dots(NT * PH - 1, 1, False)
            finish(1)


INPUTS = ("x", "c", "positions", "w_ada", "b_ada", "w_in", "conv_w", "conv_b", "w_rg_a", "b_rg_a", "w_rg_x", "b_rg_x",
          "rg_lambda", "w_rnn_out", "q_norm_g", "w_uq", "kv_norm_g", "w_ukv", "w_mla_out", "w_o", "ln1_g", "ln1_b",
          "peer_wq", "peer_keys", "peer_u", "peer_v", "ln2_g", "ln2_b")


def kernel(**inputs):
    import concourse.bacc as bacc
    from concourse.bass_utils import run_bass_kernel_spmd as run

    nc = bacc.Bacc("TRN2", target_bir_lowering=False, num_devices=1)
    arrays = {n: np.ascontiguousarray(inputs[n]) for n in INPUTS}
    arrays["cst"] = constants()
    t = {n: nc.dram_tensor(f"in_{n}", a.shape, mybir.dt.from_np(a.dtype), kind="ExternalInput").ap() for n, a in arrays.items()}
    out = nc.dram_tensor("out_y", (1, S, D), F32, kind="ExternalOutput").ap()
    build(nc, t, out)
    r = run(nc, [{f"in_{n}": a for n, a in arrays.items()}], core_ids=[0])
    return r.results[0]["out_y"]
```
